# Optimizing a Trainium2 kernel written in Bass

```python
import jax, jax.numpy as jnp
from jax import lax
import numpy as np

D_MODEL = 1024
BATCH = 1
SEQ = 1024
DEPTH = 1
DEC_BATCH = 8
DEC_SEQ = 1
PAST_LEN = 2048
PAGE_SIZE = 128

NSA_H = 8
NSA_G = 2
NSA_HPG = NSA_H // NSA_G
HD = 64
ROT_DIM = HD // 4
ROPE_THETA = 500000.0
CMP_BLOCK = 32
CMP_STRIDE = 16
CMP_HID = 128
SLC_BLOCK = 64
N_SEL = 16
SLC_QBLOCK = 64
WINDOW = 512
WIN_QBLOCK = 128
ML_H = 4
ML_D = 128
ML_W = ML_H * ML_D
CONV_W = 4
MLSTM_CHUNK = 64
MEM_T = 256
MEM_H = 4
MEM_HD = 128
MEM_W = MEM_H * MEM_HD
N_BRANCH = 3
BRANCH_W = 512
FFN_HID = -(-8 * D_MODEL // (3 * 256)) * 256
EPS = 1e-6
IN_WIDTHS = (NSA_H * HD, 3 * NSA_H, 2 * NSA_G * HD, 2 * NSA_G * HD, 2 * NSA_G * HD,
             ML_W, ML_W, ML_H, ML_H, MEM_W, N_BRANCH * D_MODEL)
IN_W = sum(IN_WIDTHS)
F32 = jnp.float32

kernel_name = 'hybrid_nsa_mlstm_memory_decoder_step'

def rmsnorm(x, g):
    xf = x.astype(F32)
    y = xf * lax.rsqrt(jnp.mean(xf * xf, axis=-1, keepdims=True) + EPS)
    return (y * g.astype(F32)).astype(x.dtype)

def rope(x, pos):
    half = ROT_DIM // 2
    freqs = ROPE_THETA ** (-jnp.arange(half, dtype=F32) / half)
    ang = pos.astype(F32)[:, None] * freqs
    ang = ang.reshape(ang.shape[:1] + (1,) * (x.ndim - 3) + (half,))
    cos, sin = jnp.cos(ang), jnp.sin(ang)
    xf = x.astype(F32)
    x1, x2, rest = xf[..., :half], xf[..., half:ROT_DIM], xf[..., ROT_DIM:]
    return jnp.concatenate([x1 * cos - x2 * sin, x2 * cos + x1 * sin, rest], -1).astype(x.dtype)

def masked_softmax(s, mask):
    s = jnp.where(mask, s.astype(F32), -jnp.inf)
    m = jnp.max(s, axis=-1, keepdims=True)
    m = jnp.where(jnp.isfinite(m), m, 0.0)
    p = jnp.exp(s - m)
    return p / jnp.maximum(p.sum(-1, keepdims=True), jnp.finfo(F32).tiny)

def dense_attend(q, k, v, mask):
    s = jnp.einsum('bsghd,btgd->bghst', q, k) * (q.shape[-1] ** -0.5)
    p = masked_softmax(s, mask)
    o = jnp.einsum('bghst,btgd->bsghd', p, v.astype(F32))
    return o.astype(q.dtype), p

def split_proj(x, norm_mix, w_in):
    offs = [int(o) for o in np.cumsum(IN_WIDTHS)[:-1]]
    return jnp.split(rmsnorm(x, norm_mix) @ w_in, offs, axis=-1)

def nsa_prep(q_raw, g_raw, kvc_raw, kvs_raw, kvw_raw, pos, q_norm, k_norm_slc, k_norm_win):
    B, S = q_raw.shape[:2]
    q = rmsnorm(q_raw.reshape(B, S, NSA_G, NSA_HPG, HD), q_norm)
    q_rot = rope(q, pos)
    gates = jax.nn.sigmoid(g_raw.reshape(B, S, 3, NSA_G, NSA_HPG).astype(F32))
    kv_cmp = kvc_raw.reshape(B, S, NSA_G, 2, HD)

    def norm_rot(raw, gain):
        kv = raw.reshape(B, S, NSA_G, 2, HD)
        k = rope(rmsnorm(kv[..., 0, :], gain), pos)
        return jnp.stack([k, kv[..., 1, :]], axis=3)

    return q, q_rot, gates, kv_cmp, norm_rot(kvs_raw, k_norm_slc), norm_rot(kvw_raw, k_norm_win)

def compress_kv(rows, cmp_pe, cmp_w1, cmp_b1, cmp_w2, k_norm_cmp):
    B, T = rows.shape[:2]
    n_ch = -(-T // CMP_STRIDE)
    rows = jnp.pad(rows, ((0, 0), (0, n_ch * CMP_STRIDE - T), (0, 0), (0, 0), (0, 0)))
    ch = rows.reshape(B, n_ch, CMP_STRIDE, NSA_G, 2, HD)
    blk = jnp.concatenate([ch[:, :-1], ch[:, 1:]], axis=2) + cmp_pe[:, None]
    n_cmp = n_ch - 1
    flat = blk.transpose(0, 1, 3, 4, 2, 5).reshape(B, n_cmp, NSA_G, 2, CMP_BLOCK * HD)
    h = jax.nn.gelu(jnp.einsum('bngcf,cfh->bngch', flat, cmp_w1) + cmp_b1)
    out = jnp.einsum('bngch,chd->bngcd', h, cmp_w2)
    end_pos = jnp.arange(n_cmp) * CMP_STRIDE + CMP_BLOCK - 1
    return rmsnorm(out[..., 0, :], k_norm_cmp), out[..., 1, :], end_pos

def select_blocks(p_cmp, pos, n_slc):
    n_cmp = p_cmp.shape[-1]
    ci = jnp.arange(n_cmp) * CMP_STRIDE
    sj = jnp.arange(n_slc) * SLC_BLOCK
    overlap = ((ci[:, None] < sj[None, :] + SLC_BLOCK) & (ci[:, None] + CMP_BLOCK > sj[None, :])).astype(F32)
    imp = jnp.einsum('bghsn,nj->bsgj', p_cmp, overlap)
    blk = jnp.arange(n_slc)
    causal = sj[None, :] <= pos[:, None]
    forced = (blk[None, :] == (pos // SLC_BLOCK)[:, None]) | (blk[None, :] == 0)
    score = jnp.where(forced[None, :, None, :], jnp.inf,
                      jnp.where(causal[None, :, None, :], imp, -jnp.inf))
    vals, idx = lax.top_k(score, min(N_SEL, n_slc))
    return idx.astype(jnp.int32), vals > -jnp.inf

def slc_attend(q, sel, idx, valid, pos):
    B, Q, G, K = idx.shape
    k = sel[..., 0, :].reshape(B, Q, G, K * SLC_BLOCK, HD)
    v = sel[..., 1, :].reshape(B, Q, G, K * SLC_BLOCK, HD)
    kpos = (idx[..., None] * SLC_BLOCK + jnp.arange(SLC_BLOCK)).reshape(B, Q, G, K * SLC_BLOCK)
    mask = jnp.repeat(valid, SLC_BLOCK, axis=-1) & (kpos <= pos[None, :, None, None])
    s = jnp.einsum('bqghd,bqgkd->bqghk', q, k) * (HD ** -0.5)
    p = masked_softmax(s, mask[:, :, :, None, :])
    return jnp.einsum('bqghk,bqgkd->bqghd', p, v.astype(F32)).astype(q.dtype)

def gather_blocks(blocks, idx):
    B, _, G, _ = idx.shape
    b_ix = jnp.arange(B)[:, None, None, None]
    g_ix = jnp.arange(G)[None, None, :, None]
    return blocks[b_ix, idx, :, g_ix]

def gather_blocks_paged(pool, page_table, kv_new, idx):
    DB, DS = kv_new.shape[:2]
    G = NSA_G
    n_past = page_table.shape[1] * PAGE_SIZE // SLC_BLOCK
    n_new = -(-DS // SLC_BLOCK)
    new_blocks = jnp.pad(kv_new, ((0, 0), (0, n_new * SLC_BLOCK - DS), (0, 0), (0, 0), (0, 0)))
    new_blocks = new_blocks.reshape(DB, n_new, SLC_BLOCK, G, 2, HD)
    b_ix = jnp.arange(DB)[:, None, None, None]
    g_ix = jnp.arange(G)[None, None, :, None]
    start = jnp.minimum(idx, n_past - 1) * SLC_BLOCK
    phys = page_table[b_ix, start // PAGE_SIZE]
    rows = (start % PAGE_SIZE)[..., None] + jnp.arange(SLC_BLOCK)
    past = pool[phys[..., None], rows, g_ix[..., None]].astype(kv_new.dtype)
    new = new_blocks[b_ix, jnp.clip(idx - n_past, 0, n_new - 1), :, g_ix]
    return jnp.where((idx < n_past)[..., None, None, None], past, new)

def slc_prompt(q_rot, kv_slc, idx, valid, pos):
    B, S = q_rot.shape[:2]
    nb = S // SLC_QBLOCK
    blocks = kv_slc.reshape(B, S // SLC_BLOCK, SLC_BLOCK, NSA_G, 2, HD)

    def to_blk(a):
        return jnp.moveaxis(a.reshape((B, nb, SLC_QBLOCK) + a.shape[2:]), 1, 0)

    def step(args):
        qb, ib, vb, pb = args
        return slc_attend(qb, gather_blocks(blocks, ib), ib, vb, pb)

    out = lax.map(step, (to_blk(q_rot), to_blk(idx), to_blk(valid), pos.reshape(nb, SLC_QBLOCK)))
    return jnp.moveaxis(out, 0, 1).reshape(q_rot.shape)

def win_prompt(q_rot, kv_win):
    B, S = q_rot.shape[:2]
    nb = S // WIN_QBLOCK
    n_band = WINDOW // WIN_QBLOCK + 1
    qb = q_rot.reshape(B, nb, WIN_QBLOCK, NSA_G, NSA_HPG, HD)
    kvb = kv_win.reshape(B, nb, WIN_QBLOCK, NSA_G, 2, HD)
    kvp = jnp.pad(kvb, ((0, 0), (n_band - 1, 0), (0, 0), (0, 0), (0, 0), (0, 0)))
    band = jnp.concatenate([kvp[:, n:n + nb] for n in range(n_band)], axis=2)
    qpos = jnp.arange(S).reshape(nb, WIN_QBLOCK)
    kpos = (jnp.arange(nb)[:, None] - (n_band - 1)) * WIN_QBLOCK + jnp.arange(n_band * WIN_QBLOCK)[None, :]
    d = qpos[:, :, None] - kpos[:, None, :]
    mask = (d >= 0) & (d <= WINDOW) & (kpos[:, None, :] >= 0)
    s = jnp.einsum('bnqghd,bnkgd->bnghqk', qb, band[..., 0, :]) * (HD ** -0.5)
    p = masked_softmax(s, mask[None, :, None, None])
    o = jnp.einsum('bnghqk,bnkgd->bnqghd', p, band[..., 1, :].astype(F32))
    return o.reshape(q_rot.shape).astype(q_rot.dtype)

def win_state_prompt(kv_win, w_buf):
    S = kv_win.shape[1]
    if S >= w_buf:
        return kv_win[:, S - w_buf:]
    return jnp.pad(kv_win, ((0, 0), (w_buf - S, 0), (0, 0), (0, 0), (0, 0)))

def win_sample(q_rot, kv_new, win_buf, pos):
    w_buf = win_buf.shape[1]
    kv = jnp.concatenate([win_buf.astype(kv_new.dtype), kv_new], axis=1)
    kpos = PAST_LEN - w_buf + jnp.arange(kv.shape[1])
    d = pos[:, None] - kpos[None, :]
    o, _ = dense_attend(q_rot, kv[..., 0, :], kv[..., 1, :], (d >= 0) & (d <= WINDOW))
    return o, kv[:, -w_buf:]

def nsa_merge(gates, o_cmp, o_slc, o_win):
    B, S = o_cmp.shape[:2]
    o = (gates[..., None] * jnp.stack([o_cmp, o_slc, o_win], axis=2).astype(F32)).sum(2)
    return o.reshape(B, S, NSA_H * HD).astype(o_cmp.dtype)

def mlstm_chunkwise(q, k, v, ig, lf, C0, n0, m0):
    B, S, H, D = q.shape
    L = MLSTM_CHUNK if S % MLSTM_CHUNK == 0 else S
    nc = S // L

    def to_chunks(a):
        return jnp.moveaxis(a.reshape((B, nc, L) + a.shape[2:]), 1, 0)

    tri = jnp.tril(jnp.ones((L, L), bool))

    def step(carry, xs):
        C, n, m = carry
        qc, kc, vc, ic, fc = xs
        b = jnp.cumsum(fc, axis=1)
        dmat = b[:, :, None, :] - b[:, None, :, :] + ic[:, None, :, :]
        dmat = jnp.where(tri[None, :, :, None], dmat, -jnp.inf)
        m_new = jnp.maximum(b + m[:, None, :], dmat.max(axis=2))
        w_in = jnp.exp(dmat - m_new[:, :, None, :]) * jnp.einsum('bthd,bshd->btsh', qc, kc)
        inter = jnp.exp(b + m[:, None, :] - m_new)
        num = inter[..., None] * jnp.einsum('bthd,bhde->bthe', qc, C) + jnp.einsum('btsh,bshe->bthe', w_in, vc)
        den = inter * jnp.einsum('bthd,bhd->bth', qc, n) + w_in.sum(2)
        h = num / jnp.maximum(jnp.abs(den), jnp.exp(-m_new))[..., None]
        m_end = m_new[:, -1]
        decay = jnp.exp(b[:, -1] + m - m_end)
        w_end = jnp.exp(b[:, -1:, :] - b + ic - m_end[:, None, :])
        C = decay[..., None, None] * C + jnp.einsum('bsh,bshd,bshe->bhde', w_end, kc, vc)
        n = decay[..., None] * n + jnp.einsum('bsh,bshd->bhd', w_end, kc)
        return (C, n, m_end), h

    (C, n, m), hs = lax.scan(step, (C0, n0, m0), (to_chunks(q), to_chunks(k), to_chunks(v), to_chunks(ig), to_chunks(lf)))
    return jnp.moveaxis(hs, 0, 1).reshape(B, S, H, D), C, n, m

def mlstm_branch(u, o_raw, i_raw, f_raw, conv_buf, C0, n0, m0,
                 conv_w, conv_b, w_ml_q, w_ml_k, w_ml_v, b_igate, b_fgate, ml_norm):
    B, S, _ = u.shape
    ext = jnp.concatenate([conv_buf.astype(u.dtype), u], axis=1)
    conv = conv_b + sum(ext[:, w:w + S] * conv_w[w] for w in range(CONV_W))
    c = jax.nn.silu(conv).reshape(B, S, ML_H, ML_D).astype(F32)
    uh = u.reshape(B, S, ML_H, ML_D).astype(F32)
    q = jnp.einsum('bshd,hde->bshe', c, w_ml_q.astype(F32)) * (ML_D ** -0.5)
    k = jnp.einsum('bshd,hde->bshe', c, w_ml_k.astype(F32))
    v = jnp.einsum('bshd,hde->bshe', uh, w_ml_v.astype(F32))
    ig = i_raw.astype(F32) + b_igate.astype(F32)
    lf = jax.nn.log_sigmoid(f_raw.astype(F32) + b_fgate.astype(F32))
    h, C, n, m = mlstm_chunkwise(q, k, v, ig, lf, C0.astype(F32), n0.astype(F32), m0.astype(F32))
    h = rmsnorm(h, ml_norm).reshape(B, S, ML_W)
    out = (jax.nn.sigmoid(o_raw.astype(F32)) * h).astype(u.dtype)
    return out, C, n, m, ext[:, -(CONV_W - 1):]

def mem_kv(mem, norm_mem, w_mem_kv, mem_k_norm):
    B, T, _ = mem.shape
    kv = (rmsnorm(mem, norm_mem) @ w_mem_kv).reshape(B, T, MEM_H, 2, MEM_HD)
    return jnp.stack([rmsnorm(kv[..., 0, :], mem_k_norm), kv[..., 1, :]], axis=3)

def mem_attend(q_raw, kv_mem, mem_q_norm):
    B, S = q_raw.shape[:2]
    q = rmsnorm(q_raw.reshape(B, S, MEM_H, 1, MEM_HD), mem_q_norm)
    kv_mem = kv_mem.astype(q.dtype)
    o, _ = dense_attend(q, kv_mem[..., 0, :], kv_mem[..., 1, :], jnp.ones((S, kv_mem.shape[1]), bool))
    return o.reshape(B, S, MEM_W)

def merge_ffn(x, gate_raw, o_nsa, o_ml, o_mem, w_branch, w_out, norm_ffn, w_ffn_in, w_ffn_out):
    B, S, _ = x.shape
    yb = jnp.einsum('bsnc,ncd->bsnd', jnp.stack([o_nsa, o_ml, o_mem], axis=2), w_branch)
    g = jax.nn.sigmoid(gate_raw.reshape(B, S, N_BRANCH, D_MODEL))
    x = x + (g * yb).sum(2) @ w_out
    a, b = jnp.split(rmsnorm(x, norm_ffn) @ w_ffn_in, 2, axis=-1)
    return x + (jax.nn.silu(a) * b) @ w_ffn_out

def setup_inputs(seed: int = 0) -> dict:
    key = jax.random.key(seed)
    ks = iter(jax.random.split(key, 48))

    def nrm(shape, scale):
        return jax.random.normal(next(ks), shape, F32) * scale

    def gain(shape):
        return 1.0 + nrm(shape, 0.02)

    n_pages = PAST_LEN // PAGE_SIZE
    n_phys = (DEC_BATCH * n_pages * 5) // 4
    w_buf = min(WINDOW, PAST_LEN)
    page_table = jax.random.permutation(next(ks), n_phys)[:DEC_BATCH * n_pages]
    page_table = page_table.reshape(DEC_BATCH, n_pages).astype(jnp.int32)
    return {
        'x_prompt': nrm((BATCH, SEQ, D_MODEL), 1.0),
        'x_sample': nrm((DEC_BATCH, DEC_SEQ, D_MODEL), 1.0),
        'cache_kv_cmp': nrm((n_phys, PAGE_SIZE, NSA_G, 2, HD), 1.0),
        'cache_kv_slc': nrm((n_phys, PAGE_SIZE, NSA_G, 2, HD), 1.0),
        'cache_kv_win': nrm((DEC_BATCH, w_buf, NSA_G, 2, HD), 1.0),
        'cache_kv_mem': nrm((DEC_BATCH, MEM_T, MEM_H, 2, MEM_HD), 1.0),
        'state_C': nrm((DEC_BATCH, ML_H, ML_D, ML_D), 0.5),
        'state_n': nrm((DEC_BATCH, ML_H, ML_D), 0.5),
        'state_m': nrm((DEC_BATCH, ML_H), 1.0),
        'state_conv': nrm((DEC_BATCH, CONV_W - 1, ML_W), 1.0),
        'page_table': page_table,
        'mem_prompt': nrm((BATCH, MEM_T, D_MODEL), 1.0),
        'norm_mix': gain((D_MODEL,)),
        'w_in': nrm((D_MODEL, IN_W), D_MODEL ** -0.5),
        'q_norm': gain((HD,)),
        'k_norm_cmp': gain((HD,)),
        'k_norm_slc': gain((HD,)),
        'k_norm_win': gain((HD,)),
        'cmp_pe': nrm((CMP_BLOCK, 2, HD), 0.5),
        'cmp_w1': nrm((2, CMP_BLOCK * HD, CMP_HID), (CMP_BLOCK * HD) ** -0.5),
        'cmp_b1': nrm((2, CMP_HID), 0.02),
        'cmp_w2': nrm((2, CMP_HID, HD), CMP_HID ** -0.5),
        'conv_w': nrm((CONV_W, ML_W), CONV_W ** -0.5),
        'conv_b': nrm((ML_W,), 0.02),
        'w_ml_q': nrm((ML_H, ML_D, ML_D), ML_D ** -0.5),
        'w_ml_k': nrm((ML_H, ML_D, ML_D), ML_D ** -0.5),
        'w_ml_v': nrm((ML_H, ML_D, ML_D), ML_D ** -0.5),
        'b_igate': nrm((ML_H,), 0.1),
        'b_fgate': 3.0 + nrm((ML_H,), 0.1),
        'ml_norm': gain((ML_H, ML_D)),
        'norm_mem': gain((D_MODEL,)),
        'w_mem_kv': nrm((D_MODEL, 2 * MEM_W), D_MODEL ** -0.5),
        'mem_q_norm': gain((MEM_HD,)),
        'mem_k_norm': gain((MEM_HD,)),
        'w_branch': nrm((N_BRANCH, BRANCH_W, D_MODEL), BRANCH_W ** -0.5),
        'w_out': nrm((D_MODEL, D_MODEL), D_MODEL ** -0.5),
        'norm_ffn': gain((D_MODEL,)),
        'w_ffn_in': nrm((D_MODEL, 2 * FFN_HID), D_MODEL ** -0.5),
        'w_ffn_out': nrm((FFN_HID, D_MODEL), FFN_HID ** -0.5),
    }

def reference(x_prompt, x_sample, cache_kv_cmp, cache_kv_slc, cache_kv_win, cache_kv_mem,
              state_C, state_n, state_m, state_conv, page_table, mem_prompt,
              norm_mix, w_in, q_norm, k_norm_cmp, k_norm_slc, k_norm_win,
              cmp_pe, cmp_w1, cmp_b1, cmp_w2, conv_w, conv_b, w_ml_q, w_ml_k, w_ml_v,
              b_igate, b_fgate, ml_norm, norm_mem, w_mem_kv, mem_q_norm, mem_k_norm,
              w_branch, w_out, norm_ffn, w_ffn_in, w_ffn_out):
    w_buf = cache_kv_win.shape[1]

    B, S, _ = x_prompt.shape
    pos_p = jnp.arange(S, dtype=jnp.int32)
    (q_raw, g_raw, kvc_raw, kvs_raw, kvw_raw, u_raw, o_raw, i_raw, f_raw,
     mq_raw, mg_raw) = split_proj(x_prompt, norm_mix, w_in)
    q_p, q_rot_p, gates_p, kv_cmp_p, kv_slc_p, kv_win_p = nsa_prep(
        q_raw, g_raw, kvc_raw, kvs_raw, kvw_raw, pos_p, q_norm, k_norm_slc, k_norm_win)
    k_c, v_c, end_c = compress_kv(kv_cmp_p, cmp_pe, cmp_w1, cmp_b1, cmp_w2, k_norm_cmp)
    o_cmp_p, p_cmp_p = dense_attend(q_p, k_c, v_c, end_c[None, :] <= pos_p[:, None])
    idx_p, valid_p = select_blocks(p_cmp_p, pos_p, -(-S // SLC_BLOCK))
    o_slc_p = slc_prompt(q_rot_p, kv_slc_p, idx_p, valid_p, pos_p)
    o_win_p = win_prompt(q_rot_p, kv_win_p)
    o_nsa_p = nsa_merge(gates_p, o_cmp_p, o_slc_p, o_win_p)
    o_ml_p, C_p, n_p, m_p, conv_p = mlstm_branch(
        u_raw, o_raw, i_raw, f_raw,
        jnp.zeros((B, CONV_W - 1, ML_W), x_prompt.dtype), jnp.zeros((B, ML_H, ML_D, ML_D), F32),
        jnp.zeros((B, ML_H, ML_D), F32), jnp.zeros((B, ML_H), F32),
        conv_w, conv_b, w_ml_q, w_ml_k, w_ml_v, b_igate, b_fgate, ml_norm)
    kv_mem_p = mem_kv(mem_prompt, norm_mem, w_mem_kv, mem_k_norm)
    o_mem_p = mem_attend(mq_raw, kv_mem_p, mem_q_norm)
    y_prompt = merge_ffn(x_prompt, mg_raw, o_nsa_p, o_ml_p, o_mem_p, w_branch, w_out, norm_ffn, w_ffn_in, w_ffn_out)
    win_p = win_state_prompt(kv_win_p, w_buf)

    DB, DS, _ = x_sample.shape
    pos_s = PAST_LEN + jnp.arange(DS, dtype=jnp.int32)
    (q_raw, g_raw, kvc_raw, kvs_raw, kvw_raw, u_raw, o_raw, i_raw, f_raw,
     mq_raw, mg_raw) = split_proj(x_sample, norm_mix, w_in)
    q_s, q_rot_s, gates_s, kv_cmp_s, kv_slc_s, kv_win_s = nsa_prep(
        q_raw, g_raw, kvc_raw, kvs_raw, kvw_raw, pos_s, q_norm, k_norm_slc, k_norm_win)
    past_cmp = cache_kv_cmp[page_table].reshape((DB, -1) + cache_kv_cmp.shape[2:]).astype(kv_cmp_s.dtype)
    rows_s = jnp.concatenate([past_cmp, kv_cmp_s], axis=1)
    k_c, v_c, end_c = compress_kv(rows_s, cmp_pe, cmp_w1, cmp_b1, cmp_w2, k_norm_cmp)
    o_cmp_s, p_cmp_s = dense_attend(q_s, k_c, v_c, end_c[None, :] <= pos_s[:, None])
    idx_s, valid_s = select_blocks(p_cmp_s, pos_s, -(-rows_s.shape[1] // SLC_BLOCK))
    sel_s = gather_blocks_paged(cache_kv_slc, page_table, kv_slc_s, idx_s)
    o_slc_s = slc_attend(q_rot_s, sel_s, idx_s, valid_s, pos_s)
    o_win_s, win_s = win_sample(q_rot_s, kv_win_s, cache_kv_win, pos_s)
    o_nsa_s = nsa_merge(gates_s, o_cmp_s, o_slc_s, o_win_s)
    o_ml_s, C_s, n_s, m_s, conv_s = mlstm_branch(
        u_raw, o_raw, i_raw, f_raw, state_conv, state_C, state_n, state_m,
        conv_w, conv_b, w_ml_q, w_ml_k, w_ml_v, b_igate, b_fgate, ml_norm)
    o_mem_s = mem_attend(mq_raw, cache_kv_mem, mem_q_norm)
    y_sample = merge_ffn(x_sample, mg_raw, o_nsa_s, o_ml_s, o_mem_s, w_branch, w_out, norm_ffn, w_ffn_in, w_ffn_out)

    return (y_prompt, y_sample, kv_cmp_p, kv_cmp_s, kv_slc_p, kv_slc_s, win_p, win_s, kv_mem_p,
            C_p, C_s, n_p, n_s, m_p, m_s, conv_p, conv_s)


_drawn_inputs = setup_inputs


def setup_inputs(seed=0):
    import zlib

    import numpy as np

    out = dict(_drawn_inputs(seed))
    spreads = {}
    factors = {'cache_kv_slc': 3.592,
     'q_norm': 8.0,
     'k_norm_cmp': 8.0,
     'k_norm_slc': 3.221,
     'k_norm_win': 31.802,
     'cmp_b1': 8.0,
     'b_fgate': 64.0,
     'ml_norm': 8.0,
     'norm_mem': 2.749,
     'mem_q_norm': 8.0,
     'mem_k_norm': 3.944,
     'norm_ffn': 3.709}
    for name, (base, spread) in spreads.items():
        noise = np.random.default_rng([zlib.crc32(name.encode()), seed]).standard_normal(out[name].shape)
        drawn = base * np.exp(spread * noise) if base else spread * noise
        out[name] = __import__('jax').numpy.asarray(drawn.astype(out[name].dtype))
    for name, factor in factors.items():
        out[name] = (out[name] * factor).astype(out[name].dtype)
    return out
```

```python
from contextlib import ExitStack, contextmanager

import numpy as np
import concourse.bass as bass
from concourse import mybir

F32 = mybir.dt.float32
I32 = mybir.dt.int32
ALU = mybir.AluOpType
ACT = mybir.ActivationFunctionType
AX = mybir.AxisListType

P = 128
D = 1024
KT = D // P
S = 1024
QT = S // P
B = 8
T = S + B
TT = QT + 1
NB3, BLK = 3, T // 3
PAST, PAGE = 2048, 128
NPG = PAST // PAGE
NPHYS = 160
H, G, HPG, HD = 8, 2, 4, 64
HALF = 8
NC = 63
NCS = 127
CH = 128
WIN = 512
MH, MD = 4, 128
L = 128
NCK = S // L
XT, XH, XD = 256, 4, 128
FH = 2816
FJ = FH // P
EPS = 1e-6
BIG = 1e30
C_Q, C_G, C_KVC, C_KVS, C_U, C_O, C_I, C_F, C_MQ, C_MG = (
    0, 512, 536, 792, 1304, 1816, 2328, 2332, 2336, 2848)
IN_W = 5920


def constant_table():
    p = np.arange(P)[:, None]
    f = np.arange(P)[None, :]
    parts, at, n = [], {}, 0

    def put(name, a):
        nonlocal n
        a = np.asarray(a, np.float32).reshape(P, -1)
        at[name] = (n, n + a.shape[1])
        parts.append(a)
        n += a.shape[1]

    put("ident", p == f)
    put("ones", np.ones((P, P)))
    put("mhalf", np.full((P, 1), -0.5))
    put("causal", np.where(f <= p, 0.0, -BIG))
    put("band", np.where(f >= p, 0.0, -BIG))
    put("future", np.where(p <= f, 0.0, BIG))
    q = np.arange(QT)[None, :, None] * P + np.arange(P)[:, None, None]
    n_ = np.arange(64)[None, None, :]
    put("cmp01", (n_ * 16 + 31 <= q) & (n_ < NC))
    pos = np.concatenate([np.arange(S).reshape(QT, P).T, np.full((P, 1), PAST)], 1).astype(np.float32)
    freqs = np.float32(500000.0) ** (-np.arange(HALF, dtype=np.float32) / np.float32(HALF))
    ang = pos[:, :, None] * freqs.astype(np.float32)
    put("cos", np.cos(ang))
    put("sin", np.sin(ang))
    col = np.arange(B * H)[None, :]
    put("expand", p == (col // H) * G + (col % H) // HPG)
    ci, sj = np.arange(P)[:, None] * 16, np.arange(33)[None, :] * 64
    put("overlap", (ci < sj + 64) & (ci + 32 > sj) & (p < NCS))
    return np.concatenate(parts, 1), at


CONST, CAT = constant_table()
NCONST = CONST.shape[1]


class Stage:

    retired = []

    @staticmethod
    def renew(nc):
        nc.clear_and_free_semaphores(Stage.retired)
        nc.all_engine_barrier()
        Stage.retired = []

    def __init__(self, nc, name):
        self.nc, self.name, self.ctx, self.sems = nc, name, ExitStack(), []

    def __enter__(self):
        return self

    def __exit__(self, *a):
        Stage.retired += self.sems
        return self.ctx.__exit__(*a)

    def sb(self, name, shape, dt=F32):
        return self.ctx.enter_context(self.nc.sbuf_tensor(f"{self.name}_{name}", shape, dt))

    def sem(self, name):
        s = self.nc.alloc_semaphore(f"{self.name}_{name}")
        self.sems.append(s)
        return s

    def block(self):
        return self.nc.Block()


class Chain:

    def __init__(self, sem):
        self.sem, self.n = sem, 0

    def link(self, eng, ins):
        self.n += 1
        ins.then_inc(self.sem, 1)
        eng.wait_ge(self.sem, self.n)


def bc(ap, axis, n):
    v = ap.unsqueeze(axis)
    shape = list(v.shape)
    shape[axis] = n
    return v.to_broadcast(shape)


def build(nc, I, O):
    top = ExitStack()
    Stage.retired = []
    with top:
        cst = top.enter_context(nc.sbuf_tensor("cst", [P, NCONST], F32))
        x2 = top.enter_context(nc.sbuf_tensor("x2", [P, TT, D], F32))
        xnT = top.enter_context(nc.sbuf_tensor("xnT", [P, KT, T], F32))
        brT = top.enter_context(nc.sbuf_tensor("brT", [P, 12, T], F32))
        ps = top.enter_context(nc.psum_tensor("ps", [P, 8, 512], F32))
        M = dict(nc=nc, I=I, O=O, cst=cst, x2=x2, xnT=xnT, brT=brT, ps=ps)
        c = lambda name: cst[:, CAT[name][0]:CAT[name][1]]
        M["c"] = c
        M["memT"] = top.enter_context(nc.sbuf_tensor("memT", [P, KT, XT], F32))
        flat = x2[:, :, :].rearrange("p t d -> p (t d)")
        names = ["ig", "lf", "b", "m", "M", "reset", "stack", "tmp"]
        M["row"] = lambda n: flat[:, names.index(n) * 1040:names.index(n) * 1040 + T]
        M["bias"] = top.enter_context(nc.sbuf_tensor("bias", [P, 2], F32))
        M["gS"] = top.enter_context(nc.sbuf_tensor("gS", [B, 280], F32))[:, :]
        stage_norm(M)
        for s in STAGES:
            if s in RENEW_BEFORE:
                Stage.renew(nc)
            s(M)


def stage_norm(M):
    nc, I, cst, xnT, ps, c = (M[k] for k in ("nc", "I", "cst", "xnT", "ps", "c"))
    NT = TT + 2
    with Stage(nc, "norm") as st:
        X = st.sb("X", [P, NT, D])
        gm = st.sb("gain", [P, 2, KT])
        ss = st.sb("ss", [P, NT])
        rs = st.sb("rs", [P, NT])
        junk = st.sb("junk", [P, D])
        memT = M["memT"]
        loaded, cleared, squared, meaned, rooted, scaled, turned, stored = (
            st.sem(n) for n in ("loaded", "cleared", "squared", "meaned", "rooted", "scaled", "turned", "stored"))

        with st.block() as block:
            @block.sync
            def _(sp):
                sp.dma_start(cst[:, :], I["const"]).then_inc(loaded, 16)
                sp.dma_start(gm[:, 0, :], I["norm_mix"].rearrange("(k p) -> p k", p=P),
                             allow_slow_non_contiguous=True).then_inc(loaded, 16)
                sp.dma_start(gm[:, 1, :], I["norm_mem"].rearrange("(k p) -> p k", p=P),
                             allow_slow_non_contiguous=True).then_inc(loaded, 16)
                sp.wait_ge(cleared, 1)
                sp.dma_start(X[0:B, QT, :], I["x_sample"].rearrange("b o d -> (b o) d")).then_inc(loaded, 16)
                sp.dma_start(X[:, TT:NT, :], I["mem_prompt"].rearrange("o (t p) d -> p (o t) d", p=P)
                             ).then_inc(loaded, 16)
                sp.dma_start(X[:, 0:QT, :], I["x_prompt"].rearrange("o (t p) d -> p (o t) d", p=P)
                             ).then_inc(loaded, 16)

            @block.gpsimd
            def _(pool):
                nc.gpsimd.memset(X[:, QT, :], 0.0).then_inc(cleared, 1)
                pool.wait_ge(meaned, 1)
                nc.gpsimd.tensor_tensor(rs[:, :], rs[:, :], c("mhalf").to_broadcast([P, NT]),
                                        ALU.pow).then_inc(rooted, 1)

            @block.scalar
            def _(act):
                act.wait_ge(loaded, 96)
                for t in range(NT):
                    if t:
                        act.wait_ge(squared, t)
                    nc.scalar.activation(junk[:, :], X[:, t, :], ACT.Square,
                                         accum_out=ss[:, t:t + 1]).then_inc(squared, 1)

            @block.vector
            def _(dve):
                dve.wait_ge(squared, NT)
                nc.vector.tensor_scalar(rs[:, :], ss[:, :], 1.0 / D, EPS, ALU.mult, ALU.add).then_inc(meaned, 1)
                dve.wait_ge(rooted, 1)
                for t in range(NT):
                    nc.vector.tensor_scalar(X[:, t, :], X[:, t, :], rs[:, t:t + 1], None,
                                            ALU.mult).then_inc(scaled, 1)
                n = 0
                for t in range(NT):
                    for kk in range(2):
                        dve.wait_ge(turned, n + 1)
                        w = B if t == QT else P
                        dst = (xnT[:, 4 * kk:4 * kk + 4, t * P:t * P + w] if t < TT
                               else memT[:, 4 * kk:4 * kk + 4, (t - TT) * P:(t - TT + 1) * P])
                        src = ps[:, n % 4, :].rearrange("p (a q) -> p a q", a=4)[:, :, 0:w]
                        g = gm[:, 0 if t < TT else 1, 4 * kk:4 * kk + 4]
                        nc.vector.tensor_tensor(dst, src, bc(g, 2, w), ALU.mult).then_inc(stored, 1)
                        n += 1

            @block.tensor
            def _(pe):
                n = 0
                for t in range(NT):
                    pe.wait_ge(scaled, t + 1)
                    for kk in range(2):
                        if n >= 4:
                            pe.wait_ge(stored, n - 3)
                        for a in range(4):
                            k = 4 * kk + a
                            ins = nc.tensor.transpose(ps[:, n % 4, a * P:(a + 1) * P],
                                                      X[:, t, k * P:(k + 1) * P], c("ident"))
                        ins.then_inc(turned, 1)
                        n += 1


def stage_ml_proj(M):
    nc, I, O, xnT, brT, ps, c = (M[k] for k in ("nc", "I", "O", "xnT", "brT", "ps", "c"))
    row = M["row"]
    uT, sigo, cT = brT[:, 0:4, :], brT[:, 4:8, :], brT[:, 8:12, :]
    NOUT = 8 * NB3
    with Stage(nc, "mlp") as st:
        w = st.sb("w", [P, 2, KT, 512])
        wif = st.sb("wif", [P, KT, 8])
        sc = st.sb("state_conv", [24, 512])
        scT = st.sb("state_convT", [P, MH, B, 3])
        cw = st.sb("conv_w", [P, MH, 4])
        cb = st.sb("conv_b", [P, MH])
        bif = st.sb("b_if", [MH, 2])
        tail = st.sb("tail", [11, 512])
        sem = st.sem
        in_w, in_small, projected, kept, convolved, silued, st_turned, st_kept, tl_turned, tl_kept, out = (
            sem(n) for n in ("in_w", "in_small", "projected", "kept", "convolved", "silued", "st_turned",
                             "st_kept", "tl_turned", "tl_kept", "out"))
        chain = Chain(sem("conv_step"))
        out_pool = sem("out_pool")
        in_g = [sem("in_u"), sem("in_o")]
        wv = I["w_in"].rearrange("(k p) n -> p k n", p=P)
        with st.block() as block:
            @block.sync
            def _(sp):
                for g, col in enumerate((C_U, C_O)):
                    for k in range(KT):
                        sp.dma_start(w[:, g, k, :], wv[:, k, col:col + 512]).then_inc(in_g[g], 16)
                sp.dma_start(wif[:, :, :], wv[:, :, C_I:C_I + 8]).then_inc(in_w, 16)
                sp.wait_ge(tl_kept, 1)
                sp.dma_start(O["conv_prompt"].rearrange("o w n -> (o w) n"), tail[0:3, :]).then_inc(out, 16)
                sp.dma_start(O["conv_sample"][:, 2, :], tail[3:11, :]).then_inc(out, 16)
                sp.wait_ge(out, 32)

            @block.gpsimd
            def _(pool):
                pool.dma_start(sc[:, :], I["state_conv"].rearrange("b w n -> (b w) n")).then_inc(in_small, 16)
                for h in range(MH):
                    pool.dma_start(cw[:, h, :], I["conv_w"][:, h * MD:(h + 1) * MD].rearrange("w p -> p w"),
                                   allow_slow_non_contiguous=True).then_inc(in_small, 16)
                pool.dma_start(cb[:, :], I["conv_b"].rearrange("(h p) -> p h", p=P),
                               allow_slow_non_contiguous=True).then_inc(in_small, 16)
                pool.dma_start(bif[:, 0:1], I["b_igate"].rearrange("(h o) -> h o", o=1)).then_inc(in_small, 16)
                pool.dma_start(bif[:, 1:2], I["b_fgate"].rearrange("(h o) -> h o", o=1)).then_inc(in_small, 16)
                pool.dma_start(O["conv_sample"][:, 0:2, :], I["state_conv"][:, 1:3, :]).then_inc(out_pool, 16)
                pool.wait_ge(out_pool, 16)

            @block.tensor
            def _(pe):
                n = 0
                for j in range(8):
                    for b in range(NB3):
                        if n >= 6:
                            pe.wait_ge(kept, n - 5)
                        for k in range(KT):
                            if n % 12 == 0:
                                pe.wait_ge(in_g[j // 4], 16 * KT)
                            ins = nc.tensor.matmul(ps[:, n % 6, 0:BLK], w[:, j // 4, k, (j % 4) * P:(j % 4 + 1) * P],
                                                   xnT[:, k, b * BLK:(b + 1) * BLK],
                                                   start=(k == 0), stop=(k == KT - 1))
                        ins.then_inc(projected, 1)
                        n += 1
                    if j == 4:
                        pe.wait_ge(in_small, 16 * 8)
                        for h in range(MH):
                            ins = nc.tensor.transpose(ps[:, 6, h * 24:(h + 1) * 24],
                                                      sc[:, h * P:(h + 1) * P], c("ident")[0:24, 0:24])
                        ins.then_inc(st_turned, 1)
                        pe.wait_ge(kept, 4 * NB3)
                        for h in range(MH):
                            ins = nc.tensor.transpose(ps[0:11, 7, h * P:(h + 1) * P],
                                                      uT[:, h, S - 3:T], c("ident"))
                        ins.then_inc(tl_turned, 1)
                pe.wait_ge(in_w, 16)
                for q in range(2):
                    for b in range(NB3):
                        pe.wait_ge(kept, n - 5)
                        for k in range(KT):
                            ins = nc.tensor.matmul(ps[0:MH, n % 6, 0:BLK], wif[:, k, q * MH:(q + 1) * MH],
                                                   xnT[:, k, b * BLK:(b + 1) * BLK],
                                                   start=(k == 0), stop=(k == KT - 1))
                        ins.then_inc(projected, 1)
                        n += 1

            @block.scalar
            def _(act):
                n = 0
                for j in range(8):
                    for b in range(NB3):
                        act.wait_ge(projected, n + 1)
                        dst = (uT if j < 4 else sigo)[:, j % 4, b * BLK:(b + 1) * BLK]
                        nc.scalar.activation(dst, ps[:, n % 6, 0:BLK],
                                             ACT.Copy if j < 4 else ACT.Sigmoid).then_inc(kept, 1)
                        n += 1
                for q in range(2):
                    for b in range(NB3):
                        act.wait_ge(projected, n + 1)
                        nc.scalar.activation(row("ig" if q == 0 else "lf")[0:MH, b * BLK:(b + 1) * BLK],
                                             ps[0:MH, n % 6, 0:BLK], ACT.Identity,
                                             bias=bif[:, q:q + 1]).then_inc(kept, 1)
                        n += 1
                for h in range(MH):
                    act.wait_ge(convolved, h + 1)
                    nc.scalar.activation(cT[:, h, :], cT[:, h, :], ACT.Silu).then_inc(silued, 1)

            @block.vector
            def _(dve):
                dve.wait_ge(st_turned, 1)
                nc.vector.tensor_copy(scT[:, :, :, :].rearrange("p h b w -> p (h b w)"),
                                      ps[:, 6, 0:MH * 24]).then_inc(st_kept, 1)
                dve.wait_ge(tl_turned, 1)
                nc.vector.tensor_copy(tail[:, :], ps[0:11, 7, :]).then_inc(tl_kept, 1)
                dve.wait_ge(in_small, 16 * 8)
                dve.wait_ge(st_kept, 1)
                for h in range(MH):
                    chain.link(dve, nc.vector.tensor_scalar(cT[:, h, :], uT[:, h, :], cw[:, h, 3:4],
                                                            cb[:, h:h + 1], ALU.mult, ALU.add))
                    for tap in range(3):
                        d = 3 - tap
                        chain.link(dve, nc.vector.scalar_tensor_tensor(
                            cT[:, h, d:S], uT[:, h, 0:S - d], cw[:, h, tap:tap + 1], cT[:, h, d:S],
                            ALU.mult, ALU.add))
                        ins = nc.vector.scalar_tensor_tensor(
                            cT[:, h, S:T], scT[:, h, :, tap], cw[:, h, tap:tap + 1], cT[:, h, S:T],
                            ALU.mult, ALU.add)
                        if tap < 2:
                            chain.link(dve, ins)
                    ins.then_inc(convolved, 1)


def stage_mlstm(M):
    nc, I, O, brT, ps, c = (M[k] for k in ("nc", "I", "O", "brT", "ps", "c"))
    row = M["row"]
    uT, sigo, cT = brT[:, 0:4, :], brT[:, 4:8, :], brT[:, 8:12, :]
    with Stage(nc, "ml") as st:
        qT = st.sb("qT", [P, MH, T])
        kT = st.sb("kT", [P, MH, T])
        ktm = brT[:, 0:4, 0:S].rearrange("p h (c e) -> p c h e", e=MD)
        va = st.sb("va", [P, NCK, MH, MD + 1])
        vs = st.sb("vs", [B, MH, MD])
        vsT = st.sb("vsT", [P, MH, B])
        bcs = st.sb("bcs", [P, 4, MH, B])
        tok = st.sb("tok", [P, NCK, 4, MH])
        m0 = st.sb("m0", [MH, B])
        gain = st.sb("gain", [P, MH])
        mS = st.sb("mS", [MH, B])
        with Stage(nc, "mlq") as s2:
            w3 = s2.sb("w3", [P, 3, MH, MD])
            tmp = row("tmp")[0:MH, :]
            dg = s2.sb("dg", [MH, 4, MH, B])
            sm = s2.sb("sm", [MH, 4, B])
            sem = s2.sem
            in_w, projected, kept, stepA, softened, rows_ready, exped, turned, tkept, diag, spread, in_m = (
                sem(n) for n in ("in_w", "projected", "kept", "stepA", "softened", "rows_ready", "exped",
                                 "turned", "tkept", "diag", "spread", "in_m"))
            chain = Chain(sem("gate_step"))
            out = sem("out")
            ones_set = sem("ones_set")
            with s2.block() as block:
                @block.sync
                def _(sp):
                    for i, n in enumerate(("w_ml_q", "w_ml_k", "w_ml_v")):
                        sp.dma_start(w3[:, i, :, :], I[n].rearrange("h d e -> d h e")).then_inc(in_w, 16)
                    sp.dma_start(m0[:, :], I["state_m"].rearrange("b h -> h b"),
                                 allow_slow_non_contiguous=True).then_inc(in_m, 16)
                    sp.dma_start(gain[:, :], I["ml_norm"].rearrange("h e -> e h"),
                                 allow_slow_non_contiguous=True).then_inc(in_m, 16)
                    sp.wait_ge(rows_ready, 1)
                    sp.dma_start(O["m_prompt"].rearrange("o h -> h o"), row("m")[0:MH, S - 1:S]).then_inc(out, 16)
                    sp.dma_start(O["m_sample"].rearrange("b h -> h b"), mS[:, :],
                                 allow_slow_non_contiguous=True).then_inc(out, 16)
                    sp.wait_ge(out, 32)

                @block.gpsimd
                def _(pool):
                    nc.gpsimd.memset(va[:, :, :, MD:MD + 1], 1.0).then_inc(ones_set, 1)
                    pool.wait_ge(ones_set, 1)

                @block.tensor
                def _(pe):
                    pe.wait_ge(in_w, 48)
                    n = 0
                    for h in range(MH):
                        for i in range(2):
                            for b in range(NB3):
                                if n >= 6:
                                    pe.wait_ge(kept, n - 5)
                                nc.tensor.matmul(ps[:, n % 6, 0:BLK], w3[:, i, h, :],
                                                 cT[:, h, b * BLK:(b + 1) * BLK],
                                                 start=True, stop=True).then_inc(projected, 1)
                                n += 1
                    for t in range(NCK):
                        pe.wait_ge(kept, n - 5)
                        for h in range(MH):
                            ins = nc.tensor.matmul(ps[:, n % 6, h * MD:(h + 1) * MD],
                                                   uT[:, h, t * L:(t + 1) * L], w3[:, 2, h, :],
                                                   start=True, stop=True)
                        ins.then_inc(projected, 1)
                        n += 1
                    pe.wait_ge(kept, n - 5)
                    for h in range(MH):
                        ins = nc.tensor.matmul(ps[0:B, n % 6, h * MD:(h + 1) * MD], uT[:, h, S:T],
                                               w3[:, 2, h, :], start=True, stop=True)
                    ins.then_inc(projected, 1)
                    n += 1
                    pe.wait_ge(kept, n - 5)
                    for h in range(MH):
                        ins = nc.tensor.matmul(ps[:, n % 6, h * B:(h + 1) * B], w3[:, 2, h, :], uT[:, h, S:T],
                                               start=True, stop=True)
                    ins.then_inc(projected, 1)
                    n += 1
                    for t in range(NCK):
                        pe.wait_ge(kept, n - 5)
                        for h in range(MH):
                            ins = nc.tensor.matmul(ps[:, n % 6, h * MD:(h + 1) * MD],
                                                   cT[:, h, t * L:(t + 1) * L], w3[:, 1, h, :],
                                                   start=True, stop=True)
                        ins.then_inc(projected, 1)
                        n += 1
                    pe.wait_ge(rows_ready, 2)
                    for t in range(NCK):
                        if t >= 1:
                            pe.wait_ge(tkept, t)
                        nc.tensor.transpose(ps[:, 6, 0:P], row("stack")[:, t * L:(t + 1) * L],
                                            c("ident")).then_inc(turned, 1)
                    pe.wait_ge(diag, 4)
                    nc.tensor.matmul(ps[:, 7, 0:P], c("ones")[0:MH, :],
                                     dg[:, :, :, :].rearrange("p a h b -> p (a h b)"),
                                     start=True, stop=True).then_inc(spread, 1)

                @block.scalar
                def _(act):
                    act.wait_ge(stepA, 1)
                    nc.scalar.activation(tmp[:, :], tmp[:, :], ACT.Exp, scale=-1.0).then_inc(softened, 1)
                    act.wait_ge(softened, 1)
                    nc.scalar.activation(tmp[:, :], tmp[:, :], ACT.Ln, bias=1.0).then_inc(softened, 1)
                    n = 0
                    for h in range(MH):
                        for i in range(2):
                            for b in range(NB3):
                                act.wait_ge(projected, n + 1)
                                nc.scalar.activation((qT if i == 0 else kT)[:, h, b * BLK:(b + 1) * BLK],
                                                     ps[:, n % 6, 0:BLK], ACT.Copy,
                                                     scale=MD ** -0.5 if i == 0 else 1.0).then_inc(kept, 1)
                                n += 1
                    for t in range(NCK):
                        act.wait_ge(projected, n + 1)
                        nc.scalar.activation(va[:, t, :, 0:MD], ps[:, n % 6, :].rearrange("p (h e) -> p h e", h=MH),
                                             ACT.Copy).then_inc(kept, 1)
                        n += 1
                    act.wait_ge(projected, n + 1)
                    nc.scalar.activation(vs[:, :, :].rearrange("p h e -> p (h e)"), ps[0:B, n % 6, :],
                                         ACT.Copy).then_inc(kept, 1)
                    n += 1
                    act.wait_ge(projected, n + 1)
                    nc.scalar.activation(vsT[:, :, :].rearrange("p h e -> p (h e)"), ps[:, n % 6, 0:MH * B],
                                         ACT.Copy).then_inc(kept, 1)
                    n += 1
                    for t in range(NCK):
                        act.wait_ge(projected, n + 1)
                        nc.scalar.activation(ktm[:, t, :, :], ps[:, n % 6, :].rearrange("p (h e) -> p h e", h=MH),
                                             ACT.Copy).then_inc(kept, 1)
                        n += 1
                    act.wait_ge(rows_ready, 1)
                    for q in (32, 64, 96):
                        nc.scalar.activation(row("stack")[q:q + MH, 0:S], row("stack")[q:q + MH, 0:S],
                                             ACT.Exp, scale=(-1.0 if q == 96 else 1.0)).then_inc(exped, 1)
                    nc.scalar.activation(sm[:, :, :], sm[:, :, :], ACT.Exp).then_inc(exped, 1)

                @block.vector
                def _(dve):
                    lf, ig, mm, mr, bb, rst = (row(x) for x in ("lf", "ig", "M", "m", "b", "reset"))
                    nc.vector.scalar_tensor_tensor(tmp[:, :], lf[0:MH, :], -1.0, lf[0:MH, :], ALU.mult, ALU.max).then_inc(stepA, 1)
                    chain.link(dve, nc.vector.memset(row("stack")[:, 0:S], 0.0))
                    chain.link(dve, nc.vector.memset(rst[0:MH, 0:S], 1.0))
                    chain.link(dve, nc.vector.memset(
                        rst[0:MH, 0:S].rearrange("p (c l) -> p c l", l=L)[:, :, 0:1], 0.0))
                    chain.link(dve, nc.vector.tensor_scalar(lf[0:MH, :], lf[0:MH, :], 0.0, None, ALU.min))
                    dve.wait_ge(softened, 2)
                    chain.link(dve, nc.vector.tensor_tensor(lf[0:MH, :], lf[0:MH, :], tmp[:, :], ALU.subtract))
                    chain.link(dve, nc.vector.tensor_tensor_scan(bb[0:MH, 0:S], rst[0:MH, 0:S], lf[0:MH, 0:S],
                                                                 0.0, ALU.mult, ALU.add))
                    chain.link(dve, nc.vector.tensor_tensor_scan(mr[0:MH, 0:S], lf[0:MH, 0:S], ig[0:MH, 0:S],
                                                                 0.0, ALU.add, ALU.max))
                    chain.link(dve, nc.vector.tensor_tensor(mm[0:MH, 0:S], mr[0:MH, 0:S], bb[0:MH, 0:S],
                                                            ALU.subtract))
                    stack = row("stack")
                    chain.link(dve, nc.vector.tensor_tensor(stack[0:MH, 0:S], ig[0:MH, 0:S], bb[0:MH, 0:S],
                                                            ALU.subtract))
                    chain.link(dve, nc.vector.tensor_copy(stack[96:96 + MH, 0:S], mr[0:MH, 0:S]))
                    ch = lambda r, p0: r[p0:p0 + MH, 0:S].rearrange("p (c l) -> p c l", l=L)
                    chain.link(dve, nc.vector.tensor_scalar(stack[32:32 + MH, 0:L], mm[0:MH, 0:L], -1.0, None,
                                                            ALU.mult))
                    chain.link(dve, nc.vector.tensor_tensor(
                        ch(stack, 32)[:, 1:, :], ch(mr, 0)[:, 0:NCK - 1, L - 1:L].to_broadcast([MH, NCK - 1, L]),
                        ch(mm, 0)[:, 1:, :], ALU.subtract))
                    chain.link(dve, nc.vector.tensor_tensor(
                        ch(stack, 64), ch(stack, 0), ch(mm, 0)[:, :, L - 1:L].to_broadcast([MH, NCK, L]),
                        ALU.subtract))
                    chain.link(dve, nc.vector.tensor_scalar(sm[:, 0, 0:1], mm[0:MH, L - 1:L], -1.0, None,
                                                            ALU.mult))
                    chain.link(dve, nc.vector.tensor_tensor(
                        sm[:, 0, 1:NCK], ch(mr, 0)[:, 0:NCK - 1, L - 1], ch(mm, 0)[:, 1:, L - 1], ALU.subtract))
                    dve.wait_ge(in_m, 32)
                    chain.link(dve, nc.vector.tensor_tensor(sm[:, 1, :], lf[0:MH, S:T], m0[:, :], ALU.add))
                    chain.link(dve, nc.vector.tensor_tensor(mS[:, :], sm[:, 1, :], ig[0:MH, S:T], ALU.max))
                    chain.link(dve, nc.vector.tensor_tensor(sm[:, 1, :], sm[:, 1, :], mS[:, :], ALU.subtract))
                    chain.link(dve, nc.vector.tensor_tensor(sm[:, 2, :], ig[0:MH, S:T], mS[:, :], ALU.subtract))
                    nc.vector.tensor_scalar(sm[:, 3, :], mS[:, :], -1.0, None, ALU.mult).then_inc(rows_ready, 1)
                    dve.wait_ge(exped, 4)
                    for a in range(4):
                        ins = nc.vector.tensor_tensor(dg[:, a, :, :], bc(sm[:, a, :], 1, MH),
                                                      bc(c("ident")[0:MH, 0:MH], 2, B), ALU.mult)
                        ins.then_inc(diag, 1)
                    nc.vector.memset(tmp[:, 0:1], 0.0).then_inc(rows_ready, 1)
                    for t in range(NCK):
                        dve.wait_ge(turned, t + 1)
                        nc.vector.tensor_copy(tok[:, t, :, :],
                                              ps[:, 6, 0:P].rearrange("p (a q) -> p a q", a=4)[:, :, 0:MH]
                                              ).then_inc(tkept, 1)
                    dve.wait_ge(spread, 1)
                    chain.link(dve, nc.vector.tensor_copy(
                        bcs[:, :, :, :].rearrange("p a h b -> p (a h b)"), ps[:, 7, 0:P]))
        mlstm_chunks(M, st, qT, kT, ktm, va, bcs, tok, gain)
        mlstm_sample(M, st, qT, kT, vs, vsT, bcs, gain)


def mlstm_chunks(M, st, qT, kT, ktm, va, bcs, tok, gain):
    nc, I, O, brT, ps, c = (M[k] for k in ("nc", "I", "O", "brT", "ps", "c"))
    row = M["row"]
    sigo, Htm = brT[:, 4:8, 0:S], brT[:, 8:12, 0:S].rearrange("p h (c e) -> p h c e", e=MD)
    N = NCK * MH
    with Stage(nc, "mlc") as s2:
        ca = s2.sb("state", [P, MH, MD + 1])
        selm = s2.sb("selm", [MH, MH, P])
        mb = s2.sb("mb", [P, 2, L])
        wgt = s2.sb("wgt", [P, 2, L])
        wT = s2.sb("wT", [P, 2, L])
        kw = s2.sb("kw", [P, 2, MD])
        inter = s2.sb("inter", [P, 2, MD + 1])
        num = s2.sb("num", [P, 2, MD + 1])
        den = s2.sb("den", [P, 2, 1])
        ss = s2.sb("ss", [P, MH, NCK])
        junk = s2.sb("junk", [P, MD])
        sem = s2.sem
        (prep, scored, masked, weighed, wready, kready, read, done_pe, interk, hdone, stated, squared, meaned,
         rooted, normed, turned, gated, out) = (
            sem(n) for n in ("prep", "scored", "masked", "weighed", "wready", "kready", "read", "done_pe",
                             "interk", "hdone", "stated", "squared", "meaned", "rooted", "normed", "turned",
                             "gated", "out"))
        chain = Chain(sem("step"))
        with s2.block() as block:
            @block.tensor
            def _(pe):
                pe.wait_ge(prep, 1)

                def first(n):
                    t, h = n // MH, n % MH
                    if n >= 2:
                        pe.wait_ge(wready, n - 1)
                    nc.tensor.matmul(ps[:, n % 2, 0:L], selm[:, h, :], row("M")[0:MH, t * L:(t + 1) * L],
                                     start=True, stop=True)
                    nc.tensor.matmul(ps[:, n % 2, L:2 * L], kT[:, h, t * L:(t + 1) * L],
                                     qT[:, h, t * L:(t + 1) * L], start=True, stop=True).then_inc(scored, 1)

                def second(n):
                    t, h = n // MH, n % MH
                    if n >= 2:
                        pe.wait_ge(hdone, n - 1)
                        pe.wait_ge(interk, n - 1)
                        pe.wait_ge(stated, n - 1)
                    b = 2 + n % 2
                    pe.wait_ge(stated, max(n - MH + 1, 0) + 1)
                    nc.tensor.matmul(ps[:, b, 0:MD + 1], qT[:, h, t * L:(t + 1) * L], ca[:, h, :],
                                     start=True, stop=True).then_inc(read, 1)
                    pe.wait_ge(wready, n + 1)
                    nc.tensor.matmul(ps[:, b + 2, 0:MD + 1], wT[:, n % 2, :], va[:, t, h, :],
                                     start=True, stop=True)
                    pe.wait_ge(kready, n + 1)
                    nc.tensor.matmul(ps[:, b + 4, 0:MD + 1], kw[:, n % 2, :], va[:, t, h, :],
                                     start=True, stop=True).then_inc(done_pe, 1)

                first(0)
                for n in range(N):
                    if n + 1 < N:
                        first(n + 1)
                    second(n)
                for h in range(MH):
                    for half in range(2):
                        n = 2 * h + half
                        pe.wait_ge(normed, h + 1)
                        if n >= 2:
                            pe.wait_ge(gated, n - 1)
                        for a in range(4):
                            ins = nc.tensor.transpose(ps[:, n % 2, a * P:(a + 1) * P],
                                                      Htm[:, h, 4 * half + a, :], c("ident"))
                        ins.then_inc(turned, 1)

            @block.gpsimd
            def _(pool):
                for n in range(N):
                    t, h = n // MH, n % MH
                    if n >= 2:
                        pool.wait_ge(done_pe, n - 1)
                    nc.gpsimd.tensor_scalar(kw[:, n % 2, :], ktm[:, t, h, :], tok[:, t, 2, h:h + 1], None,
                                            ALU.mult).then_inc(kready, 1)
                pool.wait_ge(meaned, 1)
                nc.gpsimd.tensor_tensor(ss[:, :, :], ss[:, :, :],
                                        bc(c("mhalf").to_broadcast([P, NCK]), 1, MH), ALU.pow).then_inc(rooted, 1)

            @block.scalar
            def _(act):
                for n in range(N):
                    t, h = n // MH, n % MH
                    act.wait_ge(masked, n + 1)
                    if n >= 2:
                        act.wait_ge(wready, n - 1)
                    nc.scalar.activation(wgt[:, n % 2, :], mb[:, n % 2, :], ACT.Exp, scale=-1.0,
                                         bias=tok[:, t, 0, h:h + 1]).then_inc(weighed, 1)
                    act.wait_ge(read, n + 1)
                    if n >= 2:
                        act.wait_ge(hdone, n - 1)
                    nc.scalar.activation(inter[:, n % 2, :], ps[:, 2 + n % 2, 0:MD + 1], ACT.Copy,
                                         scale=tok[:, t, 1, h:h + 1]).then_inc(interk, 1)
                for h in range(MH):
                    for t in range(NCK):
                        i = h * NCK + t
                        act.wait_ge(hdone, N)
                        if i:
                            act.wait_ge(squared, i)
                        nc.scalar.activation(junk[:, :], Htm[:, h, t, :], ACT.Square,
                                             accum_out=ss[:, h, t:t + 1]).then_inc(squared, 1)

            @block.vector
            def _(dve):
                chain.link(dve, nc.vector.tensor_copy(selm[:, :, :],
                                                      bc(c("ident")[0:MH, 0:MH], 2, P)))
                nc.vector.memset(ca[:, :, :], 0.0).then_inc(stated, 1)
                nc.vector.memset(junk[:, :], 0.0).then_inc(prep, 1)
                dve.wait_ge(prep, 1)

                def mask(n):
                    dve.wait_ge(scored, n + 1)
                    if n >= 2:
                        dve.wait_ge(weighed, n - 1)
                    nc.vector.tensor_tensor(mb[:, n % 2, :], ps[:, n % 2, 0:L], c("future"),
                                            ALU.add).then_inc(masked, 1)

                mask(0)
                for n in range(N):
                    t, h = n // MH, n % MH
                    i = n % 2
                    if n + 1 < N and n >= 0:
                        pass
                    dve.wait_ge(weighed, n + 1)
                    if n >= 2:
                        dve.wait_ge(done_pe, n - 1)
                    nc.vector.tensor_tensor(wT[:, i, :], wgt[:, i, :], ps[:, i, L:2 * L],
                                            ALU.mult).then_inc(wready, 1)
                    if n + 1 < N:
                        mask(n + 1)
                    dve.wait_ge(done_pe, n + 1)
                    dve.wait_ge(interk, n + 1)
                    chain.link(dve, nc.vector.tensor_tensor(num[:, i, :], ps[:, 4 + i, 0:MD + 1],
                                                            inter[:, i, :], ALU.add))
                    nc.vector.scalar_tensor_tensor(ca[:, h, :], ca[:, h, :], bcs[:, 0, h, t:t + 1],
                                                   ps[:, 6 + i, 0:MD + 1], ALU.mult, ALU.add).then_inc(stated, 1)
                    chain.link(dve, nc.vector.tensor_scalar(den[:, i, :], num[:, i, MD:MD + 1], -1.0,
                                                            tok[:, t, 3, h:h + 1], ALU.mult, ALU.max))
                    chain.link(dve, nc.vector.tensor_scalar(den[:, i, :], num[:, i, MD:MD + 1], den[:, i, :],
                                                            None, ALU.max))
                    chain.link(dve, nc.vector.reciprocal(den[:, i, :], den[:, i, :]))
                    nc.vector.tensor_scalar(Htm[:, h, t, :], num[:, i, 0:MD], den[:, i, :], None,
                                            ALU.mult).then_inc(hdone, 1)
                dve.wait_ge(squared, N)
                nc.vector.tensor_scalar(ss[:, :, :], ss[:, :, :], 1.0 / MD, EPS, ALU.mult,
                                        ALU.add).then_inc(meaned, 1)
                dve.wait_ge(rooted, 1)
                for h in range(MH):
                    nc.vector.tensor_tensor(Htm[:, h, :, :], Htm[:, h, :, :], bc(ss[:, h, :], 2, MD),
                                            ALU.mult).then_inc(normed, 1)
                for n in range(2 * MH):
                    h, half = n // 2, n % 2
                    dve.wait_ge(turned, n + 1)
                    dst = sigo[:, h, half * 512:(half + 1) * 512]
                    nc.vector.scalar_tensor_tensor(dst, ps[:, n % 2, :], gain[:, h:h + 1], dst,
                                                   ALU.mult, ALU.mult).then_inc(gated, 1)

            @block.sync
            def _(sp):
                sp.wait_ge(stated, N + 1)
                sp.dma_start(O["C_prompt"].rearrange("o h d e -> d (o h) e"), ca[:, :, 0:MD]).then_inc(out, 16)
                sp.dma_start(O["n_prompt"].rearrange("o h d -> d (o h)"), ca[:, :, MD],
                             allow_slow_non_contiguous=True).then_inc(out, 16)
                sp.wait_ge(out, 32)


def mlstm_sample(M, st, qT, kT, vs, vsT, bcs, gain):
    nc, I, O, brT, ps, c = (M[k] for k in ("nc", "I", "O", "brT", "ps", "c"))
    sigo = brT[:, 4:8, S:T]
    HB = MH * B
    with Stage(nc, "mls") as s2:
        C0 = s2.sb("C0", [P, 2, 4, MD])
        C1 = s2.sb("C1", [P, 2, 4, MD])
        n0 = s2.sb("n0", [HB, MD])
        nT = s2.sb("nT", [P, MH, B])
        sel = s2.sb("sel", [B, B, P])
        pr = s2.sb("pr", [P, 2, HB])
        kwt = s2.sb("kwt", [P, MH, B])
        hT = s2.sb("hT", [P, MH, B])
        t1 = s2.sb("t1", [P, MH, B])
        t2 = s2.sb("t2", [P, MH, B])
        nout = s2.sb("nout", [HB, MD])
        sem = s2.sem
        n_in, selr, nturn, nk, prods, dots, fed, spreadv, updated, stored, sq, ssum, pooled, rooted, nn, nkept, out, oth = (
            sem(n) for n in ("n_in", "selr", "nturn", "nk", "prods", "dots", "fed", "spreadv",
                             "updated", "stored", "sq", "ssum", "pooled", "rooted", "nn", "nkept", "out", "oth"))
        chain = Chain(sem("step"))
        c_in, cout = ([sem(f"{n}{q}") for q in range(2)] for n in ("c_in", "cout"))
        qs, ks = qT[:, :, S:T], kT[:, :, S:T]
        with s2.block() as block:
            @block.sync
            def _(sp):
                for h in range(MH):
                    sp.dma_start(n0[h * B:(h + 1) * B, :], I["state_n"][:, h, :]).then_inc(n_in, 16)
                for b in range(B):
                    if b >= 2:
                        sp.wait_ge(updated, b - 1)
                        sp.wait_ge(fed, b - 1)
                    sp.dma_start(C0[:, b % 2, :, :], I["state_C"][b].rearrange("h d e -> d h e")).then_inc(c_in[b % 2], 16)
                sp.wait_ge(nkept, 1)
                for h in range(MH):
                    sp.dma_start(O["n_sample"][:, h, :], nout[h * B:(h + 1) * B, :]).then_inc(out, 16)
                sp.wait_ge(out, 64)

            @block.gpsimd
            def _(pool):
                for b in range(B):
                    pool.wait_ge(updated, b + 1)
                    pool.dma_start(O["C_sample"][b].rearrange("h d e -> d h e"), C1[:, b % 2, :, :]).then_inc(cout[b % 2], 16)
                pool.wait_ge(pooled, 1)
                nc.gpsimd.tensor_tensor(t2[:, :, :], t2[:, :, :], bc(c("mhalf").to_broadcast([P, B]), 1, MH),
                                        ALU.pow).then_inc(rooted, 1)
                for q in range(2):
                    pool.wait_ge(cout[q], 16 * B // 2)

            @block.tensor
            def _(pe):
                pe.wait_ge(n_in, 64)
                nc.tensor.transpose(ps[:, 0, 0:HB], n0[:, :], c("ident")[0:HB, 0:HB]).then_inc(nturn, 1)
                pe.wait_ge(prods, 1)
                nc.tensor.matmul(ps[:, 1, 0:2 * HB], c("ones"), pr[:, :, :].rearrange("p a q -> p (a q)"),
                                 start=True, stop=True).then_inc(dots, 1)
                pe.wait_ge(selr, 1)
                for b in range(B):
                    pe.wait_ge(c_in[b % 2], 16 * (b // 2 + 1))
                    for h in range(MH):
                        ins = nc.tensor.matmul(ps[:, 2, h * B + b:h * B + b + 1], C0[:, b % 2, h, :],
                                               qT[:, h, S + b:S + b + 1], start=True, stop=True)
                    ins.then_inc(fed, 1)
                    if b >= 2:
                        pe.wait_ge(updated, b - 1)
                    nc.tensor.matmul(ps[:, 4 + b % 2, :], sel[:, b, :], vs[:, :, :].rearrange("p h e -> p (h e)"),
                                     start=True, stop=True).then_inc(spreadv, 1)
                pe.wait_ge(sq, 1)
                nc.tensor.matmul(ps[:, 3, 0:HB], c("ones"), t1[:, :, :].rearrange("p h b -> p (h b)"),
                                 start=True, stop=True).then_inc(ssum, 1)
                pe.wait_ge(nn, 1)
                nc.tensor.transpose(ps[0:HB, 6, 0:P], nT[:, :, :].rearrange("p h b -> p (h b)"),
                                    c("ident")).then_inc(oth, 1)

            @block.vector
            def _(dve):
                P1 = lambda x: x.rearrange("p (h b) -> p h b", h=MH)
                chain.link(dve, nc.vector.tensor_copy(sel[:, :, :], bc(c("ident")[0:B, 0:B], 2, P)))
                nc.vector.tensor_tensor(kwt[:, :, :], ks, bcs[:, 2, :, :], ALU.mult).then_inc(selr, 1)
                dve.wait_ge(selr, 1)
                dve.wait_ge(nturn, 1)
                chain.link(dve, nc.vector.tensor_copy(nT[:, :, :], P1(ps[:, 0, 0:HB])))
                chain.link(dve, nc.vector.tensor_tensor(P1(pr[:, 0, :]), qs, nT[:, :, :], ALU.mult))
                nc.vector.tensor_tensor(P1(pr[:, 1, :]), qs, ks, ALU.mult).then_inc(prods, 1)
                chain.link(dve, nc.vector.tensor_tensor(nT[:, :, :], nT[:, :, :], bcs[:, 1, :, :], ALU.mult))
                nc.vector.tensor_tensor(nT[:, :, :], nT[:, :, :], kwt[:, :, :], ALU.add).then_inc(nn, 1)
                for b in range(B):
                    dve.wait_ge(c_in[b % 2], 16 * (b // 2 + 1))
                    dve.wait_ge(spreadv, b + 1)
                    if b >= 2:
                        dve.wait_ge(cout[b % 2], 16 * (b // 2))
                    for h in range(MH):
                        ins = nc.vector.tensor_scalar(C1[:, b % 2, h, :], ps[:, 4 + b % 2, h * MD:(h + 1) * MD],
                                                      kwt[:, h, b:b + 1], None, ALU.mult)
                    chain.link(dve, ins)
                    for h in range(MH):
                        ins = nc.vector.scalar_tensor_tensor(C1[:, b % 2, h, :], C0[:, b % 2, h, :],
                                                             bcs[:, 1, h, b:b + 1], C1[:, b % 2, h, :],
                                                             ALU.mult, ALU.add)
                    ins.then_inc(updated, 1)
                dve.wait_ge(dots, 1)
                dve.wait_ge(fed, B)
                chain.link(dve, nc.vector.tensor_tensor(t1[:, :, :], P1(ps[:, 1, HB:2 * HB]), bcs[:, 2, :, :],
                                                        ALU.mult))
                chain.link(dve, nc.vector.tensor_tensor(hT[:, :, :], vsT[:, :, :], t1[:, :, :], ALU.mult))
                chain.link(dve, nc.vector.tensor_tensor(t2[:, :, :], P1(ps[:, 2, 0:HB]), bcs[:, 1, :, :],
                                                        ALU.mult))
                chain.link(dve, nc.vector.tensor_tensor(hT[:, :, :], hT[:, :, :], t2[:, :, :], ALU.add))
                chain.link(dve, nc.vector.tensor_tensor(t2[:, :, :], P1(ps[:, 1, 0:HB]), bcs[:, 1, :, :],
                                                        ALU.mult))
                chain.link(dve, nc.vector.tensor_tensor(t2[:, :, :], t2[:, :, :], t1[:, :, :], ALU.add))
                chain.link(dve, nc.vector.scalar_tensor_tensor(t2[:, :, :], t2[:, :, :], -1.0, t2[:, :, :],
                                                               ALU.mult, ALU.max))
                chain.link(dve, nc.vector.tensor_tensor(t2[:, :, :], t2[:, :, :], bcs[:, 3, :, :], ALU.max))
                chain.link(dve, nc.vector.reciprocal(t2[:, :, :], t2[:, :, :]))
                chain.link(dve, nc.vector.tensor_tensor(hT[:, :, :], hT[:, :, :], t2[:, :, :], ALU.mult))
                nc.vector.tensor_tensor(t1[:, :, :], hT[:, :, :], hT[:, :, :], ALU.mult).then_inc(sq, 1)
                dve.wait_ge(ssum, 1)
                nc.vector.tensor_scalar(t2[:, :, :], P1(ps[:, 3, 0:HB]), 1.0 / MD, EPS, ALU.mult,
                                        ALU.add).then_inc(pooled, 1)
                dve.wait_ge(rooted, 1)
                chain.link(dve, nc.vector.tensor_tensor(hT[:, :, :], hT[:, :, :], t2[:, :, :], ALU.mult))
                chain.link(dve, nc.vector.tensor_tensor(hT[:, :, :], hT[:, :, :], bc(gain[:, :], 2, B), ALU.mult))
                chain.link(dve, nc.vector.tensor_tensor(sigo, sigo, hT[:, :, :], ALU.mult))
                dve.wait_ge(oth, 1)
                nc.vector.tensor_copy(nout[:, :], ps[0:HB, 6, 0:P]).then_inc(nkept, 1)


def stage_tok_proj(M, A):
    nc, I, O, xnT, x2, ps, c, memT = (M[k] for k in ("nc", "I", "O", "xnT", "x2", "ps", "c", "memT"))
    wv = I["w_in"].rearrange("(k p) n -> p k n", p=P)
    mv = I["w_mem_kv"].rearrange("(k p) n -> p k n", p=P)
    groups = [(wv, C_Q, 512, A["q"]), (wv, C_G, 280, A["gk"]), (wv, C_KVS, 512, A["kvsw"]),
              (wv, C_MQ, 512, A["mq"]), (mv, 0, 512, A["kvm"]), (mv, 512, 512, A["kvm"])]
    wbuf = x2[:, :, :].rearrange("p t d -> p (t d)")[:, 0:2 * KT * 512].rearrange(
        "p (s k n) -> p s k n", s=2, k=KT)
    with Stage(nc, "tok") as st:
        sem = st.sem
        in_w = [sem(f"in_w{g}") for g in range(6)]
        projected, kept, cleared = (sem(n) for n in ("projected", "kept", "cleared"))
        steps = [(g, t) for g in range(6) for t in (range(TT) if g < 4 else range(2))]
        last = {g: max(n for n, s in enumerate(steps) if s[0] == g) for g in range(6)}
        with st.block() as block:
            @block.sync
            def _(sp):
                for g, (w, col, n, _) in enumerate(groups):
                    if g >= 2:
                        sp.wait_ge(projected, last[g - 2] + 1)
                    for k in range(0, KT, 2):
                        sp.dma_start(wbuf[:, g % 2, k:k + 2, 0:n], w[:, k:k + 2, col:col + n]
                                     ).then_inc(in_w[g], 16)

            @block.gpsimd
            def _(pool):
                for a in ("q", "gk", "kvsw", "mq"):
                    nc.gpsimd.memset(A[a][:, QT, :], 0.0).then_inc(cleared, 1)

            @block.tensor
            def _(pe):
                for n, (g, t) in enumerate(steps):
                    if n >= 6:
                        pe.wait_ge(kept, n - 5)
                    if t == 0:
                        pe.wait_ge(in_w[g], 64)
                    m = B if t == QT else P
                    w = groups[g][2]
                    src = xnT if g < 4 else memT
                    for k in range(KT):
                        ins = nc.tensor.matmul(ps[0:m, n % 6, 0:w], src[:, k, t * P:t * P + m],
                                               wbuf[:, g % 2, k, 0:w], start=(k == 0), stop=(k == KT - 1))
                    ins.then_inc(projected, 1)

            @block.scalar
            def _(act):
                act.wait_ge(cleared, 4)
                for n, (g, t) in enumerate(steps):
                    act.wait_ge(projected, n + 1)
                    m = B if t == QT else P
                    w, dst = groups[g][2:]
                    o = 512 if g == 5 else 0
                    nc.scalar.activation(dst[0:m, t, o:o + w], ps[0:m, n % 6, 0:w], ACT.Copy).then_inc(kept, 1)


def stage_prep(M, A):
    nc, I, O, x2, ps, c = (M[k] for k in ("nc", "I", "O", "x2", "ps", "c"))
    flat = x2[:, :, :].rearrange("p t d -> p (t d)")
    q, gk, kvsw, mq, kvm, qr = (A[k] for k in ("q", "gk", "kvsw", "mq", "kvm", "qr"))
    q4 = q[:, :, :].rearrange("p t (h d) -> p t h d", d=HD)
    kv5 = kvsw[:, :, :].rearrange("p t (r c d) -> p t r c d", c=2, d=HD)
    mq4 = mq[:, :, :].rearrange("p t (h d) -> p t h d", d=XD)
    km4 = kvm[:, :, :].rearrange("p t (h c d) -> p t h c d", c=2, d=XD)
    qr4 = qr[:, :, :].rearrange("p t (h d) -> p t h d", d=HD)
    norms = [(q4, H, HD, TT), (kv5[:, :, :, 0, :], 4, HD, TT), (mq4, XH, XD, TT), (km4[:, :, :, 0, :], XH, XD, 2)]
    at = [0, 72, 108, 144, 152]
    with Stage(nc, "prep") as st:
        ss = st.sb("ss", [P, 152])
        gq, gs, gw = (st.sb(n, [P, HD]) for n in ("g_q", "g_slc", "g_win"))
        gmq, gmk = (st.sb(n, [P, XD]) for n in ("g_mq", "g_mk"))
        t1 = st.sb("t1", [P, TT, H, HALF])
        t2 = st.sb("t2", [P, TT, H, HALF])
        sem = st.sem
        in_g, squared, summed, meaned, rooted, qready, qcopied, kready, mready, out, gated = (
            sem(n) for n in ("in_g", "squared", "summed", "meaned", "rooted", "qready", "qcopied", "kready",
                             "mready", "out", "gated"))
        chain = Chain(sem("step"))
        mchain = Chain(sem("mem_step"))
        buf = [flat[:, 0:4608], flat[:, 4608:9216]]

        def sqv(n):
            _, h, d, t = norms[n]
            return buf[n % 2][:, 0:t * h * d].rearrange("p (t h d) -> p t h d", h=h, d=d)

        with st.block() as block:
            @block.sync
            def _(sp):
                for dst, n in ((gq, "q_norm"), (gs, "k_norm_slc"), (gw, "k_norm_win"), (gmq, "mem_q_norm"),
                               (gmk, "mem_k_norm")):
                    sp.dma_start(dst[:, :], I[n].partition_broadcast(P)).then_inc(in_g, 16)
                raw = gk[:, :, 24:280]
                sp.dma_start(O["kv_cmp_prompt"].rearrange("o (t p) g c d -> p (o t) (g c d)", p=P),
                             raw[:, 0:QT, :]).then_inc(out, 16)
                sp.dma_start(O["kv_cmp_sample"].rearrange("b o g c d -> b (o g c d)"), raw[0:B, QT, :]).then_inc(out, 16)
                sp.wait_ge(kready, 1)
                sp.dma_start(O["kv_slc_prompt"].rearrange("o (t p) g c d -> p (o t) (g c d)", p=P),
                             kvsw[:, 0:QT, 0:256]).then_inc(out, 16)
                sp.dma_start(O["kv_slc_sample"].rearrange("b o g c d -> b (o g c d)"),
                             kvsw[0:B, QT, 0:256]).then_inc(out, 16)
                sp.dma_start(O["win_prompt"].rearrange("o (t p) g c d -> p (o t) (g c d)", p=P),
                             kvsw[:, QT - 4:QT, 256:512]).then_inc(out, 16)
                sp.dma_start(O["win_sample"][:, WIN - 1].rearrange("b g c d -> b (g c d)"),
                             kvsw[0:B, QT, 256:512]).then_inc(out, 16)
                sp.wait_ge(mready, 1)
                sp.dma_start(O["kv_mem_prompt"].rearrange("o (t p) h c d -> p (o t) (h c d)", p=P),
                             kvm[:, :, :]).then_inc(out, 16)
                sp.dma_start(O["win_sample"][:, 0:WIN - 1].rearrange("b w g c d -> b w (g c d)"),
                             I["cache_kv_win"][:, 1:WIN].rearrange("b w g c d -> b w (g c d)")).then_inc(out, 16)
                sp.wait_ge(out, 16 * 8)

            @block.scalar
            def _(act):
                for n in range(4):
                    if n >= 2:
                        act.wait_ge(summed, n - 1)
                    nc.scalar.activation(sqv(n), norms[n][0], ACT.Square).then_inc(squared, 1)
                nc.scalar.activation(gk[:, :, 0:24], gk[:, :, 0:24], ACT.Sigmoid).then_inc(gated, 1)
                act.wait_ge(qready, 1)
                act.wait_ge(summed, 4)
                nc.scalar.activation(qr[:, :, :], q[:, :, :], ACT.Copy).then_inc(qcopied, 1)

            @block.gpsimd
            def _(pool):
                pool.wait_ge(meaned, 1)
                nc.gpsimd.tensor_tensor(ss[:, :], ss[:, :], c("mhalf").to_broadcast([P, 152]),
                                        ALU.pow).then_inc(rooted, 1)
                pool.wait_ge(rooted, 1)
                pool.wait_ge(in_g, 80)
                for n, (v, h, d, t) in ((2, norms[2]), (3, norms[3])):
                    r = ss[:, at[n]:at[n + 1]].rearrange("p (t h) -> p t h", h=h)
                    g = gmq if n == 2 else gmk
                    for tt in range(t):
                        mchain.link(pool, nc.gpsimd.tensor_tensor(v[:, tt], v[:, tt], bc(r[:, tt], 2, d), ALU.mult))
                        mchain.link(pool, nc.gpsimd.tensor_tensor(v[:, tt], v[:, tt], bc(g[:, :], 1, h), ALU.mult))
                nc.gpsimd.memset(ss[:, 151:152], 0.0).then_inc(mready, 1)

            @block.vector
            def _(dve):
                for n, (v, h, d, t) in enumerate(norms):
                    dve.wait_ge(squared, n + 1)
                    nc.vector.tensor_reduce(ss[:, at[n]:at[n + 1]].rearrange("p (t h) -> p t h", h=h),
                                            sqv(n), AX.X, ALU.add).then_inc(summed, 1)
                dve.wait_ge(summed, 4)
                chain.link(dve, nc.vector.tensor_scalar(ss[:, 0:108], ss[:, 0:108], 1.0 / HD, EPS, ALU.mult, ALU.add))
                nc.vector.tensor_scalar(ss[:, 108:152], ss[:, 108:152], 1.0 / XD, EPS, ALU.mult,
                                        ALU.add).then_inc(meaned, 1)
                dve.wait_ge(rooted, 1)
                dve.wait_ge(in_g, 80)
                for n in range(2):
                    v, h, d, t = norms[n]
                    r = ss[:, at[n]:at[n + 1]].rearrange("p (t h) -> p t h", h=h)
                    chain.link(dve, nc.vector.tensor_tensor(v, v, bc(r, 3, d), ALU.mult))
                gb = lambda g, n: bc(bc(g[:, :], 1, n), 1, TT)
                nc.vector.tensor_tensor(q4, q4, gb(gq, H), ALU.mult).then_inc(qready, 1)
                kr = [kv5[:, :, 2 * r:2 * r + 2, 0, :] for r in range(2)]
                for r, g in enumerate((gs, gw)):
                    chain.link(dve, nc.vector.tensor_tensor(kr[r], kr[r], gb(g, G), ALU.mult))
                cos = c("cos").rearrange("p (t d) -> p t d", d=HALF)
                sin = c("sin").rearrange("p (t d) -> p t d", d=HALF)

                def rotate(v, n):
                    x1, x2_ = v[:, :, :, 0:HALF], v[:, :, :, HALF:2 * HALF]
                    cb, sb_ = bc(cos, 2, n), bc(sin, 2, n)
                    a, b = t1[:, :, 0:n, :], t2[:, :, 0:n, :]
                    nc.vector.tensor_tensor(a, x2_, sb_, ALU.mult)
                    chain.link(dve, nc.vector.tensor_tensor(b, x1, sb_, ALU.mult))
                    nc.vector.tensor_tensor(x1, x1, cb, ALU.mult)
                    chain.link(dve, nc.vector.tensor_tensor(x2_, x2_, cb, ALU.mult))
                    nc.vector.tensor_tensor(x1, x1, a, ALU.subtract)
                    ins = nc.vector.tensor_tensor(x2_, x2_, b, ALU.add)
                    chain.link(dve, ins)

                kk = kv5[:, :, :, 0, :]
                rotate(kk, 4)
                nc.vector.memset(ss[:, 0:1], 0.0).then_inc(kready, 1)
                dve.wait_ge(qcopied, 1)
                rotate(qr4, H)


def stage_turn(M, A):
    nc, I, O, ps, c = (M[k] for k in ("nc", "I", "O", "ps", "c"))
    gk, kvsw = (A[k] for k in ("gk", "kvsw"))
    kT, kc2, vc2, bias, w2, gcmp = (A[k] for k in ("kT", "kc2", "vc2", "bias", "w2", "gcmp"))
    NW = G * NC
    with Stage(nc, "turn") as st:
        xc = st.sb("xc", [P, 2, G, S // 2])
        w1 = st.sb("w1", [P, 2, 16, CH])
        pe_ = st.sb("pe", [P, 2, 16])
        b1 = st.sb("b1", [P, 2])
        h = st.sb("h", [P, 2, G, NC])
        sq = st.sb("sq", [NC, G, HD])
        ko = st.sb("ko", [NC, G, HD])
        kss = st.sb("kss", [NC, G])
        sem = st.sem
        in_w, turned, kept, biased, bkept, hid, hready, activated, outp, kmean, kroot, knorm, kturn, kdone = (
            sem(n) for n in ("in_w", "turned", "kept", "biased", "bkept", "hid", "hready", "activated", "outp",
                             "kmean", "kroot", "knorm", "kturn", "kdone"))
        chain = Chain(sem("step"))
        items = []
        for r in range(4):
            for half in range(2):
                items.append(("k", r, half))
        for g in range(G):
            for half in range(2):
                items.append(("x", g, half))
        with st.block() as block:
            @block.sync
            def _(sp):
                for cc in range(2):
                    sp.dma_start(w1[:, cc, :, :],
                                 I["cmp_w1"][cc].rearrange("(r q) h -> q r h", q=P)).then_inc(in_w, 16)
                rows = I["cmp_pe"].rearrange("(r p) c d -> p d c r", p=2)
                for par in range(2):
                    for cc in range(2):
                        sp.dma_start(pe_[par * HD:(par + 1) * HD, cc, :], rows[par, :, cc, :],
                                     allow_slow_non_contiguous=True).then_inc(in_w, 16)
                sp.dma_start(b1[:, :], I["cmp_b1"].rearrange("c h -> h c"),
                             allow_slow_non_contiguous=True).then_inc(in_w, 16)
                sp.dma_start(w2[:, :, :], I["cmp_w2"].rearrange("c h d -> h c d")).then_inc(in_w, 16)
                sp.dma_start(gcmp[:, :], I["k_norm_cmp"].partition_broadcast(P)).then_inc(in_w, 16)

            @block.tensor
            def _(pe):
                for n, (kind, r, half) in enumerate(items):
                    if n >= 4:
                        pe.wait_ge(kept, n - 3)
                    for a in range(4):
                        t = 4 * half + a
                        if kind == "k":
                            src, m = kvsw[:, t, r * 128:r * 128 + HD], HD
                        else:
                            src, m = gk[:, t, 24 + r * 128:24 + (r + 1) * 128], P
                        ins = nc.tensor.transpose(ps[0:m, n % 4, a * P:(a + 1) * P], src, c("ident"))
                    ins.then_inc(turned, 1)
                pe.wait_ge(in_w, 144)
                for cc in range(2):
                    for r in range(16):
                        ins = nc.tensor.matmul(ps[:, 4 + cc, 0:1], w1[:, cc, r, :], pe_[:, cc, r:r + 1],
                                               start=(r == 0), stop=(r == 15))
                ins.then_inc(biased, 1)
                pe.wait_ge(kept, len(items))
                for cc in range(2):
                    for r in range(16):
                        rhs = xc[:, cc, :, :].rearrange("p g (n s) -> p g n s", s=8)[
                            :, :, r // 8:r // 8 + NC, r % 8]
                        ins = nc.tensor.matmul(ps[:, 6 + cc, 0:NW], w1[:, cc, r, :], rhs,
                                               start=(r == 0), stop=(r == 15))
                ins.then_inc(hid, 1)
                pe.wait_ge(hready, 1)
                pe.wait_ge(activated, 2)
                for cc in range(2):
                    for g in range(G):
                        ins = nc.tensor.matmul(ps[0:NC, 0, (2 * cc + g) * HD:(2 * cc + g + 1) * HD],
                                               h[:, cc, g, :], w2[:, cc, :], start=True, stop=True)
                ins.then_inc(outp, 1)
                pe.wait_ge(knorm, 1)
                for g in range(G):
                    ins = nc.tensor.transpose(ps[0:HD, 1, g * 64:g * 64 + NC], ko[:, g, :],
                                              c("ident")[0:NC, 0:NC])
                ins.then_inc(kturn, 1)

            @block.scalar
            def _(act):
                for n, (kind, r, half) in enumerate(items):
                    act.wait_ge(turned, n + 1)
                    if kind == "k":
                        br, g = r // 2, r % 2
                        ins = nc.scalar.activation(kT[g * HD:(g + 1) * HD, br, half * 512:(half + 1) * 512],
                                                   ps[0:HD, n % 4, :], ACT.Copy)
                    else:
                        for cc in range(2):
                            for par in range(2):
                                ins = nc.scalar.activation(
                                    xc[par * HD:(par + 1) * HD, cc, r, half * 256:(half + 1) * 256],
                                    ps[cc * HD:(cc + 1) * HD, n % 4, :].rearrange("p (t e) -> p t e", e=2)[:, :, par],
                                    ACT.Copy)
                    ins.then_inc(kept, 1)
                act.wait_ge(bkept, 2)
                act.wait_ge(hid, 1)
                for cc in range(2):
                    nc.scalar.activation(h[:, cc, :, :].rearrange("p g n -> p (g n)"), ps[:, 6 + cc, 0:NW],
                                         ACT.Gelu_apprx_tanh, bias=bias[:, cc:cc + 1]).then_inc(activated, 1)

            @block.gpsimd
            def _(pool):
                pool.wait_ge(kmean, 1)
                nc.gpsimd.tensor_tensor(kss[:, :], kss[:, :], c("mhalf")[0:NC, :].to_broadcast([NC, G]),
                                        ALU.pow).then_inc(kroot, 1)

            @block.vector
            def _(dve):
                dve.wait_ge(in_w, 144)
                dve.wait_ge(biased, 1)
                for cc in range(2):
                    nc.vector.tensor_tensor(bias[:, cc:cc + 1], ps[:, 4 + cc, 0:1], b1[:, cc:cc + 1],
                                            ALU.add).then_inc(bkept, 1)
                dve.wait_ge(activated, 2)
                nc.vector.memset(vc2[:, :, :], 0.0).then_inc(hready, 1)
                dve.wait_ge(hready, 1)
                dve.wait_ge(outp, 1)
                o4 = ps[0:NC, 0, 0:4 * HD].rearrange("p (c g d) -> p c g d", c=2, g=2)
                for k in range(2):
                    nc.vector.tensor_copy(vc2[k * 64:k * 64 + NC, :, k * HD:(k + 1) * HD], o4[:, 1])
                chain.link(dve, nc.vector.tensor_copy(ko[:, :, :], o4[:, 0]))
                t = sq[:, :, :]
                chain.link(dve, nc.vector.tensor_tensor(t, ko[:, :, :], ko[:, :, :], ALU.mult))
                chain.link(dve, nc.vector.tensor_reduce(kss[:, :], t, AX.X, ALU.add))
                nc.vector.tensor_scalar(kss[:, :], kss[:, :], 1.0 / HD, EPS, ALU.mult, ALU.add).then_inc(kmean, 1)
                dve.wait_ge(kroot, 1)
                chain.link(dve, nc.vector.tensor_tensor(ko[:, :, :], ko[:, :, :], bc(kss[:, :], 2, HD), ALU.mult))
                nc.vector.tensor_tensor(ko[:, :, :], ko[:, :, :], bc(gcmp[0:NC, :], 1, G), ALU.mult).then_inc(knorm, 1)
                chain.link(dve, nc.vector.memset(kc2[:, :, :], 0.0))
                dve.wait_ge(kturn, 1)
                for k in range(2):
                    nc.vector.tensor_copy(kc2[k * HD:(k + 1) * HD, :, k * 64:k * 64 + NC],
                                          ps[0:HD, 1, 0:G * 64].rearrange("p (g n) -> p g n", g=G)[:, :, 0:NC]
                                          ).then_inc(kdone, 1)


def stage_cmp_prompt(M, A):
    nc, ps, c = (M[k] for k in ("nc", "ps", "c"))
    q, gk, kc2, vc2, acc = (A[k] for k in ("q", "gk", "kc2", "vc2", "acc"))
    HP = H // 2
    with Stage(nc, "cmp") as st:
        qT = st.sb("qT", [P, 2, HP, P])
        p_ = st.sb("p", [P, 2, H, 64])
        pT = st.sb("pT", [P, 2, HP, P])
        mx = st.sb("mx", [P, H])
        sm = st.sb("sm", [P, 2, H])
        sem = st.sem
        turned, qkept, scored, shifted, exped, masked, pturned, pkept, attended, used = (
            sem(n) for n in ("turned", "qkept", "scored", "shifted", "exped", "masked", "pturned", "pkept",
                             "attended", "used"))
        chain = Chain(sem("step"))
        neg_ = st.sb("neg", [P, QT * 64])
        neg = neg_[:, :].rearrange("p (t n) -> p t n", t=QT)
        one = c("cmp01").rearrange("p (t n) -> p t n", t=QT)
        with st.block() as block:
            @block.tensor
            def _(pe):
                def turn(i):
                    if i >= 2:
                        pe.wait_ge(qkept, i - 1)
                    for pr in range(HP):
                        ins = nc.tensor.transpose(ps[:, i % 2, pr * P:(pr + 1) * P],
                                                  q[:, i, pr * P:(pr + 1) * P], c("ident"))
                    ins.then_inc(turned, 1)

                def scores(i):
                    pe.wait_ge(qkept, i + 1)
                    if i >= 2:
                        pe.wait_ge(shifted, i - 1)
                    for pr in range(HP):
                        ins = nc.tensor.matmul(ps[:, 2 + i % 2, pr * P:(pr + 1) * P], qT[:, i % 2, pr, :],
                                               kc2[:, 2 * pr // HPG, :], start=True, stop=True)
                    ins.then_inc(scored, 1)

                def turn_p(i):
                    pe.wait_ge(masked, i + 1)
                    if i >= 2:
                        pe.wait_ge(pkept, i - 1)
                    for pr in range(HP):
                        ins = nc.tensor.transpose(ps[:, 4 + i % 2, pr * P:(pr + 1) * P],
                                                  p_[:, i % 2, 2 * pr:2 * pr + 2, :].rearrange("p h n -> p (h n)"),
                                                  c("ident"))
                    ins.then_inc(pturned, 1)

                def attend(i):
                    pe.wait_ge(pkept, i + 1)
                    if i >= 2:
                        pe.wait_ge(used, i - 1)
                    for pr in range(HP):
                        ins = nc.tensor.matmul(ps[:, 6 + i % 2, pr * P:(pr + 1) * P], pT[:, i % 2, pr, :],
                                               vc2[:, 2 * pr // HPG, :], start=True, stop=True)
                    ins.then_inc(attended, 1)

                turn(0)
                scores(0)
                for i in range(QT):
                    if i + 1 < QT:
                        turn(i + 1)
                        scores(i + 1)
                    turn_p(i)
                    if i >= 1:
                        attend(i - 1)
                attend(QT - 1)

            @block.scalar
            def _(act):
                def keep_q(i):
                    act.wait_ge(turned, i + 1)
                    if i >= 2:
                        act.wait_ge(scored, i - 1)
                    nc.scalar.activation(qT[:, i % 2, :, :].rearrange("p h q -> p (h q)"), ps[:, i % 2, :],
                                         ACT.Copy).then_inc(qkept, 1)

                def keep_p(i):
                    act.wait_ge(pturned, i + 1)
                    if i >= 2:
                        act.wait_ge(attended, i - 1)
                    nc.scalar.activation(pT[:, i % 2, :, :].rearrange("p h q -> p (h q)"), ps[:, 4 + i % 2, :],
                                         ACT.Copy).then_inc(pkept, 1)

                keep_q(0)
                for i in range(QT):
                    if i + 1 < QT:
                        keep_q(i + 1)
                    act.wait_ge(shifted, i + 1)
                    nc.scalar.activation(p_[:, i % 2, :, :], p_[:, i % 2, :, :], ACT.Exp,
                                         scale=HD ** -0.5).then_inc(exped, 1)
                    if i >= 1:
                        keep_p(i - 1)
                keep_p(QT - 1)

            @block.vector
            def _(dve):
                def shift(i):
                    dve.wait_ge(scored, i + 1)
                    if i >= 2:
                        dve.wait_ge(pturned, i - 1)
                    p = p_[:, i % 2, :, :]
                    s = ps[:, 2 + i % 2, :].rearrange("p (h n) -> p h n", h=H)
                    chain.link(dve, nc.vector.tensor_tensor(p, s, bc(neg[:, i, :], 1, H), ALU.add))
                    chain.link(dve, nc.vector.tensor_reduce(mx[:, :], p, AX.X, ALU.max))
                    nc.vector.tensor_tensor(p, p, bc(mx[:, :], 2, 64), ALU.subtract).then_inc(shifted, 1)
                    dve.wait_ge(shifted, i + 1)

                def norm(i):
                    p, f = p_[:, i % 2, :, :], sm[:, i % 2, :]
                    dve.wait_ge(exped, i + 1)
                    nc.vector.tensor_tensor(p, p, bc(one[:, i, :], 1, H), ALU.mult).then_inc(masked, 1)
                    dve.wait_ge(masked, i + 1)
                    chain.link(dve, nc.vector.tensor_reduce(f, p, AX.X, ALU.add))
                    chain.link(dve, nc.vector.tensor_scalar(f, f, float(np.finfo(np.float32).tiny), None, ALU.max))
                    chain.link(dve, nc.vector.reciprocal(f, f))
                    chain.link(dve, nc.vector.tensor_tensor(f, f, gk[:, i, 0:H], ALU.mult))

                def use(i):
                    dve.wait_ge(attended, i + 1)
                    nc.vector.tensor_tensor(
                        acc[:, :, i * P:(i + 1) * P].rearrange("p a (b d) -> p a b d", b=2),
                        ps[:, 6 + i % 2, :].rearrange("p (a b d) -> p a b d", a=4, b=2),
                        bc(sm[:, i % 2, :].rearrange("p (a b) -> p a b", b=2), 3, HD), ALU.mult).then_inc(used, 1)

                chain.link(dve, nc.vector.tensor_scalar(neg_[:, :], c("cmp01"), BIG, -BIG, ALU.mult, ALU.add))
                shift(0)
                for i in range(QT):
                    if i + 1 < QT:
                        shift(i + 1)
                    if i >= 2:
                        dve.wait_ge(used, i - 1)
                    norm(i)
                    if i >= 1:
                        use(i - 1)
                use(QT - 1)


def stage_slc_win(M, A):
    nc, ps, c, brT = (M[k] for k in ("nc", "ps", "c", "brT"))
    qr, gk, kvsw, kT, acc = (A[k] for k in ("qr", "gk", "kvsw", "kT", "acc"))
    units = [(i, h, br) for i in range(QT) for h in range(H) for br in range(2)]

    def keys(u):
        i, _, br = units[u]
        return (0 if br == 0 else max(0, i - 4)), i + 1

    items, first_item = [], []
    for u in range(len(units)):
        first_item.append(len(items))
        lo, hi = keys(u)
        n = hi - lo
        items += [(u, a, min(4, n - a)) for a in range(0, n, 4)]
    first_item.append(len(items))
    NU = len(units)
    with Stage(nc, "att") as st:
        qT = st.sb("qT", [P, 2, H, P])
        p_ = st.sb("p", [P, 2, S])
        pT = st.sb("pT", [P, 2, S])
        mx = st.sb("mx", [P, 4])
        sm = st.sb("sm", [P, 4])
        f = st.sb("f", [P, 4])
        sem = st.sem
        zeroed, turned, qkept, scored, maxed, exped, pturned, pkept_a, pkept_v, attended, used, oturned, okept = (
            sem(n) for n in ("zeroed", "turned", "qkept", "scored", "maxed", "exped", "pturned", "pkept_a", "pkept_v",
                             "attended", "used", "oturned", "okept"))
        chain = Chain(sem("step"))

        def wait_kept(eng, m):
            if (m + 1) // 2:
                eng.wait_ge(pkept_a, (m + 1) // 2)
            if m // 2:
                eng.wait_ge(pkept_v, m // 2)

        def keep(eng, m):
            u, a, n = items[m]
            eng.wait_ge(pturned, m + 1)
            if u >= 2:
                eng.wait_ge(attended, u - 1)
            dst, src = pT[:, u % 2, a * P:(a + n) * P], ps[:, 4 + m % 2, 0:n * P]
            if m % 2 == 0:
                nc.scalar.activation(dst, src, ACT.Copy).then_inc(pkept_a, 1)
            else:
                nc.vector.tensor_copy(dst, src).then_inc(pkept_v, 1)

        with st.block() as block:
            @block.tensor
            def _(pe):
                def scores(u):
                    i, h, br = units[u]
                    if h == 0 and br == 0:
                        if u >= 2:
                            pe.wait_ge(used, u - 2)
                        for hh in range(H):
                            j = 2 * i + hh // 4
                            if hh % 4 == 0 and j >= 1:
                                pe.wait_ge(qkept, j)
                            ins = nc.tensor.transpose(ps[0:HD, 7, (hh % 4) * P:(hh % 4 + 1) * P],
                                                      qr[:, i, hh * HD:(hh + 1) * HD], c("ident"))
                            if hh % 4 == 3:
                                ins.then_inc(turned, 1)
                        pe.wait_ge(qkept, 2 * i + 2)
                    if u >= 2:
                        pe.wait_ge(exped, u - 1)
                    lo, hi = keys(u)
                    for a in range(0, hi - lo, 4):
                        n = min(4, hi - lo - a)
                        ins = nc.tensor.matmul(ps[:, 2 * (u % 2) + a // 4, 0:n * P], qT[:, i % 2, h, :],
                                               kT[:, br, (lo + a) * P:(lo + a + n) * P],
                                               start=True, stop=True)
                    ins.then_inc(scored, 1)

                def products(u):
                    i, h, br = units[u]
                    g = h // HPG
                    pe.wait_ge(exped, u + 1)
                    for m in range(first_item[u], first_item[u + 1]):
                        if m >= 2:
                            wait_kept(pe, m - 1)
                        _, a, n = items[m]
                        for b in range(n):
                            ins = nc.tensor.transpose(ps[:, 4 + m % 2, b * P:(b + 1) * P],
                                                      p_[:, u % 2, (a + b) * P:(a + b + 1) * P], c("ident"))
                        ins.then_inc(pturned, 1)

                def attend(u):
                    i, h, br = units[u]
                    g = h // HPG
                    wait_kept(pe, first_item[u + 1])
                    if u >= 2:
                        pe.wait_ge(used, u - 1)
                    if u % 2 and u > 2 * H:
                        pe.wait_ge(okept, (u - 1) // (2 * H))
                    lo, hi = keys(u)
                    for b in range(hi - lo):
                        kv = kvsw[:, lo + b, br * 256 + g * 128:br * 256 + (g + 1) * 128]
                        ins = nc.tensor.matmul(ps[:, 6 + u % 2, 0:P], pT[:, u % 2, b * P:(b + 1) * P],
                                               kv, start=(b == 0), stop=(b == hi - lo - 1))
                    ins.then_inc(attended, 1)

                def turn_out(i):
                    pe.wait_ge(used, (i + 1) * 2 * H)
                    pe.wait_ge(qkept, min(2 * i + 4, 2 * QT))
                    if i:
                        pe.wait_ge(okept, i)
                    for a in range(4):
                        ins = nc.tensor.transpose(ps[:, 7, a * P:(a + 1) * P], acc[:, a, i * P:(i + 1) * P],
                                                  c("ident"))
                    ins.then_inc(oturned, 1)

                scores(0)
                for u in range(NU):
                    if u + 1 < NU:
                        if units[u + 1][1:] == (0, 0) and u > 2 * H:
                            pe.wait_ge(okept, units[u][0])
                        scores(u + 1)
                    products(u)
                    if u >= 1:
                        attend(u - 1)
                        if u % (2 * H) == 1 and u > 2 * H:
                            turn_out(u // (2 * H) - 1)
                attend(NU - 1)
                turn_out(QT - 1)

            @block.scalar
            def _(act):
                def out(act, i):
                    act.wait_ge(oturned, i + 1)
                    nc.scalar.activation(brT[:, 0:4, i * P:(i + 1) * P],
                                         ps[:, 7, :].rearrange("p (a q) -> p a q", a=4), ACT.Copy).then_inc(okept, 1)

                def keep_q(i):
                    for j in range(2):
                        act.wait_ge(turned, 2 * i + j + 1)
                        if i < 2:
                            act.wait_ge(zeroed, 1)
                        nc.scalar.activation(qT[j * HD:(j + 1) * HD, i % 2, HPG * j:HPG * (j + 1), :
                                                ].rearrange("p h q -> p (h q)"),
                                             ps[0:HD, 7, :], ACT.Copy).then_inc(qkept, 1)

                keep_q(0)
                for u in range(NU):
                    i, h, br = units[u]
                    act.wait_ge(maxed, u + 1)
                    if u >= 2:
                        act.wait_ge(pturned, first_item[u - 1])
                    lo, hi = keys(u)
                    n = (hi - lo) * P
                    if u >= 4:
                        act.wait_ge(used, u - 3)
                    src = ps[:, 2 * (u % 2):2 * (u % 2) + 2, :].rearrange("p b n -> p (b n)")[:, 0:n]
                    nc.scalar.activation(p_[:, u % 2, 0:n], src, ACT.Exp, scale=HD ** -0.5,
                                         bias=mx[:, u % 4:u % 4 + 1], accum_out=sm[:, u % 4:u % 4 + 1]
                                         ).then_inc(exped, 1)
                    if u + 1 < NU and units[u + 1][1:] == (0, 0):
                        keep_q(i + 1)
                    for m in range(first_item[u], first_item[u + 1]):
                        if m % 2 == 0:
                            keep(act, m)
                    if u % (2 * H) == 2 and u > 2 * H:
                        out(act, u // (2 * H) - 1)
                out(act, QT - 1)

            @block.vector
            def _(dve):
                def maximum(u):
                    i, h, br = units[u]
                    lo, hi = keys(u)
                    n = (hi - lo) * P
                    s = ps[:, 2 * (u % 2):2 * (u % 2) + 2, :].rearrange("p b n -> p (b n)")
                    dve.wait_ge(scored, u + 1)
                    if u >= 4:
                        dve.wait_ge(exped, u - 3)
                    if br == 1 and i >= 4:
                        chain.link(dve, nc.vector.tensor_tensor(s[:, 0:P], s[:, 0:P], c("band"), ALU.add))
                    chain.link(dve, nc.vector.tensor_tensor(s[:, n - P:n], s[:, n - P:n], c("causal"), ALU.add))
                    chain.link(dve, nc.vector.tensor_reduce(mx[:, u % 4:u % 4 + 1], s[:, 0:n], AX.X, ALU.max))
                    nc.vector.tensor_scalar(mx[:, u % 4:u % 4 + 1], mx[:, u % 4:u % 4 + 1], -(HD ** -0.5), None,
                                            ALU.mult).then_inc(maxed, 1)

                def use(u):
                    i, h, br = units[u]
                    k = u % 4
                    chain.link(dve, nc.vector.reciprocal(f[:, k:k + 1], sm[:, k:k + 1]))
                    gate = gk[:, i, (1 + br) * H + h:(1 + br) * H + h + 1]
                    chain.link(dve, nc.vector.tensor_tensor(f[:, k:k + 1], f[:, k:k + 1], gate, ALU.mult))
                    dve.wait_ge(attended, u + 1)
                    o = acc[:, h // 2, i * P + (h % 2) * HD:i * P + (h % 2 + 1) * HD]
                    if u >= 1:
                        dve.wait_ge(used, u)
                    nc.vector.scalar_tensor_tensor(o, ps[:, 6 + u % 2, HD:P], f[:, k:k + 1], o,
                                                   ALU.mult, ALU.add).then_inc(used, 1)

                nc.vector.memset(qT[:, :, :, :], 0.0).then_inc(zeroed, 1)
                maximum(0)
                for u in range(NU):
                    if u + 1 < NU:
                        maximum(u + 1)
                    for m in range(first_item[u], first_item[u + 1]):
                        if m % 2 == 1:
                            keep(dve, m)
                    if u >= 1:
                        use(u - 1)
                use(NU - 1)


def stage_mem_prompt(M, A):
    nc, ps, c, brT = (M[k] for k in ("nc", "ps", "c", "brT"))
    mq, kvm, kmT = (A[k] for k in ("mq", "kvm", "kmT"))
    SC = XD ** -0.5
    NK = XT // P
    with Stage(nc, "mem") as st:
        qT = st.sb("qT", [P, XH, P])
        p_ = st.sb("p", [P, XH, XT])
        pT = st.sb("pT", [P, XH, NK, P])
        mx = st.sb("mx", [P, XH])
        sm = st.sb("sm", [P, XH])
        o = st.sb("o", [P, XH, XD])
        sem = st.sem
        turned, qkept, scored, maxed, exped, pturned, pkept, attended, scaled, oturned, okept = (
            sem(n) for n in ("turned", "qkept", "scored", "maxed", "exped", "pturned", "pkept", "attended",
                             "scaled", "oturned", "okept"))
        chain = Chain(sem("step"))
        kturned, kkept, mqs = (sem(n) for n in ("kturned", "kkept", "mqs"))
        with st.block() as block:
            @block.sync
            def _(sp):
                sp.dma_start(A["mqS"], mq[0:B, QT, :]).then_inc(mqs, 16)
                sp.wait_ge(mqs, 16)

            @block.tensor
            def _(pe):
                for t in range(NK):
                    for h in range(XH):
                        ins = nc.tensor.transpose(ps[:, t, h * P:(h + 1) * P], kvm[:, t, h * 256:h * 256 + XD],
                                                  c("ident"))
                    ins.then_inc(kturned, 1)
                pe.wait_ge(kkept, NK)

                def turn_out(i):
                    pe.wait_ge(scaled, i + 1)
                    if i:
                        pe.wait_ge(okept, i)
                    for h in range(XH):
                        ins = nc.tensor.transpose(ps[:, 6, h * P:(h + 1) * P], o[:, h, :], c("ident"))
                    ins.then_inc(oturned, 1)

                for i in range(QT):
                    if i:
                        pe.wait_ge(qkept, i)
                    for h in range(XH):
                        ins = nc.tensor.transpose(ps[:, 7, h * P:(h + 1) * P], mq[:, i, h * XD:(h + 1) * XD],
                                                  c("ident"))
                    ins.then_inc(turned, 1)
                    pe.wait_ge(qkept, i + 1)
                    if i:
                        pe.wait_ge(exped, XH * i)
                    for h in range(XH):
                        ins = nc.tensor.matmul(ps[:, h // 2, (h % 2) * XT:(h % 2 + 1) * XT], qT[:, h, :],
                                               kmT[:, h, :], start=True, stop=True)
                    ins.then_inc(scored, 1)
                    if i:
                        turn_out(i - 1)
                    pe.wait_ge(exped, XH * (i + 1))
                    if i:
                        pe.wait_ge(pkept, 2 * i)
                    for h in range(XH):
                        for k in range(NK):
                            ins = nc.tensor.transpose(ps[:, 2 + h // 2, ((h % 2) * NK + k) * P:((h % 2) * NK + k + 1) * P],
                                                      p_[:, h, k * P:(k + 1) * P], c("ident"))
                        if h % 2 == 1:
                            ins.then_inc(pturned, 1)
                    pe.wait_ge(pkept, 2 * i + 2)
                    if i:
                        pe.wait_ge(scaled, i)
                    for h in range(XH):
                        for k in range(NK):
                            ins = nc.tensor.matmul(ps[:, 4, h * XD:(h + 1) * XD], pT[:, h, k, :],
                                                   kvm[:, k, h * 256 + XD:(h + 1) * 256],
                                                   start=(k == 0), stop=(k == NK - 1))
                    ins.then_inc(attended, 1)
                turn_out(QT - 1)

            @block.scalar
            def _(act):
                for t in range(NK):
                    act.wait_ge(kturned, t + 1)
                    nc.scalar.activation(kmT[:, :, t * P:(t + 1) * P],
                                         ps[:, t, :].rearrange("p (h q) -> p h q", h=XH), ACT.Copy).then_inc(kkept, 1)
                for i in range(QT):
                    act.wait_ge(turned, i + 1)
                    if i:
                        act.wait_ge(scored, i)
                    nc.scalar.activation(qT[:, :, :].rearrange("p h q -> p (h q)"), ps[:, 7, :],
                                         ACT.Copy).then_inc(qkept, 1)
                    act.wait_ge(maxed, i + 1)
                    if i:
                        act.wait_ge(pturned, 2 * i)
                    for h in range(XH):
                        nc.scalar.activation(p_[:, h, :], ps[:, h // 2, (h % 2) * XT:(h % 2 + 1) * XT], ACT.Exp,
                                             scale=SC, bias=mx[:, h:h + 1],
                                             accum_out=sm[:, h:h + 1]).then_inc(exped, 1)
                    for j in range(2):
                        act.wait_ge(pturned, 2 * i + j + 1)
                        if i:
                            act.wait_ge(attended, i)
                        nc.scalar.activation(pT[:, 2 * j:2 * j + 2, :, :].rearrange("p h k q -> p (h k q)"),
                                             ps[:, 2 + j, :], ACT.Copy).then_inc(pkept, 1)

            @block.vector
            def _(dve):
                def out(i):
                    dve.wait_ge(oturned, i + 1)
                    nc.vector.tensor_copy(brT[:, 8:12, i * P:(i + 1) * P],
                                          ps[:, 6, :].rearrange("p (a q) -> p a q", a=4)).then_inc(okept, 1)

                for i in range(QT):
                    dve.wait_ge(scored, i + 1)
                    if i:
                        dve.wait_ge(exped, XH * i)
                    chain.link(dve, nc.vector.tensor_reduce(
                        mx[:, :], ps[:, 0:2, :].rearrange("p b (h n) -> p b h n", h=2), AX.X, ALU.max))
                    nc.vector.tensor_scalar(mx[:, :], mx[:, :], -SC, None, ALU.mult).then_inc(maxed, 1)
                    if i:
                        out(i - 1)
                    dve.wait_ge(exped, XH * (i + 1))
                    chain.link(dve, nc.vector.reciprocal(sm[:, :], sm[:, :]))
                    dve.wait_ge(attended, i + 1)
                    nc.vector.tensor_tensor(o[:, :, :], ps[:, 4, :].rearrange("p (h d) -> p h d", h=XH),
                                            bc(sm[:, :], 2, XD), ALU.mult).then_inc(scaled, 1)
                out(QT - 1)


def stage_keep_samples(M, A):
    nc = M["nc"]
    with Stage(nc, "keep") as st:
        moved = st.sem("moved")
        with st.block() as block:
            @block.sync
            def _(sp):
                for dst, src in (("qS", "q"), ("qrS", "qr"), ("kvS", "kvsw"), ("gS", "gk")):
                    sp.dma_start(M[dst], A[src][0:B, QT, :]).then_inc(moved, 16)
                sp.wait_ge(moved, 64)


def stage_attention(M):
    nc, x2, brT, memT = (M[k] for k in ("nc", "x2", "brT", "memT"))
    flat = x2[:, :, :].rearrange("p t d -> p (t d)")
    mflat = memT[:, :, :].rearrange("p k t -> p (k t)")
    for n, name in enumerate(("qS", "qrS", "kvS", "mqS")):
        M[name] = mflat[0:B, n * 512:(n + 1) * 512]
    with Stage(nc, "a") as st:
        A = {"mqS": M["mqS"]}
        A["q"] = st.sb("q", [P, TT, 512])
        A["kvsw"] = st.sb("kvsw", [P, TT, 512])
        A["gk"] = st.sb("gk", [P, TT, 280])
        A["qr"] = flat[:, 0:TT * 512].rearrange("p (t n) -> p t n", n=512)
        A["kT"] = flat[:, 4608:4608 + 2 * S].rearrange("p (r t) -> p r t", r=2)
        A["kvm"] = brT[:, 0:2, :].rearrange("p a t -> p (a t)")[:, 0:2048].rearrange("p (t n) -> p t n", t=2)
        A["kmT"] = brT[:, 2, 0:1024].rearrange("p (h t) -> p h t", h=XH)
        A["acc"] = brT[:, 0:4, 0:S]
        with Stage(nc, "a2") as s2:
            A["mq"] = s2.sb("mq", [P, TT, 512])
            stage_tok_proj(M, A)
            stage_prep(M, A)
            stage_mem_prompt(M, A)
        A["w2"] = st.sb("w2", [P, 2, HD])
        A["gcmp"] = st.sb("gcmp", [P, HD])
        A["bias"] = M["bias"]
        A["kc2"] = st.sb("kc2", [P, G, P])
        A["vc2"] = st.sb("vc2", [P, G, P])
        stage_turn(M, A)
        stage_cmp_prompt(M, A)
        stage_slc_win(M, A)
        stage_keep_samples(M, A)


def stage_s_prep(M, A):
    nc, I, ps, c = (M[k] for k in ("nc", "I", "ps", "c"))
    with Stage(nc, "sp") as st:
        sem = st.sem
        turned, kept, loaded = (sem(n) for n in ("turned", "kept", "loaded"))
        chain = Chain(sem("step"))
        with st.block() as block:
            @block.sync
            def _(sp):
                sp.dma_start(A["pt"][:, :], I["page_table"].rearrange("b n -> (b n)").unsqueeze(0)).then_inc(loaded, 16)
                kv = M["kvS"].rearrange("b (r c d) -> b r c d", c=2, d=HD)
                for b in range(B):
                    q = 32 * (b // 2)
                    sp.dma_start(A["vrow"][q:q + 1, b % 2, :, :], kv[b:b + 1, :, 1, :]).then_inc(loaded, 16)
                sp.wait_ge(loaded, 16 * (1 + B))

            @block.tensor
            def _(pe):
                idb = c("ident")[0:B, 0:B]
                for h in range(H):
                    nc.tensor.transpose(ps[0:HD, 0, h * B:(h + 1) * B], M["qS"][:, h * HD:(h + 1) * HD], idb)
                    nc.tensor.transpose(ps[0:HD, 0, 64 + h * B:64 + (h + 1) * B], M["qrS"][:, h * HD:(h + 1) * HD], idb)
                for r in range(4):
                    nc.tensor.transpose(ps[0:HD, 0, 128 + r * B:128 + (r + 1) * B],
                                        M["kvS"][:, r * 128:r * 128 + HD], idb)
                for h in range(XH):
                    nc.tensor.transpose(ps[:, 1, h * B:(h + 1) * B], M["mqS"][:, h * XD:(h + 1) * XD], idb)
                for r in range(3):
                    ins = nc.tensor.transpose(ps[0:H, 2, r * B:(r + 1) * B], M["gS"][:, r * H:(r + 1) * H], idb)
                ins.then_inc(turned, 1)

            @block.vector
            def _(dve):
                chain.link(dve, nc.vector.memset(A["qz"][:, :, :], 0.0))
                chain.link(dve, nc.vector.memset(A["qmz"][:, :, :, :], 0.0))
                dve.wait_ge(turned, 1)
                hb = lambda ap: ap.rearrange("p (h b) -> p h b", b=B)
                nc.vector.tensor_copy(A["qcS"][:, :, :].rearrange("p b h -> p h b"), hb(ps[0:HD, 0, 0:64]))
                for g in range(G):
                    nc.vector.tensor_copy(A["qz"][g * HD:(g + 1) * HD, :, g * HPG:(g + 1) * HPG
                                                  ].rearrange("p b h -> p h b"),
                                          hb(ps[0:HD, 0, 64 + g * 32:64 + (g + 1) * 32]))
                    nc.vector.tensor_copy(A["knT"][g * HD:(g + 1) * HD, :, :],
                                          ps[0:HD, 0, 128:160].rearrange("p (r g b) -> p r g b", r=2, g=G)[:, :, g, :])
                for h in range(XH):
                    nc.vector.tensor_copy(A["qmz"][:, :, h, h], ps[:, 1, h * B:(h + 1) * B])
                nc.vector.tensor_copy(A["gT"][:, :, :], hb(ps[0:H, 2, 0:24])).then_inc(kept, 1)
                dve.wait_ge(kept, 1)


def load_pages(eng, cache, dst, pt, b, half, done):
    with eng.Fori(0, NPG // 2) as n:
        page = eng.value_load(pt[0:1, bass.ds(n * 2 + (half + NPG * b), 1)], min_val=0, max_val=NPHYS - 1)
        eng.dma_start(dst[:, bass.ds(n * 512 + half * 256, 256)],
                      cache[bass.ds(page, 1)].rearrange("o r g c d -> r (o g c d)")).then_inc(done, 16)


def stage_s_compress(M, A):
    nc, I, ps, c = (M[k] for k in ("nc", "I", "ps", "c"))
    flat = M["x2"][:, :, :].rearrange("p t d -> p (t d)")
    pt, kcT, vc, bias = (A[k] for k in ("pt", "kcT", "vc", "bias"))
    NF = NPG * G // 4
    NW = G * NCS
    with Stage(nc, "sc") as st:
        X = st.sb("X", [P, 2, NPG * 256])
        xtb = st.sb("xt", [P, 2, G, PAST // 2])
        xt = [xtb[:, :, :, :], flat[:, 0:G * PAST].rearrange("p (c g t) -> p c g t", c=2, g=G)]
        w1 = flat[:, 4096:8192].rearrange("p (c r h) -> p c r h", c=2, r=16)
        w2 = st.sb("w2", [P, 2, HD])
        gc = st.sb("gc", [P, HD])
        h = st.sb("h", [P, 2, G, NCS])
        ko = flat[0:NCS, 8192:9216].rearrange("p (n d) -> p n d", d=HD)
        kss = st.sb("kss", [NCS, B * G])
        sq = flat[0:NCS, 2048:2048 + B * G * HD].rearrange("p (n d) -> p n d", d=HD)
        sem = st.sem
        in_x = [sem(f"in_x{q}") for q in range(2)]
        in_xp = [sem(f"in_xp{q}") for q in range(2)]
        (in_w, turned, kept_a, kept_v, hid, activated, outp, okept, kmean, kroot, knorm, kturn, kdone) = (
            sem(n) for n in ("in_w", "turned", "kept_a", "kept_v", "hid", "activated", "outp", "okept",
                             "kmean", "kroot", "knorm", "kturn", "kdone"))
        chain = Chain(sem("step"))

        def keep(eng, f):
            b, k = f // NF, f % NF
            eng.wait_ge(turned, f + 1)
            if b >= 2:
                eng.wait_ge(hid, b - 1)
            for cc in range(2):
                for par in range(2):
                    dst = xt[b % 2][par * HD:(par + 1) * HD, cc, :, k * 128:(k + 1) * 128]
                    src = ps[cc * HD:(cc + 1) * HD, f % 4, :].rearrange("p (g t e) -> p g t e", g=G, e=2)[:, :, :, par]
                    if f % 2 == 0:
                        ins = nc.scalar.activation(dst, src, ACT.Copy)
                    else:
                        ins = nc.vector.tensor_copy(dst, src)
            ins.then_inc(kept_a if f % 2 == 0 else kept_v, 1)

        with st.block() as block:
            @block.sync
            def _(sp):
                for b in range(B):
                    if b >= 2:
                        sp.wait_ge(turned, NF * (b - 1))
                    load_pages(sp, I["cache_kv_cmp"], X[:, b % 2, :], pt, b, 0, in_x[b % 2])
                    if b == 0:
                        for cc in range(2):
                            sp.dma_start(w1[:, cc, :, :],
                                         I["cmp_w1"][cc].rearrange("(r q) h -> q r h", q=P)).then_inc(in_w, 16)
                        sp.dma_start(w2[:, :, :], I["cmp_w2"].rearrange("c h d -> h c d")).then_inc(in_w, 16)
                        sp.dma_start(gc[:, :], I["k_norm_cmp"].partition_broadcast(P)).then_inc(in_w, 16)

            @block.tensor
            def _(pe):
                def turn(b):
                    pe.wait_ge(in_x[b % 2], 8 * NPG * (b // 2 + 1))
                    pe.wait_ge(in_xp[b % 2], 8 * NPG * (b // 2 + 1))
                    for k in range(NF):
                        f = b * NF + k
                        if f >= 4:
                            pe.wait_ge(kept_a if f % 2 == 0 else kept_v, f // 2 - 1)
                        for g in range(G):
                            for j in range(2):
                                ins = nc.tensor.transpose(ps[:, f % 4, (2 * g + j) * P:(2 * g + j + 1) * P],
                                                          X[:, b % 2, (2 * k + j) * 256 + g * 128:(2 * k + j) * 256 + (g + 1) * 128],
                                                          c("ident"))
                        ins.then_inc(turned, 1)

                def hidden(b):
                    pe.wait_ge(kept_a, (b + 1) * NF // 2)
                    pe.wait_ge(kept_v, (b + 1) * NF // 2)
                    if b >= 1:
                        pe.wait_ge(activated, 2 * b)
                    for cc in range(2):
                        for r in range(16):
                            rhs = xt[b % 2][:, cc, :, :].rearrange("p g (n s) -> p g n s", s=8)[
                                :, :, r // 8:r // 8 + NCS, r % 8]
                            ins = nc.tensor.matmul(ps[:, 4 + cc, 0:NW], w1[:, cc, r, :], rhs,
                                                   start=(r == 0), stop=(r == 15))
                    ins.then_inc(hid, 1)

                def project(b):
                    pe.wait_ge(activated, 2 * b + 2)
                    if b >= 2:
                        pe.wait_ge(okept, b - 1)
                    for cc in range(2):
                        for g in range(G):
                            ins = nc.tensor.matmul(ps[0:NCS, 6 + b % 2, (2 * cc + g) * HD:(2 * cc + g + 1) * HD],
                                                   h[:, cc, g, :], w2[:, cc, :], start=True, stop=True)
                    ins.then_inc(outp, 1)

                turn(0)
                pe.wait_ge(in_w, 64)
                for b in range(B):
                    if b + 1 < B:
                        turn(b + 1)
                    if b >= 1:
                        project(b - 1)
                    hidden(b)
                project(B - 1)
                pe.wait_ge(knorm, 1)
                for n in range(B * G):
                    if n % 4 == 0 and n >= 16:
                        pe.wait_ge(kdone, n // 4 - 3)
                    ins = nc.tensor.transpose(ps[0:HD, n // 4, (n % 4) * P:(n % 4) * P + NCS], ko[:, n, :],
                                              c("ident")[0:NCS, 0:NCS])
                    if n % 4 == 3:
                        ins.then_inc(kturn, 1)

            @block.scalar
            def _(act):
                def gelu(b):
                    act.wait_ge(hid, b + 1)
                    if b >= 1:
                        act.wait_ge(outp, b)
                    for cc in range(2):
                        nc.scalar.activation(h[:, cc, :, :].rearrange("p g n -> p (g n)"), ps[:, 4 + cc, 0:NW],
                                             ACT.Gelu_apprx_tanh, bias=bias[:, cc:cc + 1]).then_inc(activated, 1)

                for b in range(B):
                    for k in range(0, NF, 2):
                        keep(act, b * NF + k)
                    if b >= 1:
                        gelu(b - 1)
                gelu(B - 1)

            @block.gpsimd
            def _(pool):
                for b in range(B):
                    if b >= 2:
                        pool.wait_ge(turned, NF * (b - 1))
                    load_pages(pool, I["cache_kv_cmp"], X[:, b % 2, :], pt, b, 1, in_xp[b % 2])
                pool.wait_ge(kmean, 1)
                nc.gpsimd.tensor_tensor(kss[:, :], kss[:, :], c("mhalf")[0:NCS, :].to_broadcast([NCS, B * G]),
                                        ALU.pow).then_inc(kroot, 1)

            @block.vector
            def _(dve):
                def out(b):
                    dve.wait_ge(outp, b + 1)
                    o4 = ps[0:NCS, 6 + b % 2, 0:4 * HD].rearrange("p (c g d) -> p c g d", c=2, g=2)
                    nc.vector.tensor_copy(vc[:, b, :, :], o4[:, 1])
                    nc.vector.tensor_copy(ko[:, 2 * b:2 * b + 2, :], o4[:, 0]).then_inc(okept, 1)

                for b in range(B):
                    for k in range(1, NF, 2):
                        keep(dve, b * NF + k)
                    if b >= 2:
                        out(b - 2)
                out(B - 2)
                out(B - 1)
                dve.wait_ge(okept, B)
                dve.wait_ge(hid, B)
                chain.link(dve, nc.vector.tensor_tensor(sq, ko[:, :, :], ko[:, :, :], ALU.mult))
                chain.link(dve, nc.vector.tensor_reduce(kss[:, :], sq, AX.X, ALU.add))
                nc.vector.tensor_scalar(kss[:, :], kss[:, :], 1.0 / HD, EPS, ALU.mult, ALU.add).then_inc(kmean, 1)
                dve.wait_ge(kroot, 1)
                chain.link(dve, nc.vector.tensor_tensor(ko[:, :, :], ko[:, :, :], bc(kss[:, :], 2, HD), ALU.mult))
                nc.vector.tensor_tensor(ko[:, :, :], ko[:, :, :], bc(gc[0:NCS, :], 1, B * G), ALU.mult).then_inc(knorm, 1)
                for f in range(4):
                    dve.wait_ge(kturn, f + 1)
                    nc.vector.tensor_copy(kcT[:, 4 * f:4 * f + 4, :],
                                          ps[0:HD, f, :].rearrange("p (n q) -> p n q", n=4)[:, :, 0:NCS]
                                          ).then_inc(kdone, 1)


def stage_s_select(M, A):
    nc, ps, c = (M[k] for k in ("nc", "ps", "c"))
    kcT, vc, qcS, gT, oacc, selneg = (A[k] for k in ("kcT", "vc", "qcS", "gT", "oacc", "selneg"))
    NB, R = PAST // 64 + 1, B * H
    with Stage(nc, "ss") as st:
        sT = st.sb("sT", [NCS, R])
        p_ = st.sb("p", [R, NCS])
        mx = st.sb("mx", [R, 1])
        sm = st.sb("sm", [R, 1])
        pT = st.sb("pT", [NCS, R])
        pg = st.sb("pg", [NCS, B * G])
        imp = st.sb("imp", [B * G, NB])
        cmpv = st.sb("cmpv", [B * G, NB, NB])
        eqv = st.sb("eqv", [B * G, NB, NB])
        tri = st.sb("tri", [B * G, NB, NB])
        cnt = st.sb("cnt", [B * G, NB])
        sem = st.sem
        scored, skept, sturned, maxed, exped, normed, pturned, pkept, attended, summed, ranked, spread, tri_ok = (
            sem(n) for n in ("scored", "skept", "sturned", "maxed", "exped", "normed", "pturned", "pkept",
                             "attended", "summed", "ranked", "spread", "tri_ok"))
        chain = Chain(sem("step"))
        with st.block() as block:
            @block.gpsimd
            def _(pool):
                nc.gpsimd.memset(tri[:, :, :], 1.0).then_inc(tri_ok, 1)
                pool.wait_ge(tri_ok, 1)
                nc.gpsimd.affine_select(out=tri[:, :, :], in_=tri[:, :, :], compare_op=ALU.is_ge, fill=0.0,
                                        base=-1, pattern=[[1, NB], [-1, NB]], channel_multiplier=0).then_inc(tri_ok, 1)

            @block.tensor
            def _(pe):
                for b in range(B):
                    for g in range(G):
                        lo = b * H + g * HPG
                        ins = nc.tensor.matmul(ps[0:NCS, 0, lo:lo + HPG], kcT[:, 2 * b + g, :],
                                               qcS[:, b, g * HPG:(g + 1) * HPG], start=True, stop=True)
                ins.then_inc(scored, 1)
                pe.wait_ge(skept, 1)
                nc.tensor.transpose(ps[0:R, 1, 0:NCS], sT[:, :], c("ident")[0:NCS, 0:NCS]).then_inc(sturned, 1)
                pe.wait_ge(normed, 1)
                nc.tensor.transpose(ps[0:NCS, 2, 0:R], p_[:, :], c("ident")[0:R, 0:R]).then_inc(pturned, 1)
                pe.wait_ge(pkept, 1)
                for b in range(B):
                    ins = nc.tensor.matmul(ps[0:H, 4 + b // 4, (b % 4) * P:(b % 4 + 1) * P], pT[:, b * H:(b + 1) * H],
                                           vc[:, b, :, :].rearrange("p g d -> p (g d)"), start=True, stop=True)
                ins.then_inc(attended, 1)
                pe.wait_ge(summed, 1)
                nc.tensor.matmul(ps[0:B * G, 3, 0:NB], pg[:, :], c("overlap")[0:NCS, :],
                                 start=True, stop=True).then_inc(attended, 1)
                pe.wait_ge(ranked, 1)
                for b in range(B):
                    ins = nc.tensor.matmul(ps[0:H, 6, b * NB:(b + 1) * NB], c("expand")[0:B * G, b * H:(b + 1) * H],
                                           imp[:, :], start=True, stop=True)
                ins.then_inc(spread, 1)

            @block.scalar
            def _(act):
                act.wait_ge(maxed, 1)
                nc.scalar.activation(p_[:, :], ps[0:R, 1, 0:NCS], ACT.Exp, scale=HD ** -0.5, bias=mx[:, :],
                                     accum_out=sm[:, :]).then_inc(exped, 1)

            @block.vector
            def _(dve):
                dve.wait_ge(scored, 1)
                nc.vector.tensor_copy(sT[:, :], ps[0:NCS, 0, 0:R]).then_inc(skept, 1)
                dve.wait_ge(sturned, 1)
                chain.link(dve, nc.vector.tensor_reduce(mx[:, :], ps[0:R, 1, 0:NCS], AX.X, ALU.max))
                nc.vector.tensor_scalar(mx[:, :], mx[:, :], -(HD ** -0.5), None, ALU.mult).then_inc(maxed, 1)
                dve.wait_ge(exped, 1)
                chain.link(dve, nc.vector.reciprocal(sm[:, :], sm[:, :]))
                nc.vector.tensor_scalar(p_[:, :], p_[:, :], sm[:, :], None, ALU.mult).then_inc(normed, 1)
                dve.wait_ge(pturned, 1)
                nc.vector.tensor_copy(pT[:, :], ps[0:NCS, 2, 0:R]).then_inc(pkept, 1)
                nc.vector.tensor_reduce(pg[:, :], ps[0:NCS, 2, 0:R].rearrange("p (n j) -> p n j", j=HPG), AX.X,
                                        ALU.add).then_inc(summed, 1)
                dve.wait_ge(attended, 1)
                nc.vector.tensor_tensor(oacc[:, :, :],
                                        ps[0:H, 4:6, :].rearrange("p k (b d) -> p (k b) d", d=P),
                                        bc(gT[:, 0, :], 2, P), ALU.mult)
                dve.wait_ge(attended, 2)
                chain.link(dve, nc.vector.tensor_copy(imp[:, :], ps[0:B * G, 3, 0:NB]))
                chain.link(dve, nc.vector.memset(imp[:, 0:1], BIG))
                chain.link(dve, nc.vector.memset(imp[:, NB - 1:NB], BIG))
                si, sj = bc(imp[:, :], 1, NB), bc(imp[:, :], 2, NB)
                nc.vector.tensor_tensor(cmpv[:, :, :], si, sj, ALU.is_gt)
                chain.link(dve, nc.vector.tensor_tensor(eqv[:, :, :], si, sj, ALU.is_equal))
                dve.wait_ge(tri_ok, 2)
                chain.link(dve, nc.vector.tensor_tensor(eqv[:, :, :], eqv[:, :, :], tri[:, :, :], ALU.mult))
                chain.link(dve, nc.vector.tensor_tensor(eqv[:, :, :], eqv[:, :, :], cmpv[:, :, :], ALU.add))
                chain.link(dve, nc.vector.tensor_reduce(cnt[:, :], eqv[:, :, :], AX.X, ALU.add))
                nc.vector.tensor_scalar(imp[:, :], cnt[:, :], 15.5, -BIG, ALU.is_ge, ALU.mult).then_inc(ranked, 1)
                dve.wait_ge(spread, 1)
                chain.link(dve, nc.vector.tensor_copy(selneg[:, :, :],
                                                      ps[0:H, 6, 0:B * NB].rearrange("p (b n) -> p b n", b=B)))


def stage_s_attend(M, A):
    nc, I, ps, c, brT = (M[k] for k in ("nc", "I", "ps", "c", "brT"))
    flat = M["x2"][:, :, :].rearrange("p t d -> p (t d)")
    pt, qz, qmz, knT, gT, oacc, selneg, vrow = (
        A[k] for k in ("pt", "qz", "qmz", "knT", "gT", "oacc", "selneg", "vrow"))
    units = [(k, b) for b in range(B) for k in ("slc", "win", "mem")]
    NU = len(units)
    fills_of = {"win": 2, "mem": 2, "slc": 8}
    chunks_of = {"win": 1, "mem": 1, "slc": 4}
    fill0, chunk0 = [0], [0]
    for k, _ in units:
        fill0.append(fill0[-1] + fills_of[k])
        chunk0.append(chunk0[-1] + chunks_of[k])
    LEN = PAST + 8
    with Stage(nc, "sa") as st:
        pages = st.sb("pages", [P, 2, NPG * 256])
        rows = st.sb("rows", [P, 2, 2048])
        kTb = [flat[:, q * 2048:(q + 1) * 2048] for q in range(2)]
        s_ = st.sb("s", [H, 2, LEN])
        pT = st.sb("pT", [P, 2, (NPG + 1) * H])
        mx = st.sb("mx", [H, 2])
        sm = st.sb("sm", [H, 2])
        om = flat[0:XH, 8192:9216].rearrange("p (b d) -> p b d", d=XD)
        own = st.sb("own", [XH, XH, XD])
        snew = st.sb("snew", [H, 2, B])
        sem = st.sem
        in_s = [sem(f"in_s{q}") for q in range(2)]
        in_p = [sem(f"in_p{q}") for q in range(2)]
        in_win, in_mem = sem("in_win"), sem("in_mem")
        (turned, kept_a, kept_v, scored, skept, maxed, exped, pturned, pkept, attended, used, first, newk,
         oturned) = (
            sem(n) for n in ("turned", "kept_a", "kept_v", "scored", "skept", "maxed", "exped", "pturned", "pkept",
                             "attended", "used", "first", "newk", "oturned"))
        chain = Chain(sem("step"))

        def rows_of(u):
            k, b = units[u]
            return pages[:, b % 2, :] if k == "slc" else rows[:, ("win", "mem").index(k), :]

        def wait_rows(pe, u):
            k, b = units[u]
            if k == "slc":
                pe.wait_ge(in_s[b % 2], 8 * NPG * (b // 2 + 1))
                pe.wait_ge(in_p[b % 2], 8 * NPG * (b // 2 + 1))
            else:
                pe.wait_ge(in_win if k == "win" else in_mem, 16 * (b + 1))

        bank = lambda f: ps[:, (0, 1, 2, 7)[f % 4], :]

        def heads(k):
            return XH if k == "mem" else H

        def length(k):
            return {"win": WIN + 1, "mem": XT, "slc": PAST + 1}[k]

        def keep(eng, f):
            u = max(n for n in range(NU) if fill0[n] <= f)
            k, b = units[u]
            j = f - fill0[u]
            eng.wait_ge(turned, f + 1)
            if u >= 2:
                eng.wait_ge(scored, chunk0[u - 1])
            if k == "mem":
                parts = [(kTb[u % 2][:, j * 512:(j + 1) * 512], bank(f))]
            else:
                parts = [(kTb[u % 2][g * HD:(g + 1) * HD, j * 256:(j + 1) * 256],
                          bank(f)[0:HD, g * 256:(g + 1) * 256]) for g in range(G)]
            for dst, src in parts:
                if f % 2 == 0:
                    ins = nc.scalar.activation(dst, src, ACT.Copy)
                else:
                    ins = nc.vector.tensor_copy(dst, src)
            ins.then_inc(kept_a if f % 2 == 0 else kept_v, 1)

        def wait_fills(eng, n):
            if (n + 1) // 2:
                eng.wait_ge(kept_a, (n + 1) // 2)
            if n // 2:
                eng.wait_ge(kept_v, n // 2)

        with st.block() as block:
            @block.sync
            def _(sp):
                def slc(b):
                    if b >= 2:
                        sp.wait_ge(attended, 3 * (b - 2) + 1)
                    load_pages(sp, I["cache_kv_slc"], pages[:, b % 2, :], pt, b, 0, in_s[b % 2])

                slc(0)
                for b in range(B):
                    if b + 1 < B:
                        slc(b + 1)
                    if b >= 1:
                        sp.wait_ge(attended, 3 * (b - 1) + 2)
                    sp.dma_start(rows[:, 0, 0:4 * 256].rearrange("p (t n) -> p t n", t=4),
                                 I["cache_kv_win"][b].rearrange("(t p) g c d -> p t (g c d)", p=P)
                                 ).then_inc(in_win, 16)
                    if b >= 1:
                        sp.wait_ge(attended, 3 * (b - 1) + 3)
                    sp.dma_start(rows[:, 1, :].rearrange("p (t n) -> p t n", t=2),
                                 I["cache_kv_mem"][b].rearrange("(t p) h c d -> p t (h c d)", p=P)
                                 ).then_inc(in_mem, 16)

            @block.gpsimd
            def _(pool):
                for b in range(B):
                    if b >= 2:
                        pool.wait_ge(attended, 3 * (b - 2) + 1)
                    load_pages(pool, I["cache_kv_slc"], pages[:, b % 2, :], pt, b, 1, in_p[b % 2])

            @block.tensor
            def _(pe):
                def turn(u):
                    k, b = units[u]
                    wait_rows(pe, u)
                    kv = rows_of(u)
                    for j in range(fills_of[k]):
                        f = fill0[u] + j
                        if f == 3:
                            pe.wait_ge(newk, 1)
                        if f >= 4:
                            wait_fills(pe, f - 3)
                        for a in range(4):
                            if k == "mem":
                                src, m = kv[:, j * 1024 + a * 256:j * 1024 + a * 256 + XD], P
                            else:
                                o = (2 * j + a % 2) * 256 + (a // 2) * 128
                                src, m = kv[:, o:o + HD], HD
                            ins = nc.tensor.transpose(bank(f)[0:m, a * P:(a + 1) * P], src, c("ident"))
                        ins.then_inc(turned, 1)

                def scores(u):
                    k, b = units[u]
                    wait_fills(pe, fill0[u + 1])
                    for j in range(chunks_of[k]):
                        n = chunk0[u] + j
                        if n >= 2:
                            pe.wait_ge(skept, n - 1)
                        out = ps[0:heads(k), 3 + n % 2, :]
                        if k == "mem":
                            kt = kTb[u % 2][:, 0:1024].rearrange("p (t h q) -> p t h q", t=2, h=XH)
                            for h in range(XH):
                                ins = nc.tensor.matmul(out[:, 0:XT], qmz[:, b, h, :], kt[:, :, h, :],
                                                       start=(h == 0), stop=(h == XH - 1))
                        else:
                            ins = nc.tensor.matmul(out, qz[:, b, :], kTb[u % 2][:, j * 512:(j + 1) * 512],
                                                   start=True, stop=True)
                        ins.then_inc(scored, 1)

                def turn_p(u):
                    k, b = units[u]
                    nh = heads(k)
                    pe.wait_ge(exped, u + 1)
                    if u >= 1:
                        pe.wait_ge(pkept, u)
                    full = length(k) // P
                    for t in range(full):
                        ins = nc.tensor.transpose(ps[:, 5, t * nh:(t + 1) * nh], s_[0:nh, u % 2, t * P:(t + 1) * P],
                                                  c("ident")[0:nh, 0:nh])
                    if k != "mem":
                        ins = nc.tensor.transpose(ps[0:1, 5, full * nh:(full + 1) * nh],
                                                  s_[0:nh, u % 2, full * P:full * P + 1], c("ident")[0:nh, 0:nh])
                    ins.then_inc(pturned, 1)

                def attend(u):
                    k, b = units[u]
                    kv = rows_of(u)
                    nh, full = heads(k), length(k) // P
                    pe.wait_ge(pkept, u + 1)
                    if u >= 1:
                        pe.wait_ge(used, u)
                    for t in range(full):
                        w = pT[:, u % 2, t * nh:(t + 1) * nh]
                        if k == "mem":
                            rhs = kv[:, t * 1024:(t + 1) * 1024].rearrange("p (h c d) -> p h c d", c=2, d=XD)[:, :, 1, :]
                            out = ps[0:nh, 6, 0:512]
                        else:
                            rhs = kv[:, t * 256:(t + 1) * 256].rearrange("p (g c d) -> p g c d", c=2, d=HD)[:, :, 1, :]
                            out = ps[0:nh, 6, 0:P]
                        ins = nc.tensor.matmul(out, w, rhs, start=(t == 0), stop=(t == full - 1 and k == "mem"))
                    if k != "mem":
                        br, q = 0 if k == "slc" else 1, 32 * (b // 2)
                        ins = nc.tensor.matmul(out, pT[q:q + 1, u % 2, full * nh:(full + 1) * nh],
                                               vrow[q:q + 1, b % 2, 2 * br:2 * br + 2, :].rearrange("p g d -> p (g d)"),
                                               start=False, stop=True)
                    ins.then_inc(attended, 1)

                for br in range(2):
                    for b in range(B):
                        ins = nc.tensor.matmul(ps[0:H, 7, br * B + b:br * B + b + 1], qz[:, b, :],
                                               knT[:, br, b:b + 1], start=True, stop=True)
                ins.then_inc(first, 1)
                turn(0)
                for u in range(NU):
                    if u + 1 < NU:
                        turn(u + 1)
                    if u >= 1:
                        turn_p(u - 1)
                    scores(u)
                    if u >= 1:
                        attend(u - 1)
                turn_p(NU - 1)
                attend(NU - 1)
                pe.wait_ge(used, NU)
                for b in range(B):
                    nc.tensor.transpose(ps[:, 0, b * H:(b + 1) * H], oacc[:, b, :], c("ident")[0:H, 0:H])
                    ins = nc.tensor.transpose(ps[:, 1, b * XH:(b + 1) * XH], om[:, b, :], c("ident")[0:XH, 0:XH])
                ins.then_inc(oturned, 1)

            @block.scalar
            def _(act):
                def softmax(u):
                    k, b = units[u]
                    nh, n = heads(k), length(k)
                    act.wait_ge(maxed, u + 1)
                    sc = XD ** -0.5 if k == "mem" else HD ** -0.5
                    if u >= 2:
                        act.wait_ge(used, u - 1)
                    nc.scalar.activation(s_[0:nh, u % 2, 0:n], s_[0:nh, u % 2, 0:n], ACT.Exp, scale=sc,
                                         bias=mx[0:nh, u % 2:u % 2 + 1],
                                         accum_out=sm[0:nh, u % 2:u % 2 + 1]).then_inc(exped, 1)

                def keep_p(u):
                    k, b = units[u]
                    nh, full = heads(k), length(k) // P
                    act.wait_ge(pturned, u + 1)
                    if u >= 2:
                        act.wait_ge(attended, u - 1)
                    if k == "mem":
                        nc.scalar.activation(pT[:, u % 2, 0:full * nh], ps[:, 5, 0:full * nh], ACT.Copy).then_inc(pkept, 1)
                    else:
                        nc.scalar.activation(pT[:, u % 2, 0:full * nh], ps[:, 5, 0:full * nh], ACT.Copy)
                        nc.scalar.activation(pT[32 * (b // 2):32 * (b // 2) + 1, u % 2, full * nh:(full + 1) * nh],
                                             ps[0:1, 5, full * nh:(full + 1) * nh], ACT.Copy).then_inc(pkept, 1)

                for f in range(fill0[1]):
                    if f % 2 == 0:
                        keep(act, f)
                for u in range(NU):
                    if u + 1 < NU:
                        for f in range(fill0[u + 1], fill0[u + 2]):
                            if f % 2 == 0:
                                keep(act, f)
                    if u >= 1:
                        keep_p(u - 1)
                    softmax(u)
                keep_p(NU - 1)

            @block.vector
            def _(dve):
                def gather(u):
                    k, b = units[u]
                    nh, n = heads(k), length(k)
                    if u >= 2:
                        dve.wait_ge(pturned, u - 1)
                    for j in range(chunks_of[k]):
                        cn = chunk0[u] + j
                        dve.wait_ge(scored, cn + 1)
                        src = ps[0:nh, 3 + cn % 2, :]
                        if k == "mem":
                            ins = nc.vector.tensor_copy(s_[0:nh, u % 2, 0:XT], src[:, 0:XT])
                        elif k == "win":
                            ins = nc.vector.tensor_copy(s_[:, u % 2, 0:WIN], src)
                        else:
                            ins = nc.vector.tensor_tensor(
                                s_[:, u % 2, j * 512:(j + 1) * 512].rearrange("p (n e) -> p n e", e=64),
                                src.rearrange("p (n e) -> p n e", e=64), bc(selneg[:, b, 8 * j:8 * j + 8], 2, 64),
                                ALU.add)
                        ins.then_inc(skept, 1)
                    if k != "mem":
                        br = 0 if k == "slc" else 1
                        chain.link(dve, nc.vector.tensor_copy(s_[:, u % 2, n - 1:n], snew[:, br, b:b + 1]))
                    dve.wait_ge(skept, chunk0[u + 1])
                    chain.link(dve, nc.vector.tensor_reduce(mx[0:nh, u % 2:u % 2 + 1], s_[0:nh, u % 2, 0:n], AX.X,
                                                            ALU.max))
                    sc = XD ** -0.5 if k == "mem" else HD ** -0.5
                    nc.vector.tensor_scalar(mx[0:nh, u % 2:u % 2 + 1], mx[0:nh, u % 2:u % 2 + 1], -sc, None,
                                            ALU.mult).then_inc(maxed, 1)

                def use(u):
                    k, b = units[u]
                    nh = heads(k)
                    f = sm[0:nh, u % 2:u % 2 + 1]
                    dve.wait_ge(exped, u + 1)
                    chain.link(dve, nc.vector.reciprocal(f, f))
                    if k != "mem":
                        br = 1 if k == "slc" else 2
                        chain.link(dve, nc.vector.tensor_tensor(f, f, gT[:, br, b:b + 1], ALU.mult))
                    dve.wait_ge(attended, u + 1)
                    if k == "mem":
                        chain.link(dve, nc.vector.scalar_tensor_tensor(
                            own[:, :, :], ps[0:nh, 6, :].rearrange("p (h d) -> p h d", h=XH), f,
                            bc(c("ident")[0:XH, 0:XH], 2, XD), ALU.mult, ALU.mult))
                        nc.vector.tensor_reduce(om[:, b, :], own[:, :, :].rearrange("p h d -> p d h"), AX.X,
                                                ALU.add).then_inc(used, 1)
                    else:
                        if u >= 1:
                            dve.wait_ge(used, u)
                        nc.vector.scalar_tensor_tensor(oacc[:, b, :], ps[0:nh, 6, 0:P], f, oacc[:, b, :],
                                                       ALU.mult, ALU.add).then_inc(used, 1)

                dve.wait_ge(first, 1)
                nc.vector.tensor_copy(snew[:, :, :].rearrange("p r b -> p (r b)"), ps[0:H, 7, 0:2 * B]).then_inc(newk, 1)
                dve.wait_ge(newk, 1)
                for f in range(fill0[1]):
                    if f % 2 == 1:
                        keep(dve, f)
                for u in range(NU):
                    if u + 1 < NU:
                        for f in range(fill0[u + 1], fill0[u + 2]):
                            if f % 2 == 1:
                                keep(dve, f)
                    gather(u)
                    if u >= 1:
                        use(u - 1)
                use(NU - 1)
                dve.wait_ge(oturned, 1)
                for h in range(H):
                    lo, g = (h % 2) * HD, h // HPG
                    src = ps[g * HD:(g + 1) * HD, 0, 0:B * H].rearrange("p (b h) -> p b h", h=H)[:, :, h]
                    nc.vector.tensor_copy(brT[lo:lo + HD, h // 2, S:T], src)
                chain.link(dve, nc.vector.tensor_copy(brT[:, 8:12, S:T],
                                                      ps[:, 1, 0:B * XH].rearrange("p (b h) -> p h b", h=XH)))


def stage_samples(M):
    nc = M["nc"]
    with Stage(nc, "s") as st:
        A = dict(
            pt=st.sb("pt", [1, B * NPG], I32), vrow=st.sb("vrow", [P, 2, 4, HD]),
            qcS=st.sb("qcS", [HD, B, H]), qz=st.sb("qz", [P, B, H]), knT=st.sb("knT", [P, 2, B]),
            qmz=st.sb("qmz", [P, B, XH, XH]), gT=st.sb("gT", [H, 3, B]), oacc=st.sb("oacc", [H, B, P]),
            selneg=st.sb("selneg", [H, B, PAST // 64 + 1]), bias=M["bias"])
        stage_s_prep(M, A)
        with Stage(nc, "s2") as s2:
            flat = M["x2"][:, :, :].rearrange("p t d -> p (t d)")
            A["kcT"] = flat[0:HD, 0:B * G * NCS].rearrange("p (n q) -> p n q", q=NCS)
            A["vc"] = s2.sb("vc", [NCS, B, G, HD])
            stage_s_compress(M, A)
            stage_s_select(M, A)
        stage_s_attend(M, A)


def stage_merge(M):
    nc, I, xnT, brT, ps, x2 = (M[k] for k in ("nc", "I", "xnT", "brT", "ps", "x2"))
    mixT = M["mixT"]
    wg = I["w_in"].rearrange("(k p) n -> p k n", p=P)
    wb = I["w_branch"].rearrange("n (k p) d -> p n k d", p=P)
    W = 256
    loads = [(jp, n) for jp in range(D // W) for n in range(3)]
    steps = [(l, jj, b) for l in range(len(loads)) for jj in range(W // P) for b in range(NB3)]
    per = W // P * NB3
    with Stage(nc, "mg") as st:
        wgs = st.sb("wg", [P, 2, KT, W])
        wbs = st.sb("wb", [P, 2, 4, W])
        sg = st.sb("sg", [P, 2, BLK])
        tm = st.sb("tm", [P, BLK])
        sem = st.sem
        in_w = [sem(f"in_w{q}") for q in range(2)]
        in_x, projected, gated, merged = (sem(n) for n in ("in_x", "projected", "gated", "merged"))
        chain = Chain(sem("step"))
        with st.block() as block:
            @block.sync
            def _(sp):
                for l, (jp, n) in enumerate(loads):
                    if l >= 2:
                        sp.wait_ge(projected, per * (l - 1))
                    q = l % 2
                    col = C_MG + n * D + jp * W
                    sp.dma_start(wgs[:, q, :, :], wg[:, :, col:col + W]).then_inc(in_w[q], 16)
                    sp.dma_start(wbs[:, q, :, :], wb[:, n, :, jp * W:(jp + 1) * W]).then_inc(in_w[q], 16)
                    if l == 1:
                        sp.dma_start(x2[:, 0:QT, :], I["x_prompt"].rearrange("o (t p) d -> p (o t) d", p=P)
                                     ).then_inc(in_x, 16)
                        sp.dma_start(x2[0:B, QT, :], I["x_sample"].rearrange("b o d -> (b o) d")).then_inc(in_x, 16)
                sp.wait_ge(in_x, 32)

            @block.tensor
            def _(pe):
                for s, (l, jj, b) in enumerate(steps):
                    if s % per == 0:
                        pe.wait_ge(in_w[l % 2], 32 * (l // 2 + 1))
                    if s >= 4:
                        pe.wait_ge(merged, s - 3)
                    n = loads[l][1]
                    cols, toks = slice(jj * P, (jj + 1) * P), slice(b * BLK, (b + 1) * BLK)
                    for k in range(KT):
                        nc.tensor.matmul(ps[:, s % 4, 0:BLK], wgs[:, l % 2, k, cols], xnT[:, k, toks],
                                         start=(k == 0), stop=(k == KT - 1))
                    for k in range(4):
                        ins = nc.tensor.matmul(ps[:, 4 + s % 4, 0:BLK], wbs[:, l % 2, k, cols],
                                               brT[:, 4 * n + k, toks], start=(k == 0), stop=(k == 3))
                    ins.then_inc(projected, 1)

            @block.scalar
            def _(act):
                for s in range(len(steps)):
                    act.wait_ge(projected, s + 1)
                    if s >= 2:
                        act.wait_ge(merged, s - 1)
                    nc.scalar.activation(sg[:, s % 2, :], ps[:, s % 4, 0:BLK], ACT.Sigmoid).then_inc(gated, 1)

            @block.vector
            def _(dve):
                for s, (l, jj, b) in enumerate(steps):
                    jp, n = loads[l]
                    dve.wait_ge(gated, s + 1)
                    dst = mixT[:, jp * (W // P) + jj, b * BLK:(b + 1) * BLK]
                    if n == 0:
                        nc.vector.tensor_tensor(dst, sg[:, s % 2, :], ps[:, 4 + s % 4, 0:BLK],
                                                ALU.mult).then_inc(merged, 1)
                    else:
                        dve.wait_ge(merged, s)
                        chain.link(dve, nc.vector.tensor_tensor(tm[:, :], sg[:, s % 2, :], ps[:, 4 + s % 4, 0:BLK],
                                                                ALU.mult))
                        nc.vector.tensor_tensor(dst, dst, tm[:, :], ALU.add).then_inc(merged, 1)


def stage_out(M):
    nc, I, xnT, ps, x2, c = (M[k] for k in ("nc", "I", "xnT", "ps", "x2", "c"))
    mixT = M["mixT"]
    with Stage(nc, "out") as st:
        w = st.sb("w", [P, 2, KT, 512])
        gain = st.sb("gain", [P, KT])
        ss = st.sb("ss", [P, TT])
        xs = mixT[:, :, :].rearrange("p k t -> p (k t)")
        sem = st.sem
        in_w = [sem(f"in_w{q}") for q in range(2)]
        in_g, cleared, projected, added, squared, meaned, rooted, scaled, turned, stored = (
            sem(n) for n in ("in_g", "cleared", "projected", "added", "squared", "meaned", "rooted", "scaled",
                             "turned", "stored"))
        junk = st.sb("junk", [P, D])
        wv = I["w_out"].rearrange("(k p) n -> p k n", p=P)
        with st.block() as block:
            @block.sync
            def _(sp):
                for q in range(2):
                    sp.dma_start(w[:, q, :, :], wv[:, :, q * 512:(q + 1) * 512]).then_inc(in_w[q], 16)
                sp.dma_start(gain[:, :], I["norm_ffn"].rearrange("(k p) -> p k", p=P),
                             allow_slow_non_contiguous=True).then_inc(in_g, 16)

            @block.gpsimd
            def _(pool):
                pool.wait_ge(meaned, 1)
                nc.gpsimd.tensor_tensor(ss[:, :], ss[:, :], c("mhalf").to_broadcast([P, TT]),
                                        ALU.pow).then_inc(rooted, 1)

            @block.tensor
            def _(pe):
                n = 0
                for q in range(2):
                    pe.wait_ge(in_w[q], 16)
                    for t in range(TT):
                        m = B if t == QT else P
                        if n >= 4:
                            pe.wait_ge(added, n - 3)
                        for k in range(KT):
                            ins = nc.tensor.matmul(ps[0:m, n % 4, :], mixT[:, k, t * P:t * P + m], w[:, q, k, :],
                                                   start=(k == 0), stop=(k == KT - 1))
                        ins.then_inc(projected, 1)
                        n += 1
                n = 0
                for t in range(TT):
                    m = B if t == QT else P
                    pe.wait_ge(scaled, t + 1)
                    for kk in range(2):
                        if n >= 4:
                            pe.wait_ge(stored, n - 3)
                        for a in range(4):
                            k = 4 * kk + a
                            ins = nc.tensor.transpose(ps[:, 4 + n % 4, a * P:a * P + m],
                                                      xs[0:m, (t % 4) * D + k * P:(t % 4) * D + (k + 1) * P],
                                                      c("ident")[0:m, 0:m])
                        ins.then_inc(turned, 1)
                        n += 1

            @block.scalar
            def _(act):
                for t in range(TT):
                    m = B if t == QT else P
                    act.wait_ge(added, TT + t + 1)
                    if t:
                        act.wait_ge(squared, t)
                    nc.scalar.activation(junk[0:m, :], x2[0:m, t, :], ACT.Square,
                                         accum_out=ss[0:m, t:t + 1]).then_inc(squared, 1)

            def store(dve, n):
                t, kk = n // 2, n % 2
                m = B if t == QT else P
                dve.wait_ge(turned, n + 1)
                src = ps[:, 4 + n % 4, :].rearrange("p (a q) -> p a q", a=4)[:, :, 0:m]
                nc.vector.tensor_tensor(xnT[:, 4 * kk:4 * kk + 4, t * P:t * P + m], src,
                                        bc(gain[:, 4 * kk:4 * kk + 4], 2, m), ALU.mult).then_inc(stored, 1)

            @block.vector
            def _(dve):
                nc.vector.memset(ss[:, :], 1.0).then_inc(cleared, 1)
                n = 0
                for q in range(2):
                    for t in range(TT):
                        m = B if t == QT else P
                        dve.wait_ge(projected, n + 1)
                        dst = x2[0:m, t, q * 512:(q + 1) * 512]
                        nc.vector.tensor_tensor(dst, dst, ps[0:m, n % 4, :], ALU.add).then_inc(added, 1)
                        n += 1
                dve.wait_ge(squared, TT)
                nc.vector.tensor_scalar(ss[:, :], ss[:, :], 1.0 / D, EPS, ALU.mult, ALU.add).then_inc(meaned, 1)
                dve.wait_ge(rooted, 1)
                dve.wait_ge(in_g, 16)
                for t in range(TT):
                    m = B if t == QT else P
                    if t >= 4:
                        dve.wait_ge(turned, 2 * (t - 3))
                    nc.vector.tensor_scalar(xs[0:m, (t % 4) * D:(t % 4 + 1) * D], x2[0:m, t, :], ss[0:m, t:t + 1],
                                            None, ALU.mult).then_inc(scaled, 1)
                    for n in range(2 * t - 2, 2 * t) if t else ():
                        store(dve, n)
                for n in range(2 * TT - 2, 2 * TT):
                    store(dve, n)


def stage_ffn_in(M, hid):
    nc, I, xnT, ps = (M[k] for k in ("nc", "I", "xnT", "ps"))
    wv = I["w_ffn_in"].rearrange("(k p) (s n) -> p k s n", p=P, s=2)
    W = 256
    steps = [(j, b) for j in range(FJ) for b in range(NB3)]
    per = W // P * NB3
    with Stage(nc, "fi") as st:
        w = st.sb("w", [P, 2, KT, 2, W])
        sa = M["memT"][:, :, :].rearrange("p k t -> p (k t)")[:, 0:2 * BLK].rearrange("p (s n) -> p s n", s=2)
        sem = st.sem
        in_w = [sem(f"in_w{q}") for q in range(2)]
        projected, silued, multiplied = (sem(n) for n in ("projected", "silued", "multiplied"))
        with st.block() as block:
            @block.sync
            def _(sp):
                for l in range(FH // W):
                    if l >= 2:
                        sp.wait_ge(projected, per * (l - 1))
                    for s in range(2):
                        sp.dma_start(w[:, l % 2, :, s, :], wv[:, :, s, l * W:(l + 1) * W]).then_inc(in_w[l % 2], 16)

            @block.tensor
            def _(pe):
                for s, (j, b) in enumerate(steps):
                    l, jj = j // 2, j % 2
                    if s % per == 0:
                        pe.wait_ge(in_w[l % 2], 32 * (l // 2 + 1))
                    if s >= 4:
                        pe.wait_ge(multiplied, s - 3)
                    for half in range(2):
                        for k in range(KT):
                            ins = nc.tensor.matmul(ps[:, 4 * half + s % 4, 0:BLK],
                                                   w[:, l % 2, k, half, jj * P:(jj + 1) * P],
                                                   xnT[:, k, b * BLK:(b + 1) * BLK],
                                                   start=(k == 0), stop=(k == KT - 1))
                    ins.then_inc(projected, 1)

            @block.scalar
            def _(act):
                for s in range(len(steps)):
                    act.wait_ge(projected, s + 1)
                    if s >= 2:
                        act.wait_ge(multiplied, s - 1)
                    nc.scalar.activation(sa[:, s % 2, :], ps[:, s % 4, 0:BLK], ACT.Silu).then_inc(silued, 1)

            @block.vector
            def _(dve):
                for s, (j, b) in enumerate(steps):
                    dve.wait_ge(silued, s + 1)
                    nc.vector.tensor_tensor(hid(j)[:, b * BLK:(b + 1) * BLK], sa[:, s % 2, :],
                                            ps[:, 4 + s % 4, 0:BLK], ALU.mult).then_inc(multiplied, 1)


def stage_ffn_out(M, hid):
    nc, I, O, xnT, ps, x2 = (M[k] for k in ("nc", "I", "O", "xnT", "ps", "x2"))
    wv = I["w_ffn_out"].rearrange("(j p) n -> p j n", p=P)
    with Stage(nc, "fo") as st:
        more = st.sb("w", [P, 17, 512])
        base = xnT[:, :, :].rearrange("p k t -> p (k t)")
        place = [base[:, s * 512:(s + 1) * 512] for s in range(16)] + [more[:, s, :] for s in range(17)]
        slot = lambda q, j: place[j if q == 0 else (22 + j if j < 11 else j)]
        sem = st.sem
        in_w = [sem(f"in_w{q}") for q in range(3)]
        projected, added, out = (sem(n) for n in ("projected", "added", "out"))
        with st.block() as block:
            @block.sync
            def _(sp):
                for j in range(FJ):
                    sp.dma_start(slot(0, j), wv[:, j, 0:512]).then_inc(in_w[0], 16)
                for j in range(11):
                    sp.dma_start(slot(1, j), wv[:, j, 512:1024]).then_inc(in_w[1], 16)
                sp.wait_ge(projected, TT)
                for j in range(11, FJ):
                    sp.dma_start(slot(1, j), wv[:, j, 512:1024]).then_inc(in_w[2], 16)
                for n in range(2 * TT):
                    q, t = n // TT, n % TT
                    sp.wait_ge(added, n + 1)
                    cols = slice(q * 512, (q + 1) * 512)
                    if t < QT:
                        sp.dma_start(O["y_prompt"][0, t * P:(t + 1) * P, cols], x2[:, t, cols]).then_inc(out, 16)
                    else:
                        sp.dma_start(O["y_sample"][:, 0, cols], x2[0:B, t, cols]).then_inc(out, 16)
                sp.wait_ge(out, 16 * 2 * TT)

            @block.tensor
            def _(pe):
                for n in range(2 * TT):
                    q, t = n // TT, n % TT
                    m = B if t == QT else P
                    if n >= 4:
                        pe.wait_ge(added, n - 3)
                    if t == 0:
                        pe.wait_ge(in_w[q], 16 * (FJ if q == 0 else 11))
                    for j in range(FJ):
                        if q == 1 and t == 0 and j == 11:
                            pe.wait_ge(in_w[2], 16 * 11)
                        ins = nc.tensor.matmul(ps[0:m, n % 4, :], hid(j)[:, t * P:t * P + m], slot(q, j),
                                               start=(j == 0), stop=(j == FJ - 1))
                    ins.then_inc(projected, 1)

            @block.vector
            def _(dve):
                for n in range(2 * TT):
                    q, t = n // TT, n % TT
                    m = B if t == QT else P
                    dve.wait_ge(projected, n + 1)
                    dst = x2[0:m, t, q * 512:(q + 1) * 512]
                    nc.vector.tensor_tensor(dst, dst, ps[0:m, n % 4, :], ALU.add).then_inc(added, 1)


def stage_tail(M):
    nc, brT = M["nc"], M["brT"]
    with Stage(nc, "t1") as st:
        M["mixT"] = st.sb("mixT", [P, KT, T])
        stage_merge(M)
        stage_out(M)
    with Stage(nc, "t2") as st:
        more = st.sb("hid", [P, FJ - 12, T])
        hid = lambda j: brT[:, j, :] if j < 12 else more[:, j - 12, :]
        stage_ffn_in(M, hid)
        stage_ffn_out(M, hid)


STAGES = [stage_ml_proj, stage_mlstm, stage_attention, stage_samples, stage_tail]
RENEW_BEFORE = [stage_attention, stage_samples, stage_tail]

IN_SHAPES = None
OUT_SHAPES = [
    ("y_prompt", (1, S, D)), ("y_sample", (B, 1, D)),
    ("kv_cmp_prompt", (1, S, G, 2, HD)), ("kv_cmp_sample", (B, 1, G, 2, HD)),
    ("kv_slc_prompt", (1, S, G, 2, HD)), ("kv_slc_sample", (B, 1, G, 2, HD)),
    ("win_prompt", (1, WIN, G, 2, HD)), ("win_sample", (B, WIN, G, 2, HD)),
    ("kv_mem_prompt", (1, XT, XH, 2, XD)),
    ("C_prompt", (1, MH, MD, MD)), ("C_sample", (B, MH, MD, MD)),
    ("n_prompt", (1, MH, MD)), ("n_sample", (B, MH, MD)),
    ("m_prompt", (1, MH)), ("m_sample", (B, MH)),
    ("conv_prompt", (1, 3, MH * MD)), ("conv_sample", (B, 3, MH * MD)),
]


def kernel(**inputs):
    import concourse.bacc as bacc
    from concourse.bass_utils import run_bass_kernel_spmd

    nc = bacc.Bacc("TRN2", target_bir_lowering=False, num_devices=1)
    arrays, I, O = {}, {}, {}
    inputs = dict(inputs)
    inputs["const"] = CONST
    for name, a in inputs.items():
        a = np.ascontiguousarray(a)
        arrays[f"in_{name}"] = a
        I[name] = nc.dram_tensor(f"in_{name}", a.shape, mybir.dt.from_np(a.dtype), kind="ExternalInput").ap()
    for name, shape in OUT_SHAPES:
        O[name] = nc.dram_tensor(f"out_{name}", shape, F32, kind="ExternalOutput").ap()
    build(nc, I, O)
    r = run_bass_kernel_spmd(nc, [arrays], core_ids=[0])
    return tuple(r.results[0][f"out_{name}"] for name, _ in OUT_SHAPES)
```

```python
from contextlib import ExitStack

import numpy as np
import concourse.bass as bass
from concourse import mybir

F32 = mybir.dt.float32
FR = mybir.dt.float32r
I32 = mybir.dt.int32
ALU = mybir.AluOpType
ACT = mybir.ActivationFunctionType
AX = mybir.AxisListType

P = 128
D = 1024
KT = D // P
S = 1024
QT = S // P
B = 8
T = S + B
TT = QT + 1
NB3, BLK = 3, T // 3
PAST, PAGE = 2048, 128
NPG = PAST // PAGE
NPHYS = 160
H, G, HPG, HD = 8, 2, 4, 64
HALF = 8
NC = 63
NCS = 127
CH = 128
WIN = 512
MH, MD = 4, 128
L = 128
NCK = S // L
XT, XH, XD = 256, 4, 128
FH = 2816
FJ = FH // P
EPS = 1e-6
BIG = 1e30
C_Q, C_G, C_KVC, C_KVS, C_U, C_O, C_I, C_F, C_MQ, C_MG = (
    0, 512, 536, 792, 1304, 1816, 2328, 2332, 2336, 2848)
IN_W = 5920


def constant_table():
    p = np.arange(P)[:, None]
    f = np.arange(P)[None, :]
    parts, at, n = [], {}, 0

    def put(name, a):
        nonlocal n
        a = np.asarray(a, np.float32).reshape(P, -1)
        at[name] = (n, n + a.shape[1])
        parts.append(a)
        n += a.shape[1]

    put("ident", p == f)
    put("ones", np.ones((P, P)))
    put("mhalf", np.full((P, 1), -0.5))
    put("causal", np.where(f <= p, 0.0, -BIG))
    put("band", np.where(f >= p, 0.0, -BIG))
    put("future", np.where(p <= f, 0.0, BIG))
    q = np.arange(QT)[None, :, None] * P + np.arange(P)[:, None, None]
    n_ = np.arange(64)[None, None, :]
    put("cmp01", (n_ * 16 + 31 <= q) & (n_ < NC))
    pos = np.concatenate([np.arange(S).reshape(QT, P).T, np.full((P, 1), PAST)], 1).astype(np.float32)
    freqs = np.float32(500000.0) ** (-np.arange(HALF, dtype=np.float32) / np.float32(HALF))
    ang = pos[:, :, None] * freqs.astype(np.float32)
    put("cos", np.cos(ang))
    put("sin", np.sin(ang))
    col = np.arange(B * H)[None, :]
    put("expand", p == (col // H) * G + (col % H) // HPG)
    ci, sj = np.arange(P)[:, None] * 16, np.arange(33)[None, :] * 64
    put("overlap", (ci < sj + 64) & (ci + 32 > sj) & (p < NCS))
    return np.concatenate(parts, 1), at


CONST, CAT = constant_table()
NCONST = CONST.shape[1]


class Stage:

    retired = []

    @staticmethod
    def renew(nc):
        nc.clear_and_free_semaphores(Stage.retired)
        nc.all_engine_barrier()
        Stage.retired = []

    def __init__(self, nc, name):
        self.nc, self.name, self.ctx, self.sems = nc, name, ExitStack(), []

    def __enter__(self):
        return self

    def __exit__(self, *a):
        Stage.retired += self.sems
        return self.ctx.__exit__(*a)

    def sb(self, name, shape, dt=F32):
        return self.ctx.enter_context(self.nc.sbuf_tensor(f"{self.name}_{name}", shape, dt))

    def pair(self, name, shape):
        return pair(self.nc, self.ctx, f"{self.name}_{name}", shape)

    def sem(self, name):
        s = self.nc.alloc_semaphore(f"{self.name}_{name}")
        self.sems.append(s)
        return s

    def block(self):
        return self.nc.Block()


class Chain:

    def __init__(self, sem):
        self.sem, self.n = sem, 0

    def link(self, eng, ins):
        self.n += 1
        ins.then_inc(self.sem, 1)
        eng.wait_ge(self.sem, self.n)


def bc(ap, axis, n):
    v = ap.unsqueeze(axis)
    shape = list(v.shape)
    shape[axis] = n
    return v.to_broadcast(shape)


def pair(nc, ctx, name, shape):
    at = (nc.sbuf_base + 31) // 32 * 32
    x = ctx.enter_context(nc.sbuf_tensor(name, shape, F32))
    return x, nc.alloc_sbuf_tensor_at(name + "_r", shape, FR, offset=at)


def high(nc, hi, x):
    return nc.scalar.activation(hi, x, ACT.Copy)


def low(nc, lo, x, hi):
    return nc.vector.tensor_tensor(lo, x, hi.bitcast(F32), ALU.subtract)


def whole(nc, x, lo, hi):
    return nc.vector.tensor_tensor(x, lo.bitcast(F32), hi.bitcast(F32), ALU.add)


def products(nc, out, pairs, first=True, last=True):
    n = len(pairs)
    for k, ((wh, wl), (xh, xl)) in enumerate(pairs):
        nc.tensor.matmul(out, wh, xh, start=(first and k == 0), stop=False)
        nc.tensor.matmul(out, wh, xl, start=False, stop=False)
        ins = nc.tensor.matmul(out, wl, xh, start=False, stop=(last and k == n - 1))
    return ins


def build(nc, I, O):
    top = ExitStack()
    Stage.retired = []
    with top:
        cst = top.enter_context(nc.sbuf_tensor("cst", [P, NCONST], F32))
        x2, x2R = pair(nc, top, "x2", [P, TT, D])
        xnT, xnR = pair(nc, top, "xnT", [P, KT, T])
        brT, brR = pair(nc, top, "brT", [P, 12, T])
        ps = top.enter_context(nc.psum_tensor("ps", [P, 8, 512], F32))
        M = dict(nc=nc, I=I, O=O, cst=cst, x2=x2, xnT=xnT, brT=brT, ps=ps)
        c = lambda name: cst[:, CAT[name][0]:CAT[name][1]]
        M["c"] = c
        M["memT"], M["memR"] = pair(nc, top, "memT", [P, KT, XT])
        M.update(x2R=x2R, xnR=xnR, brR=brR)
        flat = x2[:, :, :].rearrange("p t d -> p (t d)")
        names = ["ig", "lf", "b", "m", "M", "reset", "stack", "tmp"]
        M["row"] = lambda n: flat[:, names.index(n) * 1040:names.index(n) * 1040 + T]
        M["bias"] = top.enter_context(nc.sbuf_tensor("bias", [P, 2], F32))
        M["gS"] = top.enter_context(nc.sbuf_tensor("gS", [B, 280], F32))[:, :]
        stage_norm(M)
        for s in STAGES:
            if s in RENEW_BEFORE:
                Stage.renew(nc)
            s(M)


def stage_norm(M):
    nc, I, cst, xnT, ps, c = (M[k] for k in ("nc", "I", "cst", "xnT", "ps", "c"))
    NT = TT + 2
    groups = [(t, t + 2) for t in range(0, QT, 2)] + [(QT, NT)]
    with Stage(nc, "norm") as st:
        X = st.sb("X", [P, NT, D])
        gm = st.sb("gain", [P, 2, KT])
        ss = st.sb("ss", [P, NT])
        rs = st.sb("rs", [P, NT])
        junk = st.sb("junk", [P, D])
        memT = M["memT"]
        in_c, cleared, squared, meaned, rooted, scaled, turned, stored = (
            st.sem(n) for n in ("in_c", "cleared", "squared", "meaned", "rooted", "scaled", "turned", "stored"))
        in_x = [st.sem(f"in_x{g}") for g in range(len(groups))]

        with st.block() as block:
            @block.sync
            def _(sp):
                xp = I["x_prompt"].rearrange("o (t p) d -> p (o t) d", p=P)
                for g, (lo, hi) in enumerate(groups[:-1]):
                    sp.dma_start(X[:, lo:hi, :], xp[:, lo:hi, :]).then_inc(in_x[g], 16)
                    if g == 0:
                        sp.dma_start(cst[:, :], I["const"]).then_inc(in_c, 16)
                sp.wait_ge(cleared, 1)
                sp.dma_start(X[0:B, QT, :], I["x_sample"].rearrange("b o d -> (b o) d")).then_inc(in_x[-1], 16)
                sp.dma_start(X[:, TT:NT, :], I["mem_prompt"].rearrange("o (t p) d -> p (o t) d", p=P)
                             ).then_inc(in_x[-1], 16)

            @block.gpsimd
            def _(pool):
                nc.gpsimd.memset(X[:, QT, :], 0.0).then_inc(cleared, 1)
                pool.wait_ge(in_c, 48)
                for g, (lo, hi) in enumerate(groups):
                    pool.wait_ge(meaned, g + 1)
                    nc.gpsimd.tensor_tensor(rs[:, lo:hi], rs[:, lo:hi], c("mhalf").to_broadcast([P, hi - lo]),
                                            ALU.pow).then_inc(rooted, 1)

            @block.scalar
            def _(act):
                for n, name in enumerate(("norm_mix", "norm_mem")):
                    act.dma_start(gm[:, n, :], I[name].rearrange("(k p) -> p k", p=P),
                                  allow_slow_non_contiguous=True).then_inc(in_c, 16)
                for g, (lo, hi) in enumerate(groups):
                    act.wait_ge(in_x[g], 32 if hi == NT else 16)
                    for t in range(lo, hi):
                        if t:
                            act.wait_ge(squared, t)
                        nc.scalar.activation(junk[:, :], X[:, t, :], ACT.Square,
                                             accum_out=ss[:, t:t + 1]).then_inc(squared, 1)

            @block.vector
            def _(dve):
                def store(t):
                    for kk in range(2):
                        n = 2 * t + kk
                        dve.wait_ge(turned, n + 1)
                        w = B if t == QT else P
                        dst = (xnT[:, 4 * kk:4 * kk + 4, t * P:t * P + w] if t < TT
                               else memT[:, 4 * kk:4 * kk + 4, (t - TT) * P:(t - TT + 1) * P])
                        src = ps[:, n % 4, :].rearrange("p (a q) -> p a q", a=4)[:, :, 0:w]
                        gain = gm[:, 0 if t < TT else 1, 4 * kk:4 * kk + 4]
                        nc.vector.tensor_tensor(dst, src, bc(gain, 2, w), ALU.mult).then_inc(stored, 1)

                dve.wait_ge(in_c, 48)
                for g, (lo, hi) in enumerate(groups):
                    dve.wait_ge(squared, hi)
                    nc.vector.tensor_scalar(rs[:, lo:hi], ss[:, lo:hi], 1.0 / D, EPS, ALU.mult,
                                            ALU.add).then_inc(meaned, 1)
                    dve.wait_ge(rooted, g + 1)
                    for t in range(lo, hi):
                        nc.vector.tensor_scalar(X[:, t, :], X[:, t, :], rs[:, t:t + 1], None,
                                                ALU.mult).then_inc(scaled, 1)
                        if t >= 2:
                            store(t - 2)
                store(NT - 2)
                store(NT - 1)

            @block.tensor
            def _(pe):
                pe.wait_ge(in_c, 48)
                n = 0
                for t in range(NT):
                    pe.wait_ge(scaled, t + 1)
                    for kk in range(2):
                        if n >= 4:
                            pe.wait_ge(stored, n - 3)
                        for a in range(4):
                            k = 4 * kk + a
                            ins = nc.tensor.transpose(ps[:, n % 4, a * P:(a + 1) * P],
                                                      X[:, t, k * P:(k + 1) * P], c("ident"))
                        ins.then_inc(turned, 1)
                        n += 1


def stage_ml_proj(M):
    nc, I, O, xnT, brT, ps, c = (M[k] for k in ("nc", "I", "O", "xnT", "brT", "ps", "c"))
    row = M["row"]
    uT, sigo, cT = brT[:, 0:4, :], brT[:, 4:8, :], brT[:, 8:12, :]
    NOUT = 8 * NB3
    with Stage(nc, "mlp") as st:
        xnR = M["xnR"]
        xh = st.sb("xh", [P, KT, T], FR)
        w, wl = st.pair("w", [P, 4, KT, P])
        wh = st.sb("wh", [P, 4, KT, P], FR)
        wif, wifl = st.pair("wif", [P, KT, 8])
        wifh = st.sb("wifh", [P, KT, 8], FR)
        sc = st.sb("state_conv", [24, 512])
        scT = st.sb("state_convT", [P, MH, B, 3])
        cw = st.sb("conv_w", [P, MH, 4])
        cb = st.sb("conv_b", [P, MH])
        bif = st.sb("b_if", [MH, 2])
        tail = st.sb("tail", [11, 512])
        sem = st.sem
        in_w, in_small, projected, kept, convolved, silued, st_turned, st_kept, tl_turned, tl_kept, out = (
            sem(n) for n in ("in_w", "in_small", "projected", "kept", "convolved", "silued", "st_turned",
                             "st_kept", "tl_turned", "tl_kept", "out"))
        chain = Chain(sem("conv_step"))
        out_pool = sem("out_pool")
        in_t = [sem(f"in_t{q}") for q in range(4)]
        x_high, x_low, w_high, w_low, restored = (sem(n) for n in ("x_high", "x_low", "w_high", "w_low", "restored"))
        tok = lambda b: slice(b * BLK, (b + 1) * BLK)
        wv = I["w_in"].rearrange("(k p) n -> p k n", p=P)
        with st.block() as block:
            @block.sync
            def _(sp):
                for j in range(8):
                    col = (C_U, C_O)[j // 4] + j % 4 * P
                    if j >= 4:
                        sp.wait_ge(projected, NB3 * (j - 3))
                    sp.dma_start(w[:, j % 4, :, :], wv[:, :, col:col + P]).then_inc(in_t[j % 4], 16)
                    if j == 3:
                        sp.dma_start(wif[:, :, :], wv[:, :, C_I:C_I + 8]).then_inc(in_w, 16)
                sp.wait_ge(tl_kept, 1)
                sp.dma_start(O["conv_prompt"].rearrange("o w n -> (o w) n"), tail[0:3, :]).then_inc(out, 16)
                sp.dma_start(O["conv_sample"][:, 2, :], tail[3:11, :]).then_inc(out, 16)
                sp.wait_ge(out, 32)

            @block.gpsimd
            def _(pool):
                pool.dma_start(sc[:, :], I["state_conv"].rearrange("b w n -> (b w) n")).then_inc(in_small, 16)
                for h in range(MH):
                    pool.dma_start(cw[:, h, :], I["conv_w"][:, h * MD:(h + 1) * MD].rearrange("w p -> p w"),
                                   allow_slow_non_contiguous=True).then_inc(in_small, 16)
                pool.dma_start(cb[:, :], I["conv_b"].rearrange("(h p) -> p h", p=P),
                               allow_slow_non_contiguous=True).then_inc(in_small, 16)
                pool.dma_start(bif[:, 0:1], I["b_igate"].rearrange("(h o) -> h o", o=1)).then_inc(in_small, 16)
                pool.dma_start(bif[:, 1:2], I["b_fgate"].rearrange("(h o) -> h o", o=1)).then_inc(in_small, 16)
                pool.dma_start(O["conv_sample"][:, 0:2, :], I["state_conv"][:, 1:3, :]).then_inc(out_pool, 16)
                pool.wait_ge(out_pool, 16)

            @block.tensor
            def _(pe):
                n = 0
                for j in range(8):
                    for b in range(NB3):
                        if n >= 6:
                            pe.wait_ge(kept, n - 5)
                        if b == 0:
                            pe.wait_ge(w_low, j + 1)
                        if j == 0:
                            pe.wait_ge(x_low, b + 1)
                        products(nc, ps[:, n % 6, 0:BLK],
                                 [((wh[:, j % 4, k, :], wl[:, j % 4, k, :]), (xh[:, k, tok(b)], xnR[:, k, tok(b)]))
                                  for k in range(KT)]).then_inc(projected, 1)
                        n += 1
                    if j == 4:
                        pe.wait_ge(in_small, 16 * 8)
                        for h in range(MH):
                            ins = nc.tensor.transpose(ps[:, 6, h * 24:(h + 1) * 24],
                                                      sc[:, h * P:(h + 1) * P], c("ident")[0:24, 0:24])
                        ins.then_inc(st_turned, 1)
                        pe.wait_ge(kept, 4 * NB3)
                        for h in range(MH):
                            ins = nc.tensor.transpose(ps[0:11, 7, h * P:(h + 1) * P],
                                                      uT[:, h, S - 3:T], c("ident"))
                        ins.then_inc(tl_turned, 1)
                pe.wait_ge(w_low, 9)
                for q in range(2):
                    for b in range(NB3):
                        pe.wait_ge(kept, n - 5)
                        cols = slice(q * MH, (q + 1) * MH)
                        products(nc, ps[0:MH, n % 6, 0:BLK],
                                 [((wifh[:, k, cols], wifl[:, k, cols]), (xh[:, k, tok(b)], xnR[:, k, tok(b)]))
                                  for k in range(KT)]).then_inc(projected, 1)
                        n += 1

            @block.scalar
            def _(act):
                def split_w(j):
                    act.wait_ge(in_t[j % 4], 16 * (j // 4 + 1))
                    high(nc, wh[:, j % 4, :, :], w[:, j % 4, :, :]).then_inc(w_high, 1)

                for b in range(NB3):
                    high(nc, xh[:, :, tok(b)], xnT[:, :, tok(b)]).then_inc(x_high, 1)
                    if b == 0:
                        split_w(0)
                n = 0
                for j in range(8):
                    if j < 3:
                        split_w(j + 1)
                    for b in range(NB3):
                        if b == 1 and 3 <= j < 7:
                            split_w(j + 1)
                        if b == 1 and j == 7:
                            act.wait_ge(in_w, 16)
                            high(nc, wifh[:, :, :], wif[:, :, :]).then_inc(w_high, 1)
                        act.wait_ge(projected, n + 1)
                        dst = (uT if j < 4 else sigo)[:, j % 4, b * BLK:(b + 1) * BLK]
                        nc.scalar.activation(dst, ps[:, n % 6, 0:BLK],
                                             ACT.Copy if j < 4 else ACT.Sigmoid).then_inc(kept, 1)
                        n += 1
                for q in range(2):
                    for b in range(NB3):
                        act.wait_ge(projected, n + 1)
                        nc.scalar.activation(row("ig" if q == 0 else "lf")[0:MH, b * BLK:(b + 1) * BLK],
                                             ps[0:MH, n % 6, 0:BLK], ACT.Identity,
                                             bias=bif[:, q:q + 1]).then_inc(kept, 1)
                        n += 1
                for h in range(MH):
                    act.wait_ge(convolved, h + 1)
                    nc.scalar.activation(cT[:, h, :], cT[:, h, :], ACT.Silu).then_inc(silued, 1)

            @block.vector
            def _(dve):
                def split_w(j):
                    dve.wait_ge(w_high, j + 1)
                    low(nc, wl[:, j % 4, :, :], w[:, j % 4, :, :], wh[:, j % 4, :, :]).then_inc(w_low, 1)

                for b in range(NB3):
                    dve.wait_ge(x_high, b + 1)
                    low(nc, xnR[:, :, tok(b)], xnT[:, :, tok(b)], xh[:, :, tok(b)]).then_inc(x_low, 1)
                    if b == 0:
                        split_w(0)
                for j in range(1, 5):
                    split_w(j)
                dve.wait_ge(st_turned, 1)
                nc.vector.tensor_copy(scT[:, :, :, :].rearrange("p h b w -> p (h b w)"),
                                      ps[:, 6, 0:MH * 24]).then_inc(st_kept, 1)
                dve.wait_ge(tl_turned, 1)
                nc.vector.tensor_copy(tail[:, :], ps[0:11, 7, :]).then_inc(tl_kept, 1)
                for j in range(5, 8):
                    split_w(j)
                dve.wait_ge(w_high, 9)
                low(nc, wifl[:, :, :], wif[:, :, :], wifh[:, :, :]).then_inc(w_low, 1)
                dve.wait_ge(in_small, 16 * 8)
                dve.wait_ge(st_kept, 1)
                for h in range(MH):
                    chain.link(dve, nc.vector.tensor_scalar(cT[:, h, :], uT[:, h, :], cw[:, h, 3:4],
                                                            cb[:, h:h + 1], ALU.mult, ALU.add))
                    for tap in range(3):
                        d = 3 - tap
                        chain.link(dve, nc.vector.scalar_tensor_tensor(
                            cT[:, h, d:S], uT[:, h, 0:S - d], cw[:, h, tap:tap + 1], cT[:, h, d:S],
                            ALU.mult, ALU.add))
                        ins = nc.vector.scalar_tensor_tensor(
                            cT[:, h, S:T], scT[:, h, :, tap], cw[:, h, tap:tap + 1], cT[:, h, S:T],
                            ALU.mult, ALU.add)
                        if tap < 2:
                            chain.link(dve, ins)
                    ins.then_inc(convolved, 1)
                for b in range(NB3):
                    dve.wait_ge(projected, 9 * NB3 + b + 1)
                    whole(nc, xnT[:, :, tok(b)], xnR[:, :, tok(b)], xh[:, :, tok(b)]).then_inc(restored, 1)


def stage_mlstm(M):
    nc, I, O, brT, ps, c = (M[k] for k in ("nc", "I", "O", "brT", "ps", "c"))
    row = M["row"]
    uT, sigo, cT = brT[:, 0:4, :], brT[:, 4:8, :], brT[:, 8:12, :]
    with Stage(nc, "ml") as st:
        qT = st.sb("qT", [P, MH, T])
        kT = st.sb("kT", [P, MH, T])
        ktm = brT[:, 0:4, 0:S].rearrange("p h (c e) -> p c h e", e=MD)
        va = st.sb("va", [P, NCK, MH, MD + 1])
        vs = st.sb("vs", [B, MH, MD])
        vsT = st.sb("vsT", [P, MH, B])
        bcs = st.sb("bcs", [P, 4, MH, B])
        tok = st.sb("tok", [P, NCK, 4, MH])
        m0 = st.sb("m0", [MH, B])
        gain = st.sb("gain", [P, MH])
        mS = st.sb("mS", [MH, B])
        with Stage(nc, "mlq") as s2:
            w3 = s2.sb("w3", [P, 3, MH, MD])
            tmp = row("tmp")[0:MH, :]
            dg = s2.sb("dg", [MH, 4, MH, B])
            sm = s2.sb("sm", [MH, 4, B])
            sem = s2.sem
            in_w, projected, kept, stepA, softened, rows_ready, exped, turned, tkept, diag, spread, in_m = (
                sem(n) for n in ("in_w", "projected", "kept", "stepA", "softened", "rows_ready", "exped",
                                 "turned", "tkept", "diag", "spread", "in_m"))
            chain = Chain(sem("gate_step"))
            out = sem("out")
            ones_set = sem("ones_set")
            with s2.block() as block:
                @block.sync
                def _(sp):
                    for i, n in enumerate(("w_ml_q", "w_ml_k", "w_ml_v")):
                        sp.dma_start(w3[:, i, :, :], I[n].rearrange("h d e -> d h e")).then_inc(in_w, 16)
                    sp.dma_start(m0[:, :], I["state_m"].rearrange("b h -> h b"),
                                 allow_slow_non_contiguous=True).then_inc(in_m, 16)
                    sp.dma_start(gain[:, :], I["ml_norm"].rearrange("h e -> e h"),
                                 allow_slow_non_contiguous=True).then_inc(in_m, 16)
                    sp.wait_ge(rows_ready, 1)
                    sp.dma_start(O["m_prompt"].rearrange("o h -> h o"), row("m")[0:MH, S - 1:S]).then_inc(out, 16)
                    sp.dma_start(O["m_sample"].rearrange("b h -> h b"), mS[:, :],
                                 allow_slow_non_contiguous=True).then_inc(out, 16)
                    sp.wait_ge(out, 32)

                @block.gpsimd
                def _(pool):
                    nc.gpsimd.memset(va[:, :, :, MD:MD + 1], 1.0).then_inc(ones_set, 1)
                    pool.wait_ge(ones_set, 1)

                @block.tensor
                def _(pe):
                    pe.wait_ge(in_w, 48)
                    n = 0
                    for h in range(MH):
                        for i in range(2):
                            for b in range(NB3):
                                if n >= 6:
                                    pe.wait_ge(kept, n - 5)
                                nc.tensor.matmul(ps[:, n % 6, 0:BLK], w3[:, i, h, :],
                                                 cT[:, h, b * BLK:(b + 1) * BLK],
                                                 start=True, stop=True).then_inc(projected, 1)
                                n += 1
                    for t in range(NCK):
                        pe.wait_ge(kept, n - 5)
                        for h in range(MH):
                            ins = nc.tensor.matmul(ps[:, n % 6, h * MD:(h + 1) * MD],
                                                   uT[:, h, t * L:(t + 1) * L], w3[:, 2, h, :],
                                                   start=True, stop=True)
                        ins.then_inc(projected, 1)
                        n += 1
                    pe.wait_ge(kept, n - 5)
                    for h in range(MH):
                        ins = nc.tensor.matmul(ps[0:B, n % 6, h * MD:(h + 1) * MD], uT[:, h, S:T],
                                               w3[:, 2, h, :], start=True, stop=True)
                    ins.then_inc(projected, 1)
                    n += 1
                    pe.wait_ge(kept, n - 5)
                    for h in range(MH):
                        ins = nc.tensor.matmul(ps[:, n % 6, h * B:(h + 1) * B], w3[:, 2, h, :], uT[:, h, S:T],
                                               start=True, stop=True)
                    ins.then_inc(projected, 1)
                    n += 1
                    for t in range(NCK):
                        pe.wait_ge(kept, n - 5)
                        for h in range(MH):
                            ins = nc.tensor.matmul(ps[:, n % 6, h * MD:(h + 1) * MD],
                                                   cT[:, h, t * L:(t + 1) * L], w3[:, 1, h, :],
                                                   start=True, stop=True)
                        ins.then_inc(projected, 1)
                        n += 1
                    pe.wait_ge(rows_ready, 2)
                    for t in range(NCK):
                        if t >= 1:
                            pe.wait_ge(tkept, t)
                        nc.tensor.transpose(ps[:, 6, 0:P], row("stack")[:, t * L:(t + 1) * L],
                                            c("ident")).then_inc(turned, 1)
                    pe.wait_ge(diag, 4)
                    nc.tensor.matmul(ps[:, 7, 0:P], c("ones")[0:MH, :],
                                     dg[:, :, :, :].rearrange("p a h b -> p (a h b)"),
                                     start=True, stop=True).then_inc(spread, 1)

                @block.scalar
                def _(act):
                    act.wait_ge(stepA, 1)
                    nc.scalar.activation(tmp[:, :], tmp[:, :], ACT.Exp, scale=-1.0).then_inc(softened, 1)
                    act.wait_ge(softened, 1)
                    nc.scalar.activation(tmp[:, :], tmp[:, :], ACT.Ln, bias=1.0).then_inc(softened, 1)
                    n = 0
                    for h in range(MH):
                        for i in range(2):
                            for b in range(NB3):
                                act.wait_ge(projected, n + 1)
                                nc.scalar.activation((qT if i == 0 else kT)[:, h, b * BLK:(b + 1) * BLK],
                                                     ps[:, n % 6, 0:BLK], ACT.Copy,
                                                     scale=MD ** -0.5 if i == 0 else 1.0).then_inc(kept, 1)
                                n += 1
                    for t in range(NCK):
                        act.wait_ge(projected, n + 1)
                        nc.scalar.activation(va[:, t, :, 0:MD], ps[:, n % 6, :].rearrange("p (h e) -> p h e", h=MH),
                                             ACT.Copy).then_inc(kept, 1)
                        n += 1
                    act.wait_ge(projected, n + 1)
                    nc.scalar.activation(vs[:, :, :].rearrange("p h e -> p (h e)"), ps[0:B, n % 6, :],
                                         ACT.Copy).then_inc(kept, 1)
                    n += 1
                    act.wait_ge(projected, n + 1)
                    nc.scalar.activation(vsT[:, :, :].rearrange("p h e -> p (h e)"), ps[:, n % 6, 0:MH * B],
                                         ACT.Copy).then_inc(kept, 1)
                    n += 1
                    for t in range(NCK):
                        act.wait_ge(projected, n + 1)
                        nc.scalar.activation(ktm[:, t, :, :], ps[:, n % 6, :].rearrange("p (h e) -> p h e", h=MH),
                                             ACT.Copy).then_inc(kept, 1)
                        n += 1
                    act.wait_ge(rows_ready, 1)
                    for q in (32, 64, 96):
                        nc.scalar.activation(row("stack")[q:q + MH, 0:S], row("stack")[q:q + MH, 0:S],
                                             ACT.Exp, scale=(-1.0 if q == 96 else 1.0)).then_inc(exped, 1)
                    nc.scalar.activation(sm[:, :, :], sm[:, :, :], ACT.Exp).then_inc(exped, 1)

                @block.vector
                def _(dve):
                    lf, ig, mm, mr, bb, rst = (row(x) for x in ("lf", "ig", "M", "m", "b", "reset"))
                    nc.vector.scalar_tensor_tensor(tmp[:, :], lf[0:MH, :], -1.0, lf[0:MH, :], ALU.mult, ALU.max).then_inc(stepA, 1)
                    chain.link(dve, nc.vector.memset(row("stack")[:, 0:S], 0.0))
                    chain.link(dve, nc.vector.memset(rst[0:MH, 0:S], 1.0))
                    chain.link(dve, nc.vector.memset(
                        rst[0:MH, 0:S].rearrange("p (c l) -> p c l", l=L)[:, :, 0:1], 0.0))
                    chain.link(dve, nc.vector.tensor_scalar(lf[0:MH, :], lf[0:MH, :], 0.0, None, ALU.min))
                    dve.wait_ge(softened, 2)
                    chain.link(dve, nc.vector.tensor_tensor(lf[0:MH, :], lf[0:MH, :], tmp[:, :], ALU.subtract))
                    chain.link(dve, nc.vector.tensor_tensor_scan(bb[0:MH, 0:S], rst[0:MH, 0:S], lf[0:MH, 0:S],
                                                                 0.0, ALU.mult, ALU.add))
                    chain.link(dve, nc.vector.tensor_tensor_scan(mr[0:MH, 0:S], lf[0:MH, 0:S], ig[0:MH, 0:S],
                                                                 0.0, ALU.add, ALU.max))
                    chain.link(dve, nc.vector.tensor_tensor(mm[0:MH, 0:S], mr[0:MH, 0:S], bb[0:MH, 0:S],
                                                            ALU.subtract))
                    stack = row("stack")
                    chain.link(dve, nc.vector.tensor_tensor(stack[0:MH, 0:S], ig[0:MH, 0:S], bb[0:MH, 0:S],
                                                            ALU.subtract))
                    chain.link(dve, nc.vector.tensor_copy(stack[96:96 + MH, 0:S], mr[0:MH, 0:S]))
                    ch = lambda r, p0: r[p0:p0 + MH, 0:S].rearrange("p (c l) -> p c l", l=L)
                    chain.link(dve, nc.vector.tensor_scalar(stack[32:32 + MH, 0:L], mm[0:MH, 0:L], -1.0, None,
                                                            ALU.mult))
                    chain.link(dve, nc.vector.tensor_tensor(
                        ch(stack, 32)[:, 1:, :], ch(mr, 0)[:, 0:NCK - 1, L - 1:L].to_broadcast([MH, NCK - 1, L]),
                        ch(mm, 0)[:, 1:, :], ALU.subtract))
                    chain.link(dve, nc.vector.tensor_tensor(
                        ch(stack, 64), ch(stack, 0), ch(mm, 0)[:, :, L - 1:L].to_broadcast([MH, NCK, L]),
                        ALU.subtract))
                    chain.link(dve, nc.vector.tensor_scalar(sm[:, 0, 0:1], mm[0:MH, L - 1:L], -1.0, None,
                                                            ALU.mult))
                    chain.link(dve, nc.vector.tensor_tensor(
                        sm[:, 0, 1:NCK], ch(mr, 0)[:, 0:NCK - 1, L - 1], ch(mm, 0)[:, 1:, L - 1], ALU.subtract))
                    dve.wait_ge(in_m, 32)
                    chain.link(dve, nc.vector.tensor_tensor(sm[:, 1, :], lf[0:MH, S:T], m0[:, :], ALU.add))
                    chain.link(dve, nc.vector.tensor_tensor(mS[:, :], sm[:, 1, :], ig[0:MH, S:T], ALU.max))
                    chain.link(dve, nc.vector.tensor_tensor(sm[:, 1, :], sm[:, 1, :], mS[:, :], ALU.subtract))
                    chain.link(dve, nc.vector.tensor_tensor(sm[:, 2, :], ig[0:MH, S:T], mS[:, :], ALU.subtract))
                    nc.vector.tensor_scalar(sm[:, 3, :], mS[:, :], -1.0, None, ALU.mult).then_inc(rows_ready, 1)
                    dve.wait_ge(exped, 4)
                    for a in range(4):
                        ins = nc.vector.tensor_tensor(dg[:, a, :, :], bc(sm[:, a, :], 1, MH),
                                                      bc(c("ident")[0:MH, 0:MH], 2, B), ALU.mult)
                        ins.then_inc(diag, 1)
                    nc.vector.memset(tmp[:, 0:1], 0.0).then_inc(rows_ready, 1)
                    for t in range(NCK):
                        dve.wait_ge(turned, t + 1)
                        nc.vector.tensor_copy(tok[:, t, :, :],
                                              ps[:, 6, 0:P].rearrange("p (a q) -> p a q", a=4)[:, :, 0:MH]
                                              ).then_inc(tkept, 1)
                    dve.wait_ge(spread, 1)
                    chain.link(dve, nc.vector.tensor_copy(
                        bcs[:, :, :, :].rearrange("p a h b -> p (a h b)"), ps[:, 7, 0:P]))
        mlstm_chunks(M, st, qT, kT, ktm, va, bcs, tok, gain)
        mlstm_sample(M, st, qT, kT, vs, vsT, bcs, gain)


def mlstm_chunks(M, st, qT, kT, ktm, va, bcs, tok, gain):
    nc, I, O, brT, ps, c = (M[k] for k in ("nc", "I", "O", "brT", "ps", "c"))
    row = M["row"]
    sigo, Htm = brT[:, 4:8, 0:S], brT[:, 8:12, 0:S].rearrange("p h (c e) -> p h c e", e=MD)
    N = NCK * MH
    with Stage(nc, "mlc") as s2:
        ca = s2.sb("state", [P, MH, MD + 1])
        selm = s2.sb("selm", [MH, MH, P])
        mb = s2.sb("mb", [P, 2, L])
        wgt = s2.sb("wgt", [P, 2, L])
        wT = s2.sb("wT", [P, 2, L])
        kw = s2.sb("kw", [P, 2, MD])
        inter = s2.sb("inter", [P, 2, MD + 1])
        num = s2.sb("num", [P, 2, MD + 1])
        den = s2.sb("den", [P, 2, 1])
        ss = s2.sb("ss", [P, MH, NCK])
        junk = s2.sb("junk", [P, MD])
        sem = s2.sem
        (prep, scored, masked, weighed, wready, kready, read, done_pe, interk, hdone, stated, squared, meaned,
         rooted, normed, turned, gated, out) = (
            sem(n) for n in ("prep", "scored", "masked", "weighed", "wready", "kready", "read", "done_pe",
                             "interk", "hdone", "stated", "squared", "meaned", "rooted", "normed", "turned",
                             "gated", "out"))
        chain = Chain(sem("step"))
        with s2.block() as block:
            @block.tensor
            def _(pe):
                pe.wait_ge(prep, 1)

                def first(n):
                    t, h = n // MH, n % MH
                    if n >= 2:
                        pe.wait_ge(wready, n - 1)
                    nc.tensor.matmul(ps[:, n % 2, 0:L], selm[:, h, :], row("M")[0:MH, t * L:(t + 1) * L],
                                     start=True, stop=True)
                    nc.tensor.matmul(ps[:, n % 2, L:2 * L], kT[:, h, t * L:(t + 1) * L],
                                     qT[:, h, t * L:(t + 1) * L], start=True, stop=True).then_inc(scored, 1)

                def second(n):
                    t, h = n // MH, n % MH
                    if n >= 2:
                        pe.wait_ge(hdone, n - 1)
                        pe.wait_ge(interk, n - 1)
                        pe.wait_ge(stated, n - 1)
                    b = 2 + n % 2
                    pe.wait_ge(stated, max(n - MH + 1, 0) + 1)
                    nc.tensor.matmul(ps[:, b, 0:MD + 1], qT[:, h, t * L:(t + 1) * L], ca[:, h, :],
                                     start=True, stop=True).then_inc(read, 1)
                    pe.wait_ge(wready, n + 1)
                    nc.tensor.matmul(ps[:, b + 2, 0:MD + 1], wT[:, n % 2, :], va[:, t, h, :],
                                     start=True, stop=True)
                    pe.wait_ge(kready, n + 1)
                    nc.tensor.matmul(ps[:, b + 4, 0:MD + 1], kw[:, n % 2, :], va[:, t, h, :],
                                     start=True, stop=True).then_inc(done_pe, 1)

                first(0)
                for n in range(N):
                    if n + 1 < N:
                        first(n + 1)
                    second(n)
                for h in range(MH):
                    for half in range(2):
                        n = 2 * h + half
                        pe.wait_ge(normed, h + 1)
                        if n >= 2:
                            pe.wait_ge(gated, n - 1)
                        for a in range(4):
                            ins = nc.tensor.transpose(ps[:, n % 2, a * P:(a + 1) * P],
                                                      Htm[:, h, 4 * half + a, :], c("ident"))
                        ins.then_inc(turned, 1)

            @block.gpsimd
            def _(pool):
                for n in range(N):
                    t, h = n // MH, n % MH
                    if n >= 2:
                        pool.wait_ge(done_pe, n - 1)
                    nc.gpsimd.tensor_scalar(kw[:, n % 2, :], ktm[:, t, h, :], tok[:, t, 2, h:h + 1], None,
                                            ALU.mult).then_inc(kready, 1)
                pool.wait_ge(meaned, 1)
                nc.gpsimd.tensor_tensor(ss[:, :, :], ss[:, :, :],
                                        bc(c("mhalf").to_broadcast([P, NCK]), 1, MH), ALU.pow).then_inc(rooted, 1)

            @block.scalar
            def _(act):
                def square(n):
                    t, h = n // MH, n % MH
                    act.wait_ge(hdone, n + 1)
                    if n:
                        act.wait_ge(squared, n)
                    nc.scalar.activation(junk[:, :], Htm[:, h, t, :], ACT.Square,
                                         accum_out=ss[:, h, t:t + 1]).then_inc(squared, 1)

                for n in range(N):
                    t, h = n // MH, n % MH
                    act.wait_ge(masked, n + 1)
                    if n >= 2:
                        act.wait_ge(wready, n - 1)
                    nc.scalar.activation(wgt[:, n % 2, :], mb[:, n % 2, :], ACT.Exp, scale=-1.0,
                                         bias=tok[:, t, 0, h:h + 1]).then_inc(weighed, 1)
                    act.wait_ge(read, n + 1)
                    if n >= 2:
                        act.wait_ge(hdone, n - 1)
                    nc.scalar.activation(inter[:, n % 2, :], ps[:, 2 + n % 2, 0:MD + 1], ACT.Copy,
                                         scale=tok[:, t, 1, h:h + 1]).then_inc(interk, 1)
                    if n >= 2:
                        square(n - 2)
                square(N - 2)
                square(N - 1)

            @block.vector
            def _(dve):
                chain.link(dve, nc.vector.tensor_copy(selm[:, :, :],
                                                      bc(c("ident")[0:MH, 0:MH], 2, P)))
                nc.vector.memset(ca[:, :, :], 0.0).then_inc(stated, 1)
                nc.vector.memset(junk[:, :], 0.0).then_inc(prep, 1)
                dve.wait_ge(prep, 1)

                def mask(n):
                    dve.wait_ge(scored, n + 1)
                    if n >= 2:
                        dve.wait_ge(weighed, n - 1)
                    nc.vector.tensor_tensor(mb[:, n % 2, :], ps[:, n % 2, 0:L], c("future"),
                                            ALU.add).then_inc(masked, 1)

                mask(0)
                for n in range(N):
                    t, h = n // MH, n % MH
                    i = n % 2
                    dve.wait_ge(weighed, n + 1)
                    if n >= 2:
                        dve.wait_ge(done_pe, n - 1)
                    nc.vector.tensor_tensor(wT[:, i, :], wgt[:, i, :], ps[:, i, L:2 * L],
                                            ALU.mult).then_inc(wready, 1)
                    if n + 1 < N:
                        mask(n + 1)
                    dve.wait_ge(done_pe, n + 1)
                    dve.wait_ge(interk, n + 1)
                    chain.link(dve, nc.vector.tensor_tensor(num[:, i, :], ps[:, 4 + i, 0:MD + 1],
                                                            inter[:, i, :], ALU.add))
                    nc.vector.scalar_tensor_tensor(ca[:, h, :], ca[:, h, :], bcs[:, 0, h, t:t + 1],
                                                   ps[:, 6 + i, 0:MD + 1], ALU.mult, ALU.add).then_inc(stated, 1)
                    chain.link(dve, nc.vector.tensor_scalar(den[:, i, :], num[:, i, MD:MD + 1], -1.0,
                                                            tok[:, t, 3, h:h + 1], ALU.mult, ALU.max))
                    chain.link(dve, nc.vector.tensor_scalar(den[:, i, :], num[:, i, MD:MD + 1], den[:, i, :],
                                                            None, ALU.max))
                    chain.link(dve, nc.vector.reciprocal(den[:, i, :], den[:, i, :]))
                    nc.vector.tensor_scalar(Htm[:, h, t, :], num[:, i, 0:MD], den[:, i, :], None,
                                            ALU.mult).then_inc(hdone, 1)
                dve.wait_ge(squared, N)
                nc.vector.tensor_scalar(ss[:, :, :], ss[:, :, :], 1.0 / MD, EPS, ALU.mult,
                                        ALU.add).then_inc(meaned, 1)
                dve.wait_ge(rooted, 1)
                for h in range(MH):
                    nc.vector.tensor_tensor(Htm[:, h, :, :], Htm[:, h, :, :], bc(ss[:, h, :], 2, MD),
                                            ALU.mult).then_inc(normed, 1)
                for n in range(2 * MH):
                    h, half = n // 2, n % 2
                    dve.wait_ge(turned, n + 1)
                    dst = sigo[:, h, half * 512:(half + 1) * 512]
                    nc.vector.scalar_tensor_tensor(dst, ps[:, n % 2, :], gain[:, h:h + 1], dst,
                                                   ALU.mult, ALU.mult).then_inc(gated, 1)

            @block.sync
            def _(sp):
                sp.wait_ge(stated, N + 1)
                sp.dma_start(O["C_prompt"].rearrange("o h d e -> d (o h) e"), ca[:, :, 0:MD]).then_inc(out, 16)
                sp.dma_start(O["n_prompt"].rearrange("o h d -> d (o h)"), ca[:, :, MD],
                             allow_slow_non_contiguous=True).then_inc(out, 16)
                sp.wait_ge(out, 32)


def mlstm_sample(M, st, qT, kT, vs, vsT, bcs, gain):
    nc, I, O, brT, ps, c = (M[k] for k in ("nc", "I", "O", "brT", "ps", "c"))
    sigo = brT[:, 4:8, S:T]
    HB = MH * B
    with Stage(nc, "mls") as s2:
        C0 = s2.sb("C0", [P, 4, MH, MD])
        C1 = s2.sb("C1", [P, 4, MH, MD])
        n0 = s2.sb("n0", [HB, MD])
        nT = s2.sb("nT", [P, MH, B])
        sel = s2.sb("sel", [B, B, P])
        pr = s2.sb("pr", [P, 2, HB])
        kwt = s2.sb("kwt", [P, MH, B])
        hT = s2.sb("hT", [P, MH, B])
        t1 = s2.sb("t1", [P, MH, B])
        t2 = s2.sb("t2", [P, MH, B])
        nout = s2.sb("nout", [HB, MD])
        sem = s2.sem
        n_in, selr, nturn, nk, prods, dots, fed, spreadv, updated, stored, sq, ssum, pooled, rooted, nn, nkept, out, oth = (
            sem(n) for n in ("n_in", "selr", "nturn", "nk", "prods", "dots", "fed", "spreadv",
                             "updated", "stored", "sq", "ssum", "pooled", "rooted", "nn", "nkept", "out", "oth"))
        chain = Chain(sem("step"))
        c_in, cout = ([sem(f"{n}{q}") for q in range(4)] for n in ("c_in", "cout"))
        qs, ks = qT[:, :, S:T], kT[:, :, S:T]
        with s2.block() as block:
            @block.sync
            def _(sp):
                for h in range(MH):
                    sp.dma_start(n0[h * B:(h + 1) * B, :], I["state_n"][:, h, :]).then_inc(n_in, 16)
                for b in range(B):
                    if b >= 4:
                        sp.wait_ge(updated, b - 3)
                        sp.wait_ge(fed, b - 3)
                    sp.dma_start(C0[:, b % 4, :, :], I["state_C"][b].rearrange("h d e -> d h e")).then_inc(c_in[b % 4], 16)
                sp.wait_ge(nkept, 1)
                for h in range(MH):
                    sp.dma_start(O["n_sample"][:, h, :], nout[h * B:(h + 1) * B, :]).then_inc(out, 16)
                sp.wait_ge(out, 64)

            @block.gpsimd
            def _(pool):
                for b in range(B):
                    pool.wait_ge(updated, b + 1)
                    pool.dma_start(O["C_sample"][b].rearrange("h d e -> d h e"), C1[:, b % 4, :, :]).then_inc(cout[b % 4], 16)
                pool.wait_ge(pooled, 1)
                nc.gpsimd.tensor_tensor(t2[:, :, :], t2[:, :, :], bc(c("mhalf").to_broadcast([P, B]), 1, MH),
                                        ALU.pow).then_inc(rooted, 1)
                for q in range(4):
                    pool.wait_ge(cout[q], 16 * B // 4)

            @block.tensor
            def _(pe):
                pe.wait_ge(n_in, 64)
                nc.tensor.transpose(ps[:, 0, 0:HB], n0[:, :], c("ident")[0:HB, 0:HB]).then_inc(nturn, 1)
                pe.wait_ge(prods, 1)
                nc.tensor.matmul(ps[:, 1, 0:2 * HB], c("ones"), pr[:, :, :].rearrange("p a q -> p (a q)"),
                                 start=True, stop=True).then_inc(dots, 1)
                pe.wait_ge(selr, 1)
                for b in range(B):
                    pe.wait_ge(c_in[b % 4], 16 * (b // 4 + 1))
                    for h in range(MH):
                        ins = nc.tensor.matmul(ps[:, 2, h * B + b:h * B + b + 1], C0[:, b % 4, h, :],
                                               qT[:, h, S + b:S + b + 1], start=True, stop=True)
                    ins.then_inc(fed, 1)
                    if b >= 2:
                        pe.wait_ge(updated, b - 1)
                    nc.tensor.matmul(ps[:, 4 + b % 2, :], sel[:, b, :], vs[:, :, :].rearrange("p h e -> p (h e)"),
                                     start=True, stop=True).then_inc(spreadv, 1)
                pe.wait_ge(sq, 1)
                nc.tensor.matmul(ps[:, 3, 0:HB], c("ones"), t1[:, :, :].rearrange("p h b -> p (h b)"),
                                 start=True, stop=True).then_inc(ssum, 1)
                pe.wait_ge(nn, 1)
                nc.tensor.transpose(ps[0:HB, 6, 0:P], nT[:, :, :].rearrange("p h b -> p (h b)"),
                                    c("ident")).then_inc(oth, 1)

            @block.vector
            def _(dve):
                P1 = lambda x: x.rearrange("p (h b) -> p h b", h=MH)
                chain.link(dve, nc.vector.tensor_copy(sel[:, :, :], bc(c("ident")[0:B, 0:B], 2, P)))
                nc.vector.tensor_tensor(kwt[:, :, :], ks, bcs[:, 2, :, :], ALU.mult).then_inc(selr, 1)
                dve.wait_ge(selr, 1)
                dve.wait_ge(nturn, 1)
                chain.link(dve, nc.vector.tensor_copy(nT[:, :, :], P1(ps[:, 0, 0:HB])))
                chain.link(dve, nc.vector.tensor_tensor(P1(pr[:, 0, :]), qs, nT[:, :, :], ALU.mult))
                nc.vector.tensor_tensor(P1(pr[:, 1, :]), qs, ks, ALU.mult).then_inc(prods, 1)
                chain.link(dve, nc.vector.tensor_tensor(nT[:, :, :], nT[:, :, :], bcs[:, 1, :, :], ALU.mult))
                nc.vector.tensor_tensor(nT[:, :, :], nT[:, :, :], kwt[:, :, :], ALU.add).then_inc(nn, 1)
                for b in range(B):
                    dve.wait_ge(c_in[b % 4], 16 * (b // 4 + 1))
                    dve.wait_ge(spreadv, b + 1)
                    if b >= 4:
                        dve.wait_ge(cout[b % 4], 16 * (b // 4))
                    for h in range(MH):
                        ins = nc.vector.tensor_scalar(C1[:, b % 4, h, :], ps[:, 4 + b % 2, h * MD:(h + 1) * MD],
                                                      kwt[:, h, b:b + 1], None, ALU.mult)
                    chain.link(dve, ins)
                    for h in range(MH):
                        ins = nc.vector.scalar_tensor_tensor(C1[:, b % 4, h, :], C0[:, b % 4, h, :],
                                                             bcs[:, 1, h, b:b + 1], C1[:, b % 4, h, :],
                                                             ALU.mult, ALU.add)
                    ins.then_inc(updated, 1)
                dve.wait_ge(dots, 1)
                dve.wait_ge(fed, B)
                chain.link(dve, nc.vector.tensor_tensor(t1[:, :, :], P1(ps[:, 1, HB:2 * HB]), bcs[:, 2, :, :],
                                                        ALU.mult))
                chain.link(dve, nc.vector.tensor_tensor(hT[:, :, :], vsT[:, :, :], t1[:, :, :], ALU.mult))
                chain.link(dve, nc.vector.tensor_tensor(t2[:, :, :], P1(ps[:, 2, 0:HB]), bcs[:, 1, :, :],
                                                        ALU.mult))
                chain.link(dve, nc.vector.tensor_tensor(hT[:, :, :], hT[:, :, :], t2[:, :, :], ALU.add))
                chain.link(dve, nc.vector.tensor_tensor(t2[:, :, :], P1(ps[:, 1, 0:HB]), bcs[:, 1, :, :],
                                                        ALU.mult))
                chain.link(dve, nc.vector.tensor_tensor(t2[:, :, :], t2[:, :, :], t1[:, :, :], ALU.add))
                chain.link(dve, nc.vector.scalar_tensor_tensor(t2[:, :, :], t2[:, :, :], -1.0, t2[:, :, :],
                                                               ALU.mult, ALU.max))
                chain.link(dve, nc.vector.tensor_tensor(t2[:, :, :], t2[:, :, :], bcs[:, 3, :, :], ALU.max))
                chain.link(dve, nc.vector.reciprocal(t2[:, :, :], t2[:, :, :]))
                chain.link(dve, nc.vector.tensor_tensor(hT[:, :, :], hT[:, :, :], t2[:, :, :], ALU.mult))
                nc.vector.tensor_tensor(t1[:, :, :], hT[:, :, :], hT[:, :, :], ALU.mult).then_inc(sq, 1)
                dve.wait_ge(ssum, 1)
                nc.vector.tensor_scalar(t2[:, :, :], P1(ps[:, 3, 0:HB]), 1.0 / MD, EPS, ALU.mult,
                                        ALU.add).then_inc(pooled, 1)
                dve.wait_ge(rooted, 1)
                chain.link(dve, nc.vector.tensor_tensor(hT[:, :, :], hT[:, :, :], t2[:, :, :], ALU.mult))
                chain.link(dve, nc.vector.tensor_tensor(hT[:, :, :], hT[:, :, :], bc(gain[:, :], 2, B), ALU.mult))
                chain.link(dve, nc.vector.tensor_tensor(sigo, sigo, hT[:, :, :], ALU.mult))
                dve.wait_ge(oth, 1)
                nc.vector.tensor_copy(nout[:, :], ps[0:HB, 6, 0:P]).then_inc(nkept, 1)


def stage_tok_proj(M, A):
    nc, I, O, xnT, brT, x2, ps, memT = (M[k] for k in ("nc", "I", "O", "xnT", "brT", "x2", "ps", "memT"))
    wv = I["w_in"].rearrange("(k p) n -> p k n", p=P)
    mv = I["w_mem_kv"].rearrange("(k p) n -> p k n", p=P)
    groups = [(wv, C_Q + o, 256, A["q"], o) for o in (0, 256)]
    groups += [(wv, C_G, 280, A["gk"], 0)]
    groups += [(wv, C_KVS + o, 256, A["kvsw"], o) for o in (0, 256)]
    groups += [(wv, C_MQ + o, 256, A["mq"], o) for o in (0, 256)]
    NX = len(groups)
    groups += [(mv, o, 256, A["kvm"], o) for o in (0, 256, 512, 768)]
    NGR = len(groups)
    xnR, brR, memR = M["xnR"], M["brR"], M["memR"]
    flats = [x[:, :, :].rearrange("p t d -> p (t d)") for x in (x2, M["x2R"])]
    half = TT * D // 4

    def weights(g, part):
        n = groups[g][2]
        at = (2 * (g % 2) + (part == "hi")) * half
        return flats[part != "raw"][:, at:at + KT * n].rearrange("p (k n) -> p k n", k=KT)

    with Stage(nc, "tok") as st:
        memh = st.sb("memh", [P, KT, XT], FR)
        junk = st.sb("junk", [P, 4, P])
        ss = A["ss"]

        def normed_heads(g, t):
            if g < 2:
                return [(j * HD, HD, t * H + 4 * g + j) for j in range(4)]
            if g in (3, 4):
                return [(j * 2 * HD, HD, 72 + t * 4 + 2 * (g - 3) + j) for j in range(2)]
            if g in (5, 6):
                return [(j * XD, XD, 108 + t * XH + 2 * (g - 5) + j) for j in range(2)]
            if g >= NX:
                return [(0, XD, 144 + t * XH + g - NX)]
            return []

        xh = lambda k: brR[:, k, :] if k < 4 else brR[:, 4 + k, :]
        sem = st.sem
        in_w = [sem(f"in_w{q}") for q in range(2)]
        projected, kept, cleared, x_high, x_low, m_high, m_low, w_high, w_low, restored, moved, squared = (
            sem(n) for n in ("projected", "kept", "cleared", "x_high", "x_low", "m_high", "m_low", "w_high",
                             "w_low", "restored", "moved", "squared"))
        steps = [(g, t) for g in range(NGR) for t in (range(TT) if g < NX else range(2))]
        first = {g: min(n for n, s in enumerate(steps) if s[0] == g) for g in range(NGR)}
        last = {g: max(n for n, s in enumerate(steps) if s[0] == g) for g in range(NGR)}
        with st.block() as block:
            @block.sync
            def _(sp):
                for g, (w, col, n, _, _) in enumerate(groups):
                    if g >= 2:
                        sp.wait_ge(projected, last[g - 2] + 1)
                    sp.dma_start(weights(g, "raw"), w[:, :, col:col + n]).then_inc(in_w[g % 2], 16)
                    if g == 2:
                        sp.dma_start(O["win_sample"][:, 0:WIN - 1].rearrange("b w g c d -> b w (g c d)"),
                                     I["cache_kv_win"][:, 1:WIN].rearrange("b w g c d -> b w (g c d)")
                                     ).then_inc(moved, 16)
                sp.wait_ge(moved, 16)

            @block.gpsimd
            def _(pool):
                for a in ("q", "gk", "kvsw", "mq"):
                    nc.gpsimd.memset(A[a][:, QT, :], 0.0).then_inc(cleared, 1)
                nc.gpsimd.memset(ss[:, :], 1.0).then_inc(cleared, 1)

            @block.tensor
            def _(pe):
                for n, (g, t) in enumerate(steps):
                    if n >= 6:
                        pe.wait_ge(kept, n - 5)
                    if t == 0:
                        pe.wait_ge(w_low, g + 1)
                    if g == 0 and t % 4 == 0:
                        pe.wait_ge(x_low, 2 * min(t // 4 + 1, 2) if t < QT else 6)
                    if g == NX and t == 0:
                        pe.wait_ge(m_low, 1)
                    m = B if t == QT else P
                    w = groups[g][2]
                    rows = slice(t * P, t * P + m)
                    x = (lambda k: (xh(k)[:, rows], xnR[:, k, rows])) if g < NX else (
                        lambda k: (memh[:, k, rows], memR[:, k, rows]))
                    products(nc, ps[0:m, n % 6, 0:w],
                             [(x(k), (weights(g, "hi")[:, k, :], weights(g, "lo")[:, k, :])) for k in range(KT)]
                             ).then_inc(projected, 1)

            def spans():
                for lo, hi in ((0, 512), (512, 1024), (1024, T)):
                    for k in (0, 4):
                        yield slice(lo, hi), slice(k, k + 4), slice(k if k == 0 else 8, (k if k == 0 else 8) + 4)

            @block.scalar
            def _(act):
                def split_w(g):
                    act.wait_ge(in_w[g % 2], 16 * (g // 2 + 1))
                    high(nc, weights(g, "hi"), weights(g, "raw")).then_inc(w_high, 1)

                for i, (tok, ks, kb) in enumerate(spans()):
                    high(nc, brR[:, kb, tok], xnT[:, ks, tok]).then_inc(x_high, 1)
                    if i == 1:
                        split_w(0)
                high(nc, memh[:, :, :], memT[:, :, :]).then_inc(m_high, 1)
                split_w(1)
                act.wait_ge(cleared, 5)
                sq = 0
                for n, (g, t) in enumerate(steps):
                    act.wait_ge(projected, n + 1)
                    m = B if t == QT else P
                    for col, width, i in normed_heads(g, t):
                        if sq >= 4:
                            act.wait_ge(squared, sq - 3)
                        nc.scalar.activation(junk[0:m, sq % 4, 0:width], ps[0:m, n % 6, col:col + width], ACT.Square,
                                             accum_out=ss[0:m, i:i + 1]).then_inc(squared, 1)
                        sq += 1
                    w, dst, o = groups[g][2:]
                    if dst is A["kvm"] and n == first[NX]:
                        act.wait_ge(restored, 1)
                    nc.scalar.activation(dst[0:m, t, o:o + w], ps[0:m, n % 6, 0:w], ACT.Copy).then_inc(kept, 1)
                    if t == 1 and 1 <= g < NGR - 1:
                        split_w(g + 1)

            @block.vector
            def _(dve):
                def split_w(g):
                    dve.wait_ge(w_high, g + 1)
                    low(nc, weights(g, "lo"), weights(g, "raw"), weights(g, "hi")).then_inc(w_low, 1)

                for i, (tok, ks, kb) in enumerate(spans()):
                    dve.wait_ge(x_high, i + 1)
                    low(nc, xnR[:, ks, tok], xnT[:, ks, tok], brR[:, kb, tok]).then_inc(x_low, 1)
                    if i == 1:
                        split_w(0)
                dve.wait_ge(m_high, 1)
                low(nc, memR[:, :, :], memT[:, :, :], memh[:, :, :]).then_inc(m_low, 1)
                for g in range(1, NX + 1):
                    split_w(g)
                dve.wait_ge(projected, last[NX - 1] + 1)
                for ks, kb in ((slice(0, 4), slice(0, 4)), (slice(4, 8), slice(8, 12))):
                    ins = whole(nc, xnT[:, ks, :], xnR[:, ks, :], brR[:, kb, :])
                ins.then_inc(restored, 1)
                for g in range(NX + 1, NGR):
                    split_w(g)


def stage_prep(M, A):
    nc, I, O, x2, ps, c = (M[k] for k in ("nc", "I", "O", "x2", "ps", "c"))
    q, gk, kvsw, mq, kvm, qr = (A[k] for k in ("q", "gk", "kvsw", "mq", "kvm", "qr"))
    q4 = q[:, :, :].rearrange("p t (h d) -> p t h d", d=HD)
    kv5 = kvsw[:, :, :].rearrange("p t (r c d) -> p t r c d", c=2, d=HD)
    mq4 = mq[:, :, :].rearrange("p t (h d) -> p t h d", d=XD)
    km4 = kvm[:, :, :].rearrange("p t (h c d) -> p t h c d", c=2, d=XD)
    qr4 = qr[:, :, :].rearrange("p t (h d) -> p t h d", d=HD)
    norms = [(q4, H, HD, TT), (kv5[:, :, :, 0, :], 4, HD, TT), (mq4, XH, XD, TT), (km4[:, :, :, 0, :], XH, XD, 2)]
    at = [0, 72, 108, 144, 152]
    with Stage(nc, "prep") as st:
        ss = A["ss"]
        r0 = st.sb("r0", [P, 152])
        r1 = st.sb("r1", [P, 152])
        gq, gs, gw = (st.sb(n, [P, HD]) for n in ("g_q", "g_slc", "g_win"))
        gmq, gmk = (st.sb(n, [P, XD]) for n in ("g_mq", "g_mk"))
        t1 = st.sb("t1", [P, TT, H, HALF])
        t2 = st.sb("t2", [P, TT, H, HALF])
        sem = st.sem
        sqrted, mscaled, in_g, meaned, rooted, qready, qcopied, kready, mready, out, gated = (
            sem(n) for n in ("sqrted", "mscaled", "in_g", "meaned", "rooted", "qready", "qcopied", "kready",
                             "mready", "out", "gated"))
        chain = Chain(sem("step"))
        mchain = Chain(sem("mem_step"))
        A["prep_out"] = out
        w1 = M["brT"][:, 8:12, :].rearrange("p a t -> p (a t)")[:, 0:2 * 16 * CH].rearrange(
            "p (c r h) -> p c r h", c=2, r=16)
        pe_ = st.sb("pe", [P, 2, 16])
        b1 = st.sb("b1", [P, 2])
        bias = M["bias"]
        in_w, biased = sem("in_w"), sem("biased")

        with st.block() as block:
            @block.sync
            def _(sp):
                for dst, n in ((gq, "q_norm"), (gs, "k_norm_slc"), (gw, "k_norm_win"), (gmq, "mem_q_norm"),
                               (gmk, "mem_k_norm")):
                    sp.dma_start(dst[:, :], I[n].partition_broadcast(P)).then_inc(in_g, 16)
                for cc in range(2):
                    sp.dma_start(w1[:, cc, :, :],
                                 I["cmp_w1"][cc].rearrange("(r q) h -> q r h", q=P)).then_inc(in_w, 16)
                rows = I["cmp_pe"].rearrange("(r p) c d -> p d c r", p=2)
                for par in range(2):
                    for cc in range(2):
                        sp.dma_start(pe_[par * HD:(par + 1) * HD, cc, :], rows[par, :, cc, :],
                                     allow_slow_non_contiguous=True).then_inc(in_w, 16)
                sp.dma_start(b1[:, :], I["cmp_b1"].rearrange("c h -> h c"),
                             allow_slow_non_contiguous=True).then_inc(in_w, 16)
                raw = gk[:, :, 24:280]
                sp.dma_start(O["kv_cmp_prompt"].rearrange("o (t p) g c d -> p (o t) (g c d)", p=P),
                             raw[:, 0:QT, :]).then_inc(out, 16)
                sp.dma_start(O["kv_cmp_sample"].rearrange("b o g c d -> b (o g c d)"), raw[0:B, QT, :]).then_inc(out, 16)
                sp.wait_ge(kready, 1)
                sp.dma_start(O["kv_slc_prompt"].rearrange("o (t p) g c d -> p (o t) (g c d)", p=P),
                             kvsw[:, 0:QT, 0:256]).then_inc(out, 16)
                sp.dma_start(O["kv_slc_sample"].rearrange("b o g c d -> b (o g c d)"),
                             kvsw[0:B, QT, 0:256]).then_inc(out, 16)
                sp.dma_start(O["win_prompt"].rearrange("o (t p) g c d -> p (o t) (g c d)", p=P),
                             kvsw[:, QT - 4:QT, 256:512]).then_inc(out, 16)
                sp.dma_start(O["win_sample"][:, WIN - 1].rearrange("b g c d -> b (g c d)"),
                             kvsw[0:B, QT, 256:512]).then_inc(out, 16)
                sp.wait_ge(mready, 1)
                sp.dma_start(O["kv_mem_prompt"].rearrange("o (t p) h c d -> p (o t) (h c d)", p=P),
                             kvm[:, :, :]).then_inc(out, 16)

            @block.tensor
            def _(pe):
                pe.wait_ge(in_w, 16 * 7)
                for cc in range(2):
                    for r in range(16):
                        ins = nc.tensor.matmul(ps[:, cc, 0:1], w1[:, cc, r, :], pe_[:, cc, r:r + 1],
                                               start=(r == 0), stop=(r == 15))
                ins.then_inc(biased, 1)

            @block.scalar
            def _(act):
                nc.scalar.activation(gk[:, :, 0:24], gk[:, :, 0:24], ACT.Sigmoid).then_inc(gated, 1)
                act.wait_ge(meaned, 1)
                nc.scalar.activation(r0[:, :], ss[:, :], ACT.Sqrt).then_inc(sqrted, 1)
                act.wait_ge(rooted, 1)
                for n in (2, 3):
                    v, h, d, t = norms[n]
                    for tt in range(t):
                        for hh in range(h):
                            i = at[n] + tt * h + hh
                            ins = nc.scalar.activation(v[:, tt, hh, :], v[:, tt, hh, :], ACT.Identity,
                                                       scale=ss[:, i:i + 1])
                        ins.then_inc(mscaled, 1)
                act.wait_ge(qready, 1)
                nc.scalar.activation(qr[:, :, :], q[:, :, :], ACT.Copy).then_inc(qcopied, 1)

            @block.gpsimd
            def _(pool):
                pool.wait_ge(in_g, 80)
                done = 0
                for n in (2, 3):
                    v, h, d, t = norms[n]
                    g = gmq if n == 2 else gmk
                    for tt in range(t):
                        done += 1
                        pool.wait_ge(mscaled, done)
                        mchain.link(pool, nc.gpsimd.tensor_tensor(v[:, tt], v[:, tt], bc(g[:, :], 1, h), ALU.mult))
                nc.gpsimd.memset(ss[:, 151:152], 0.0).then_inc(mready, 1)

            @block.vector
            def _(dve):
                chain.link(dve, nc.vector.tensor_scalar(ss[:, 0:108], ss[:, 0:108], 1.0 / HD, EPS, ALU.mult, ALU.add))
                nc.vector.tensor_scalar(ss[:, 108:152], ss[:, 108:152], 1.0 / XD, EPS, ALU.mult,
                                        ALU.add).then_inc(meaned, 1)
                dve.wait_ge(sqrted, 1)
                r, t = r0[:, :], r1[:, :]
                chain.link(dve, nc.vector.reciprocal(r, r))
                chain.link(dve, nc.vector.tensor_tensor(t, r, r, ALU.mult))
                chain.link(dve, nc.vector.tensor_tensor(t, t, ss[:, :], ALU.mult))
                chain.link(dve, nc.vector.tensor_scalar(t, t, -0.5, 1.5, ALU.mult, ALU.add))
                nc.vector.tensor_tensor(ss[:, :], r, t, ALU.mult).then_inc(rooted, 1)
                dve.wait_ge(rooted, 1)
                dve.wait_ge(in_g, 80)
                for n in range(2):
                    v, h, d, t = norms[n]
                    r = ss[:, at[n]:at[n + 1]].rearrange("p (t h) -> p t h", h=h)
                    chain.link(dve, nc.vector.tensor_tensor(v, v, bc(r, 3, d), ALU.mult))
                gb = lambda g, n: bc(bc(g[:, :], 1, n), 1, TT)
                nc.vector.tensor_tensor(q4, q4, gb(gq, H), ALU.mult).then_inc(qready, 1)
                kr = [kv5[:, :, 2 * r:2 * r + 2, 0, :] for r in range(2)]
                for r, g in enumerate((gs, gw)):
                    chain.link(dve, nc.vector.tensor_tensor(kr[r], kr[r], gb(g, G), ALU.mult))
                cos = c("cos").rearrange("p (t d) -> p t d", d=HALF)
                sin = c("sin").rearrange("p (t d) -> p t d", d=HALF)

                def rotate(v, n):
                    x1, x2_ = v[:, :, :, 0:HALF], v[:, :, :, HALF:2 * HALF]
                    cb, sb_ = bc(cos, 2, n), bc(sin, 2, n)
                    a, b = t1[:, :, 0:n, :], t2[:, :, 0:n, :]
                    nc.vector.tensor_tensor(a, x2_, sb_, ALU.mult)
                    chain.link(dve, nc.vector.tensor_tensor(b, x1, sb_, ALU.mult))
                    nc.vector.tensor_tensor(x1, x1, cb, ALU.mult)
                    chain.link(dve, nc.vector.tensor_tensor(x2_, x2_, cb, ALU.mult))
                    nc.vector.tensor_tensor(x1, x1, a, ALU.subtract)
                    ins = nc.vector.tensor_tensor(x2_, x2_, b, ALU.add)
                    chain.link(dve, ins)

                kk = kv5[:, :, :, 0, :]
                rotate(kk, 4)
                nc.vector.memset(ss[:, 0:1], 0.0).then_inc(kready, 1)
                dve.wait_ge(qcopied, 1)
                rotate(qr4, H)
                dve.wait_ge(in_w, 16 * 7)
                dve.wait_ge(biased, 1)
                for cc in range(2):
                    nc.vector.tensor_tensor(bias[:, cc:cc + 1], ps[:, cc, 0:1], b1[:, cc:cc + 1], ALU.add)


def stage_turn(M, A):
    nc, I, O, ps, c = (M[k] for k in ("nc", "I", "O", "ps", "c"))
    gk, kvsw = (A[k] for k in ("gk", "kvsw"))
    kT, kc2, vc2, bias, w2, gcmp = (A[k] for k in ("kT", "kc2", "vc2", "bias", "w2", "gcmp"))
    NW = G * NC
    with Stage(nc, "turn") as st:
        xc = st.sb("xc", [P, 2, G, S // 2])
        w1 = st.sb("w1", [P, 2, 16, CH])
        h = st.sb("h", [P, 2, G, NC])
        sq = st.sb("sq", [NC, G, HD])
        ko = st.sb("ko", [NC, G, HD])
        kss = st.sb("kss", [NC, G])
        sem = st.sem
        in_w, turned, kept, hid, hready, activated, outp, kmean, kroot, knorm, kturn, kdone = (
            sem(n) for n in ("in_w", "turned", "kept", "hid", "hready", "activated", "outp",
                             "kmean", "kroot", "knorm", "kturn", "kdone"))
        chain = Chain(sem("step"))
        items = []
        for r in range(4):
            for half in range(2):
                items.append(("k", r, half))
        for g in range(G):
            for half in range(2):
                items.append(("x", g, half))
        with st.block() as block:
            @block.sync
            def _(sp):
                for cc in range(2):
                    sp.dma_start(w1[:, cc, :, :],
                                 I["cmp_w1"][cc].rearrange("(r q) h -> q r h", q=P)).then_inc(in_w, 16)
                sp.dma_start(w2[:, :, :], I["cmp_w2"].rearrange("c h d -> h c d")).then_inc(in_w, 16)
                sp.dma_start(gcmp[:, :], I["k_norm_cmp"].partition_broadcast(P)).then_inc(in_w, 16)

            @block.tensor
            def _(pe):
                for n, (kind, r, half) in enumerate(items):
                    if n >= 4:
                        pe.wait_ge(kept, n - 3)
                    for a in range(4):
                        t = 4 * half + a
                        if kind == "k":
                            src, m = kvsw[:, t, r * 128:r * 128 + HD], HD
                        else:
                            src, m = gk[:, t, 24 + r * 128:24 + (r + 1) * 128], P
                        ins = nc.tensor.transpose(ps[0:m, n % 4, a * P:(a + 1) * P], src, c("ident"))
                    ins.then_inc(turned, 1)
                pe.wait_ge(in_w, 64)
                pe.wait_ge(kept, len(items))
                for cc in range(2):
                    for r in range(16):
                        rhs = xc[:, cc, :, :].rearrange("p g (n s) -> p g n s", s=8)[
                            :, :, r // 8:r // 8 + NC, r % 8]
                        ins = nc.tensor.matmul(ps[:, 6 + cc, 0:NW], w1[:, cc, r, :], rhs,
                                               start=(r == 0), stop=(r == 15))
                ins.then_inc(hid, 1)
                pe.wait_ge(hready, 1)
                pe.wait_ge(activated, 2)
                for cc in range(2):
                    for g in range(G):
                        ins = nc.tensor.matmul(ps[0:NC, 0, (2 * cc + g) * HD:(2 * cc + g + 1) * HD],
                                               h[:, cc, g, :], w2[:, cc, :], start=True, stop=True)
                ins.then_inc(outp, 1)
                pe.wait_ge(knorm, 1)
                for g in range(G):
                    ins = nc.tensor.transpose(ps[0:HD, 1, g * 64:g * 64 + NC], ko[:, g, :],
                                              c("ident")[0:NC, 0:NC])
                ins.then_inc(kturn, 1)

            @block.scalar
            def _(act):
                for n, (kind, r, half) in enumerate(items):
                    act.wait_ge(turned, n + 1)
                    if kind == "k":
                        br, g = r // 2, r % 2
                        ins = nc.scalar.activation(kT[g * HD:(g + 1) * HD, br, half * 512:(half + 1) * 512],
                                                   ps[0:HD, n % 4, :], ACT.Copy)
                    else:
                        for cc in range(2):
                            for par in range(2):
                                ins = nc.scalar.activation(
                                    xc[par * HD:(par + 1) * HD, cc, r, half * 256:(half + 1) * 256],
                                    ps[cc * HD:(cc + 1) * HD, n % 4, :].rearrange("p (t e) -> p t e", e=2)[:, :, par],
                                    ACT.Copy)
                    ins.then_inc(kept, 1)
                act.wait_ge(hid, 1)
                for cc in range(2):
                    nc.scalar.activation(h[:, cc, :, :].rearrange("p g n -> p (g n)"), ps[:, 6 + cc, 0:NW],
                                         ACT.Gelu_apprx_tanh, bias=bias[:, cc:cc + 1]).then_inc(activated, 1)

            @block.gpsimd
            def _(pool):
                pool.wait_ge(kmean, 1)
                nc.gpsimd.tensor_tensor(kss[:, :], kss[:, :], c("mhalf")[0:NC, :].to_broadcast([NC, G]),
                                        ALU.pow).then_inc(kroot, 1)

            @block.vector
            def _(dve):
                dve.wait_ge(in_w, 64)
                dve.wait_ge(activated, 2)
                nc.vector.memset(vc2[:, :, :], 0.0).then_inc(hready, 1)
                dve.wait_ge(hready, 1)
                dve.wait_ge(outp, 1)
                o4 = ps[0:NC, 0, 0:4 * HD].rearrange("p (c g d) -> p c g d", c=2, g=2)
                for k in range(2):
                    nc.vector.tensor_copy(vc2[k * 64:k * 64 + NC, :, k * HD:(k + 1) * HD], o4[:, 1])
                chain.link(dve, nc.vector.tensor_copy(ko[:, :, :], o4[:, 0]))
                t = sq[:, :, :]
                chain.link(dve, nc.vector.tensor_tensor(t, ko[:, :, :], ko[:, :, :], ALU.mult))
                chain.link(dve, nc.vector.tensor_reduce(kss[:, :], t, AX.X, ALU.add))
                nc.vector.tensor_scalar(kss[:, :], kss[:, :], 1.0 / HD, EPS, ALU.mult, ALU.add).then_inc(kmean, 1)
                dve.wait_ge(kroot, 1)
                chain.link(dve, nc.vector.tensor_tensor(ko[:, :, :], ko[:, :, :], bc(kss[:, :], 2, HD), ALU.mult))
                nc.vector.tensor_tensor(ko[:, :, :], ko[:, :, :], bc(gcmp[0:NC, :], 1, G), ALU.mult).then_inc(knorm, 1)
                chain.link(dve, nc.vector.memset(kc2[:, :, :], 0.0))
                dve.wait_ge(kturn, 1)
                for k in range(2):
                    nc.vector.tensor_copy(kc2[k * HD:(k + 1) * HD, :, k * 64:k * 64 + NC],
                                          ps[0:HD, 1, 0:G * 64].rearrange("p (g n) -> p g n", g=G)[:, :, 0:NC]
                                          ).then_inc(kdone, 1)


def stage_cmp_prompt(M, A):
    nc, ps, c = (M[k] for k in ("nc", "ps", "c"))
    q, gk, kc2, vc2, acc = (A[k] for k in ("q", "gk", "kc2", "vc2", "acc"))
    HP = H // 2
    with Stage(nc, "cmp") as st:
        qT = st.sb("qT", [P, 2, HP, P])
        p_ = st.sb("p", [P, 2, H, 64])
        pT = st.sb("pT", [P, 2, HP, P])
        mx = st.sb("mx", [P, H])
        sm = st.sb("sm", [P, 2, H])
        sem = st.sem
        turned, qkept, scored, shifted, exped, masked, pturned, pkept, attended, used = (
            sem(n) for n in ("turned", "qkept", "scored", "shifted", "exped", "masked", "pturned", "pkept",
                             "attended", "used"))
        chain = Chain(sem("step"))
        neg_ = st.sb("neg", [P, QT * 64])
        neg = neg_[:, :].rearrange("p (t n) -> p t n", t=QT)
        one = c("cmp01").rearrange("p (t n) -> p t n", t=QT)
        with st.block() as block:
            @block.tensor
            def _(pe):
                def turn(i):
                    if i >= 2:
                        pe.wait_ge(qkept, i - 1)
                    for pr in range(HP):
                        ins = nc.tensor.transpose(ps[:, i % 2, pr * P:(pr + 1) * P],
                                                  q[:, i, pr * P:(pr + 1) * P], c("ident"))
                    ins.then_inc(turned, 1)

                def scores(i):
                    pe.wait_ge(qkept, i + 1)
                    if i >= 2:
                        pe.wait_ge(shifted, i - 1)
                    for pr in range(HP):
                        ins = nc.tensor.matmul(ps[:, 2 + i % 2, pr * P:(pr + 1) * P], qT[:, i % 2, pr, :],
                                               kc2[:, 2 * pr // HPG, :], start=True, stop=True)
                    ins.then_inc(scored, 1)

                def turn_p(i):
                    pe.wait_ge(masked, i + 1)
                    if i >= 2:
                        pe.wait_ge(pkept, i - 1)
                    for pr in range(HP):
                        ins = nc.tensor.transpose(ps[:, 4 + i % 2, pr * P:(pr + 1) * P],
                                                  p_[:, i % 2, 2 * pr:2 * pr + 2, :].rearrange("p h n -> p (h n)"),
                                                  c("ident"))
                    ins.then_inc(pturned, 1)

                def attend(i):
                    pe.wait_ge(pkept, i + 1)
                    if i >= 2:
                        pe.wait_ge(used, i - 1)
                    for pr in range(HP):
                        ins = nc.tensor.matmul(ps[:, 6 + i % 2, pr * P:(pr + 1) * P], pT[:, i % 2, pr, :],
                                               vc2[:, 2 * pr // HPG, :], start=True, stop=True)
                    ins.then_inc(attended, 1)

                turn(0)
                scores(0)
                for i in range(QT):
                    if i + 1 < QT:
                        turn(i + 1)
                        scores(i + 1)
                    turn_p(i)
                    if i >= 1:
                        attend(i - 1)
                attend(QT - 1)

            @block.scalar
            def _(act):
                def keep_q(i):
                    act.wait_ge(turned, i + 1)
                    if i >= 2:
                        act.wait_ge(scored, i - 1)
                    nc.scalar.activation(qT[:, i % 2, :, :].rearrange("p h q -> p (h q)"), ps[:, i % 2, :],
                                         ACT.Copy).then_inc(qkept, 1)

                def keep_p(i):
                    act.wait_ge(pturned, i + 1)
                    if i >= 2:
                        act.wait_ge(attended, i - 1)
                    nc.scalar.activation(pT[:, i % 2, :, :].rearrange("p h q -> p (h q)"), ps[:, 4 + i % 2, :],
                                         ACT.Copy).then_inc(pkept, 1)

                keep_q(0)
                for i in range(QT):
                    if i + 1 < QT:
                        keep_q(i + 1)
                    act.wait_ge(shifted, i + 1)
                    nc.scalar.activation(p_[:, i % 2, :, :], p_[:, i % 2, :, :], ACT.Exp,
                                         scale=HD ** -0.5).then_inc(exped, 1)
                    if i >= 1:
                        keep_p(i - 1)
                keep_p(QT - 1)

            @block.vector
            def _(dve):
                def shift(i):
                    dve.wait_ge(scored, i + 1)
                    if i >= 2:
                        dve.wait_ge(pturned, i - 1)
                    p = p_[:, i % 2, :, :]
                    s = ps[:, 2 + i % 2, :].rearrange("p (h n) -> p h n", h=H)
                    chain.link(dve, nc.vector.tensor_tensor(p, s, bc(neg[:, i, :], 1, H), ALU.add))
                    chain.link(dve, nc.vector.tensor_reduce(mx[:, :], p, AX.X, ALU.max))
                    nc.vector.tensor_tensor(p, p, bc(mx[:, :], 2, 64), ALU.subtract).then_inc(shifted, 1)
                    dve.wait_ge(shifted, i + 1)

                def norm(i):
                    p, f = p_[:, i % 2, :, :], sm[:, i % 2, :]
                    dve.wait_ge(exped, i + 1)
                    nc.vector.tensor_tensor(p, p, bc(one[:, i, :], 1, H), ALU.mult).then_inc(masked, 1)
                    dve.wait_ge(masked, i + 1)
                    chain.link(dve, nc.vector.tensor_reduce(f, p, AX.X, ALU.add))
                    chain.link(dve, nc.vector.tensor_scalar(f, f, float(np.finfo(np.float32).tiny), None, ALU.max))
                    chain.link(dve, nc.vector.reciprocal(f, f))
                    chain.link(dve, nc.vector.tensor_tensor(f, f, gk[:, i, 0:H], ALU.mult))

                def use(i):
                    dve.wait_ge(attended, i + 1)
                    nc.vector.tensor_tensor(
                        acc[:, :, i * P:(i + 1) * P].rearrange("p a (b d) -> p a b d", b=2),
                        ps[:, 6 + i % 2, :].rearrange("p (a b d) -> p a b d", a=4, b=2),
                        bc(sm[:, i % 2, :].rearrange("p (a b) -> p a b", b=2), 3, HD), ALU.mult).then_inc(used, 1)

                chain.link(dve, nc.vector.tensor_scalar(neg_[:, :], c("cmp01"), BIG, -BIG, ALU.mult, ALU.add))
                shift(0)
                for i in range(QT):
                    if i + 1 < QT:
                        shift(i + 1)
                    if i >= 2:
                        dve.wait_ge(used, i - 1)
                    norm(i)
                    if i >= 1:
                        use(i - 1)
                use(QT - 1)


def stage_slc_win(M, A):
    nc, ps, c, brT = (M[k] for k in ("nc", "ps", "c", "brT"))
    qr, gk, kvsw, kT, acc = (A[k] for k in ("qr", "gk", "kvsw", "kT", "acc"))
    units = [(i, h, br) for i in range(QT) for h in range(H) for br in range(2)]

    def keys(u):
        i, _, br = units[u]
        return (0 if br == 0 else max(0, i - 4)), i + 1

    items, first_item = [], []
    for u in range(len(units)):
        first_item.append(len(items))
        lo, hi = keys(u)
        n = hi - lo
        items += [(u, a, min(4, n - a)) for a in range(0, n, 4)]
    first_item.append(len(items))
    NU = len(units)
    with Stage(nc, "att") as st:
        qT = st.sb("qT", [P, 2, H, P])
        p_ = st.sb("p", [P, 2, S])
        pT = st.sb("pT", [P, 2, S])
        mx = st.sb("mx", [P, 4])
        sm = st.sb("sm", [P, 4])
        f = st.sb("f", [P, 4])
        sem = st.sem
        zeroed, turned, qkept, scored, maxed, exped, pturned, pkept_a, pkept_v, attended, used, oturned, okept = (
            sem(n) for n in ("zeroed", "turned", "qkept", "scored", "maxed", "exped", "pturned", "pkept_a", "pkept_v",
                             "attended", "used", "oturned", "okept"))
        chain = Chain(sem("step"))

        def wait_kept(eng, m):
            if (m + 1) // 2:
                eng.wait_ge(pkept_a, (m + 1) // 2)
            if m // 2:
                eng.wait_ge(pkept_v, m // 2)

        def keep(eng, m):
            u, a, n = items[m]
            eng.wait_ge(pturned, m + 1)
            if u >= 2:
                eng.wait_ge(attended, u - 1)
            dst, src = pT[:, u % 2, a * P:(a + n) * P], ps[:, 4 + m % 2, 0:n * P]
            if m % 2 == 0:
                nc.scalar.activation(dst, src, ACT.Copy).then_inc(pkept_a, 1)
            else:
                nc.vector.tensor_copy(dst, src).then_inc(pkept_v, 1)

        with st.block() as block:
            @block.tensor
            def _(pe):
                def scores(u):
                    i, h, br = units[u]
                    if h == 0 and br == 0:
                        if u >= 2:
                            pe.wait_ge(used, u - 2)
                        for hh in range(H):
                            j = 2 * i + hh // 4
                            if hh % 4 == 0 and j >= 1:
                                pe.wait_ge(qkept, j)
                            ins = nc.tensor.transpose(ps[0:HD, 7, (hh % 4) * P:(hh % 4 + 1) * P],
                                                      qr[:, i, hh * HD:(hh + 1) * HD], c("ident"))
                            if hh % 4 == 3:
                                ins.then_inc(turned, 1)
                        pe.wait_ge(qkept, 2 * i + 2)
                    if u >= 2:
                        pe.wait_ge(exped, u - 1)
                    lo, hi = keys(u)
                    for a in range(0, hi - lo, 4):
                        n = min(4, hi - lo - a)
                        ins = nc.tensor.matmul(ps[:, 2 * (u % 2) + a // 4, 0:n * P], qT[:, i % 2, h, :],
                                               kT[:, br, (lo + a) * P:(lo + a + n) * P],
                                               start=True, stop=True)
                    ins.then_inc(scored, 1)

                def products(u):
                    i, h, br = units[u]
                    g = h // HPG
                    pe.wait_ge(exped, u + 1)
                    for m in range(first_item[u], first_item[u + 1]):
                        if m >= 2:
                            wait_kept(pe, m - 1)
                        _, a, n = items[m]
                        for b in range(n):
                            ins = nc.tensor.transpose(ps[:, 4 + m % 2, b * P:(b + 1) * P],
                                                      p_[:, u % 2, (a + b) * P:(a + b + 1) * P], c("ident"))
                        ins.then_inc(pturned, 1)

                def attend(u):
                    i, h, br = units[u]
                    g = h // HPG
                    wait_kept(pe, first_item[u + 1])
                    if u >= 2:
                        pe.wait_ge(used, u - 1)
                    if u % 2 and u > 2 * H:
                        pe.wait_ge(okept, (u - 1) // (2 * H))
                    lo, hi = keys(u)
                    for b in range(hi - lo):
                        kv = kvsw[:, lo + b, br * 256 + g * 128:br * 256 + (g + 1) * 128]
                        ins = nc.tensor.matmul(ps[:, 6 + u % 2, 0:P], pT[:, u % 2, b * P:(b + 1) * P],
                                               kv, start=(b == 0), stop=(b == hi - lo - 1))
                    ins.then_inc(attended, 1)

                def turn_out(i):
                    pe.wait_ge(used, (i + 1) * 2 * H)
                    pe.wait_ge(qkept, min(2 * i + 4, 2 * QT))
                    if i:
                        pe.wait_ge(okept, i)
                    for a in range(4):
                        ins = nc.tensor.transpose(ps[:, 7, a * P:(a + 1) * P], acc[:, a, i * P:(i + 1) * P],
                                                  c("ident"))
                    ins.then_inc(oturned, 1)

                scores(0)
                for u in range(NU):
                    if u + 1 < NU:
                        if units[u + 1][1:] == (0, 0) and u > 2 * H:
                            pe.wait_ge(okept, units[u][0])
                        scores(u + 1)
                    products(u)
                    if u >= 1:
                        attend(u - 1)
                        if u % (2 * H) == 1 and u > 2 * H:
                            turn_out(u // (2 * H) - 1)
                attend(NU - 1)
                turn_out(QT - 1)

            @block.scalar
            def _(act):
                def out(act, i):
                    act.wait_ge(oturned, i + 1)
                    nc.scalar.activation(brT[:, 0:4, i * P:(i + 1) * P],
                                         ps[:, 7, :].rearrange("p (a q) -> p a q", a=4), ACT.Copy).then_inc(okept, 1)

                def keep_q(i):
                    for j in range(2):
                        act.wait_ge(turned, 2 * i + j + 1)
                        if i < 2:
                            act.wait_ge(zeroed, 1)
                        nc.scalar.activation(qT[j * HD:(j + 1) * HD, i % 2, HPG * j:HPG * (j + 1), :
                                                ].rearrange("p h q -> p (h q)"),
                                             ps[0:HD, 7, :], ACT.Copy, scale=-(HD ** -0.5)).then_inc(qkept, 1)

                keep_q(0)
                for u in range(NU):
                    i, h, br = units[u]
                    act.wait_ge(maxed, u + 1)
                    if u >= 2:
                        act.wait_ge(pturned, first_item[u - 1])
                    lo, hi = keys(u)
                    n = (hi - lo) * P
                    if u >= 4:
                        act.wait_ge(used, u - 3)
                    src = ps[:, 2 * (u % 2):2 * (u % 2) + 2, :].rearrange("p b n -> p (b n)")[:, 0:n]
                    nc.scalar.activation(p_[:, u % 2, 0:n], src, ACT.Exp, scale=-1.0,
                                         bias=mx[:, u % 4:u % 4 + 1], accum_out=sm[:, u % 4:u % 4 + 1]
                                         ).then_inc(exped, 1)
                    if u + 1 < NU and units[u + 1][1:] == (0, 0):
                        keep_q(i + 1)
                    for m in range(first_item[u], first_item[u + 1]):
                        if m % 2 == 0:
                            keep(act, m)
                    if u % (2 * H) == 2 and u > 2 * H:
                        out(act, u // (2 * H) - 1)
                out(act, QT - 1)

            @block.vector
            def _(dve):
                def maximum(u):
                    i, h, br = units[u]
                    lo, hi = keys(u)
                    n = (hi - lo) * P
                    s = ps[:, 2 * (u % 2):2 * (u % 2) + 2, :].rearrange("p b n -> p (b n)")
                    dve.wait_ge(scored, u + 1)
                    if u >= 4:
                        dve.wait_ge(exped, u - 3)
                    if br == 1 and i >= 4:
                        chain.link(dve, nc.vector.tensor_tensor(s[:, 0:P], s[:, 0:P], c("band"), ALU.subtract))
                    chain.link(dve, nc.vector.tensor_tensor(s[:, n - P:n], s[:, n - P:n], c("causal"),
                                                            ALU.subtract))
                    nc.vector.tensor_reduce(mx[:, u % 4:u % 4 + 1], s[:, 0:n], AX.X, ALU.min).then_inc(maxed, 1)

                def use(u):
                    i, h, br = units[u]
                    k = u % 4
                    chain.link(dve, nc.vector.reciprocal(f[:, k:k + 1], sm[:, k:k + 1]))
                    gate = gk[:, i, (1 + br) * H + h:(1 + br) * H + h + 1]
                    chain.link(dve, nc.vector.tensor_tensor(f[:, k:k + 1], f[:, k:k + 1], gate, ALU.mult))
                    dve.wait_ge(attended, u + 1)
                    o = acc[:, h // 2, i * P + (h % 2) * HD:i * P + (h % 2 + 1) * HD]
                    if u >= 1:
                        dve.wait_ge(used, u)
                    nc.vector.scalar_tensor_tensor(o, ps[:, 6 + u % 2, HD:P], f[:, k:k + 1], o,
                                                   ALU.mult, ALU.add).then_inc(used, 1)

                nc.vector.memset(qT[:, :, :, :], 0.0).then_inc(zeroed, 1)
                maximum(0)
                for u in range(NU):
                    if u + 1 < NU:
                        maximum(u + 1)
                    for m in range(first_item[u], first_item[u + 1]):
                        if m % 2 == 1:
                            keep(dve, m)
                    if u >= 1:
                        use(u - 1)
                use(NU - 1)


def stage_mem_prompt(M, A):
    nc, ps, c, brT = (M[k] for k in ("nc", "ps", "c", "brT"))
    mq, kvm, kmT = (A[k] for k in ("mq", "kvm", "kmT"))
    SC = XD ** -0.5
    NK = XT // P
    with Stage(nc, "mem") as st:
        qT = st.sb("qT", [P, 2, XH, P])
        p_ = st.sb("p", [P, 2, XH, XT])
        pT = brT[:, 3, 0:1024].rearrange("p (h k q) -> p h k q", h=XH, k=NK)
        mx = st.sb("mx", [P, 2, XH])
        sm = st.sb("sm", [P, 2, XH])
        sem = st.sem
        turned, qkept, scored, maxed, exped, normed, pturned, pkept_a, pkept_v, attended, okept = (
            sem(n) for n in ("turned", "qkept", "scored", "maxed", "exped", "normed", "pturned", "pkept_a",
                             "pkept_v", "attended", "okept"))
        chain = Chain(sem("step"))
        kturned, kkept, mqs = (sem(n) for n in ("kturned", "kkept", "mqs"))
        sbank = lambda i, h: ps[:, 2 * (i % 2) + h // 2, (h % 2) * XT:(h % 2 + 1) * XT]
        with st.block() as block:
            @block.sync
            def _(sp):
                sp.dma_start(A["mqS"], mq[0:B, QT, :]).then_inc(mqs, 16)
                sp.wait_ge(mqs, 16)
                sp.wait_ge(A["prep_out"], 16 * 7)

            @block.tensor
            def _(pe):
                for t in range(NK):
                    for h in range(XH):
                        ins = nc.tensor.transpose(ps[:, t, h * P:(h + 1) * P], kvm[:, t, h * 256:h * 256 + XD],
                                                  c("ident"))
                    ins.then_inc(kturned, 1)

                def turn(i):
                    if i:
                        pe.wait_ge(qkept, i)
                    for h in range(XH):
                        ins = nc.tensor.transpose(ps[:, 7, h * P:(h + 1) * P], mq[:, i, h * XD:(h + 1) * XD],
                                                  c("ident"))
                    ins.then_inc(turned, 1)

                def scores(i):
                    pe.wait_ge(qkept, i + 1)
                    if i >= 2:
                        pe.wait_ge(exped, i - 1)
                    for h in range(XH):
                        ins = nc.tensor.matmul(sbank(i, h), qT[:, i % 2, h, :], kmT[:, h, :], start=True, stop=True)
                    ins.then_inc(scored, 1)

                def turn_p(i):
                    pe.wait_ge(normed, i + 1)
                    if i:
                        pe.wait_ge(pkept_a, i)
                        pe.wait_ge(pkept_v, i)
                    for h in range(XH):
                        for k in range(NK):
                            a = (h % 2) * NK + k
                            ins = nc.tensor.transpose(ps[:, 4 + h // 2, a * P:(a + 1) * P],
                                                      p_[:, i % 2, h, k * P:(k + 1) * P], c("ident"))
                        if h % 2 == 1:
                            ins.then_inc(pturned, 1)

                def attend(i):
                    pe.wait_ge(pkept_a, i + 1)
                    pe.wait_ge(pkept_v, i + 1)
                    if i:
                        pe.wait_ge(okept, i)
                    for h in range(XH):
                        for k in range(NK):
                            ins = nc.tensor.matmul(ps[:, 6, h * P:(h + 1) * P], kvm[:, k, h * 256 + XD:(h + 1) * 256],
                                                   pT[:, h, k, :], start=(k == 0), stop=(k == NK - 1))
                    ins.then_inc(attended, 1)

                turn(0)
                pe.wait_ge(kkept, NK)
                scores(0)
                turn(1)
                scores(1)
                for i in range(QT):
                    turn_p(i)
                    if i + 2 < QT:
                        turn(i + 2)
                        scores(i + 2)
                    attend(i)

            @block.scalar
            def _(act):
                def keep_q(i):
                    act.wait_ge(turned, i + 1)
                    if i >= 2:
                        act.wait_ge(scored, i - 1)
                    nc.scalar.activation(qT[:, i % 2, :, :].rearrange("p h q -> p (h q)"), ps[:, 7, :],
                                         ACT.Copy).then_inc(qkept, 1)

                for t in range(NK):
                    act.wait_ge(kturned, t + 1)
                    nc.scalar.activation(kmT[:, :, t * P:(t + 1) * P],
                                         ps[:, t, :].rearrange("p (h q) -> p h q", h=XH), ACT.Copy).then_inc(kkept, 1)
                keep_q(0)
                keep_q(1)
                for i in range(QT):
                    act.wait_ge(maxed, i + 1)
                    if i >= 2:
                        act.wait_ge(pturned, 2 * (i - 1))
                    for h in range(XH):
                        ins = nc.scalar.activation(p_[:, i % 2, h, :], sbank(i, h), ACT.Exp, scale=SC,
                                                   bias=mx[:, i % 2, h:h + 1], accum_out=sm[:, i % 2, h:h + 1])
                    ins.then_inc(exped, 1)
                    act.wait_ge(pturned, 2 * i + 1)
                    if i:
                        act.wait_ge(attended, i)
                    nc.scalar.activation(pT[:, 0:2, :, :].rearrange("p h k q -> p (h k q)"),
                                         ps[:, 4, :], ACT.Copy).then_inc(pkept_a, 1)
                    if i + 2 < QT:
                        keep_q(i + 2)

            @block.vector
            def _(dve):
                def maximum(i):
                    m = mx[:, i % 2, :]
                    dve.wait_ge(scored, i + 1)
                    if i >= 2:
                        dve.wait_ge(exped, i - 1)
                    chain.link(dve, nc.vector.tensor_reduce(
                        m, ps[:, 2 * (i % 2):2 * (i % 2) + 2, :].rearrange("p b (h n) -> p b h n", h=2),
                        AX.X, ALU.max))
                    nc.vector.tensor_scalar(m, m, -SC, None, ALU.mult).then_inc(maxed, 1)

                def norm(i):
                    f, p = sm[:, i % 2, :], p_[:, i % 2, :, :]
                    dve.wait_ge(exped, i + 1)
                    chain.link(dve, nc.vector.reciprocal(f, f))
                    nc.vector.tensor_tensor(p, p, bc(f, 2, XT), ALU.mult).then_inc(normed, 1)

                def out(i):
                    dve.wait_ge(attended, i + 1)
                    nc.vector.tensor_copy(brT[:, 8:12, i * P:(i + 1) * P],
                                          ps[:, 6, :].rearrange("p (a q) -> p a q", a=4)).then_inc(okept, 1)

                maximum(0)
                for i in range(QT):
                    norm(i)
                    if i + 1 < QT:
                        maximum(i + 1)
                    dve.wait_ge(pturned, 2 * i + 2)
                    if i:
                        dve.wait_ge(attended, i)
                    nc.vector.tensor_copy(pT[:, 2:4, :, :].rearrange("p h k q -> p (h k q)"),
                                          ps[:, 5, :]).then_inc(pkept_v, 1)
                    out(i)


def stage_keep_samples(M, A):
    nc = M["nc"]
    with Stage(nc, "keep") as st:
        moved = st.sem("moved")
        with st.block() as block:
            @block.sync
            def _(sp):
                for dst, src in (("qS", "q"), ("qrS", "qr"), ("kvS", "kvsw"), ("gS", "gk")):
                    sp.dma_start(M[dst], A[src][0:B, QT, :]).then_inc(moved, 16)
                sp.wait_ge(moved, 64)


def stage_attention(M):
    nc, x2, brT, memT = (M[k] for k in ("nc", "x2", "brT", "memT"))
    flat = x2[:, :, :].rearrange("p t d -> p (t d)")
    mflat = memT[:, :, :].rearrange("p k t -> p (k t)")
    for n, name in enumerate(("qS", "qrS", "kvS", "mqS")):
        M[name] = mflat[0:B, n * 512:(n + 1) * 512]
    with Stage(nc, "a") as st:
        A = {"mqS": M["mqS"]}
        A["q"] = st.sb("q", [P, TT, 512])
        A["kvsw"] = st.sb("kvsw", [P, TT, 512])
        A["gk"] = st.sb("gk", [P, TT, 280])
        A["qr"] = flat[:, 0:TT * 512].rearrange("p (t n) -> p t n", n=512)
        A["kT"] = flat[:, 4608:4608 + 2 * S].rearrange("p (r t) -> p r t", r=2)
        A["kvm"] = brT[:, 0:2, :].rearrange("p a t -> p (a t)")[:, 0:2048].rearrange("p (t n) -> p t n", t=2)
        A["kmT"] = brT[:, 2, 0:1024].rearrange("p (h t) -> p h t", h=XH)
        A["acc"] = brT[:, 0:4, 0:S]
        with Stage(nc, "a2") as s2:
            A["mq"] = s2.sb("mq", [P, TT, 512])
            A["ss"] = s2.sb("ss", [P, 152])
            stage_tok_proj(M, A)
            stage_prep(M, A)
            stage_mem_prompt(M, A)
        A["w2"] = st.sb("w2", [P, 2, HD])
        A["gcmp"] = st.sb("gcmp", [P, HD])
        A["bias"] = M["bias"]
        A["kc2"] = st.sb("kc2", [P, G, P])
        A["vc2"] = st.sb("vc2", [P, G, P])
        stage_turn(M, A)
        stage_cmp_prompt(M, A)
        stage_slc_win(M, A)
        stage_keep_samples(M, A)


def stage_s_prep(M, A):
    nc, I, ps, c = (M[k] for k in ("nc", "I", "ps", "c"))
    with Stage(nc, "sp") as st:
        sem = st.sem
        turned, kept, loaded = (sem(n) for n in ("turned", "kept", "loaded"))
        chain = Chain(sem("step"))
        with st.block() as block:
            @block.sync
            def _(sp):
                sp.dma_start(A["pt"][:, :], I["page_table"].rearrange("b n -> (b n)").unsqueeze(0)).then_inc(loaded, 16)
                sp.wait_ge(loaded, 16)

            @block.tensor
            def _(pe):
                idb = c("ident")[0:B, 0:B]
                for h in range(H):
                    nc.tensor.transpose(ps[0:HD, 0, h * B:(h + 1) * B], M["qS"][:, h * HD:(h + 1) * HD], idb)
                    nc.tensor.transpose(ps[0:HD, 0, 64 + h * B:64 + (h + 1) * B], M["qrS"][:, h * HD:(h + 1) * HD], idb)
                for r in range(4):
                    nc.tensor.transpose(ps[0:HD, 0, 128 + r * B:128 + (r + 1) * B],
                                        M["kvS"][:, r * 128:r * 128 + HD], idb)
                for h in range(XH):
                    nc.tensor.transpose(ps[:, 1, h * B:(h + 1) * B], M["mqS"][:, h * XD:(h + 1) * XD], idb)
                for r in range(3):
                    ins = nc.tensor.transpose(ps[0:H, 2, r * B:(r + 1) * B], M["gS"][:, r * H:(r + 1) * H], idb)
                ins.then_inc(turned, 1)

            @block.vector
            def _(dve):
                chain.link(dve, nc.vector.memset(A["qz"][:, :, :], 0.0))
                chain.link(dve, nc.vector.memset(A["qmz"][:, :, :, :], 0.0))
                dve.wait_ge(turned, 1)
                hb = lambda ap: ap.rearrange("p (h b) -> p h b", b=B)
                nc.vector.tensor_copy(A["qcS"][:, :, :].rearrange("p b h -> p h b"), hb(ps[0:HD, 0, 0:64]))
                for g in range(G):
                    nc.vector.tensor_copy(A["qz"][g * HD:(g + 1) * HD, :, g * HPG:(g + 1) * HPG
                                                  ].rearrange("p b h -> p h b"),
                                          hb(ps[0:HD, 0, 64 + g * 32:64 + (g + 1) * 32]))
                    nc.vector.tensor_copy(A["knT"][g * HD:(g + 1) * HD, :, :],
                                          ps[0:HD, 0, 128:160].rearrange("p (r g b) -> p r g b", r=2, g=G)[:, :, g, :])
                for h in range(XH):
                    nc.vector.tensor_copy(A["qmz"][:, :, h, h], ps[:, 1, h * B:(h + 1) * B])
                nc.vector.tensor_copy(A["gT"][:, :, :], hb(ps[0:H, 2, 0:24])).then_inc(kept, 1)
                dve.wait_ge(kept, 1)


def load_pages(eng, cache, dst, pt, b, half, done):
    with eng.Fori(0, NPG // 2) as n:
        page = eng.value_load(pt[0:1, bass.ds(n * 2 + (half + NPG * b), 1)], min_val=0, max_val=NPHYS - 1)
        eng.dma_start(dst[:, bass.ds(n * 512 + half * 256, 256)],
                      cache[bass.ds(page, 1)].rearrange("o r g c d -> r (o g c d)")).then_inc(done, 16)


def stage_s_compress(M, A):
    nc, I, ps, c = (M[k] for k in ("nc", "I", "ps", "c"))
    flat = M["x2"][:, :, :].rearrange("p t d -> p (t d)")
    pt, kcT, vc, bias = (A[k] for k in ("pt", "kcT", "vc", "bias"))
    NF = NPG * G // 4
    NW = G * NCS
    with Stage(nc, "sc") as st:
        X = st.sb("X", [P, 2, NPG * 256])
        xtb = st.sb("xt", [P, 2, G, PAST // 2])
        xt = [xtb[:, :, :, :], flat[:, 0:G * PAST].rearrange("p (c g t) -> p c g t", c=2, g=G)]
        w1 = flat[:, 4096:8192].rearrange("p (c r h) -> p c r h", c=2, r=16)
        w2 = st.sb("w2", [P, 2, HD])
        gc = st.sb("gc", [P, HD])
        h = st.sb("h", [P, 2, G, NCS])
        ko = flat[0:NCS, 8192:9216].rearrange("p (n d) -> p n d", d=HD)
        kss = st.sb("kss", [NCS, B * G])
        sq = flat[0:NCS, 2048:2048 + B * G * HD].rearrange("p (n d) -> p n d", d=HD)
        sem = st.sem
        in_x = [sem(f"in_x{q}") for q in range(2)]
        in_xp = [sem(f"in_xp{q}") for q in range(2)]
        (in_w, turned, kept_a, kept_v, hid, activated, outp, okept, kmean, kroot, knorm, kturn, kdone) = (
            sem(n) for n in ("in_w", "turned", "kept_a", "kept_v", "hid", "activated", "outp", "okept",
                             "kmean", "kroot", "knorm", "kturn", "kdone"))
        chain = Chain(sem("step"))

        def keep(eng, f):
            b, k = f // NF, f % NF
            eng.wait_ge(turned, f + 1)
            if b >= 2:
                eng.wait_ge(hid, b - 1)
            for cc in range(2):
                for par in range(2):
                    dst = xt[b % 2][par * HD:(par + 1) * HD, cc, :, k * 128:(k + 1) * 128]
                    src = ps[cc * HD:(cc + 1) * HD, f % 4, :].rearrange("p (g t e) -> p g t e", g=G, e=2)[:, :, :, par]
                    if f % 2 == 0:
                        ins = nc.scalar.activation(dst, src, ACT.Copy)
                    else:
                        ins = nc.vector.tensor_copy(dst, src)
            ins.then_inc(kept_a if f % 2 == 0 else kept_v, 1)

        with st.block() as block:
            @block.sync
            def _(sp):
                for b in range(B):
                    if b >= 2:
                        sp.wait_ge(turned, NF * (b - 1))
                    load_pages(sp, I["cache_kv_cmp"], X[:, b % 2, :], pt, b, 0, in_x[b % 2])
                    if b == 0:
                        for cc in range(2):
                            sp.dma_start(w1[:, cc, :, :],
                                         I["cmp_w1"][cc].rearrange("(r q) h -> q r h", q=P)).then_inc(in_w, 16)
                        sp.dma_start(w2[:, :, :], I["cmp_w2"].rearrange("c h d -> h c d")).then_inc(in_w, 16)
                        sp.dma_start(gc[:, :], I["k_norm_cmp"].partition_broadcast(P)).then_inc(in_w, 16)

            @block.tensor
            def _(pe):
                def turn(b):
                    pe.wait_ge(in_x[b % 2], 8 * NPG * (b // 2 + 1))
                    pe.wait_ge(in_xp[b % 2], 8 * NPG * (b // 2 + 1))
                    for k in range(NF):
                        f = b * NF + k
                        if f >= 4:
                            pe.wait_ge(kept_a if f % 2 == 0 else kept_v, f // 2 - 1)
                        for g in range(G):
                            for j in range(2):
                                ins = nc.tensor.transpose(ps[:, f % 4, (2 * g + j) * P:(2 * g + j + 1) * P],
                                                          X[:, b % 2, (2 * k + j) * 256 + g * 128:(2 * k + j) * 256 + (g + 1) * 128],
                                                          c("ident"))
                        ins.then_inc(turned, 1)

                def hidden(b):
                    pe.wait_ge(kept_a, (b + 1) * NF // 2)
                    pe.wait_ge(kept_v, (b + 1) * NF // 2)
                    if b >= 1:
                        pe.wait_ge(activated, 2 * b)
                    for cc in range(2):
                        for r in range(16):
                            rhs = xt[b % 2][:, cc, :, :].rearrange("p g (n s) -> p g n s", s=8)[
                                :, :, r // 8:r // 8 + NCS, r % 8]
                            ins = nc.tensor.matmul(ps[:, 4 + cc, 0:NW], w1[:, cc, r, :], rhs,
                                                   start=(r == 0), stop=(r == 15))
                    ins.then_inc(hid, 1)

                def project(b):
                    pe.wait_ge(activated, 2 * b + 2)
                    if b >= 2:
                        pe.wait_ge(okept, b - 1)
                    for cc in range(2):
                        for g in range(G):
                            ins = nc.tensor.matmul(ps[0:NCS, 6 + b % 2, (2 * cc + g) * HD:(2 * cc + g + 1) * HD],
                                                   h[:, cc, g, :], w2[:, cc, :], start=True, stop=True)
                    ins.then_inc(outp, 1)

                turn(0)
                pe.wait_ge(in_w, 64)
                for b in range(B):
                    if b + 1 < B:
                        turn(b + 1)
                    if b >= 1:
                        project(b - 1)
                    hidden(b)
                project(B - 1)
                pe.wait_ge(knorm, 1)
                for n in range(B * G):
                    if n % 4 == 0 and n >= 16:
                        pe.wait_ge(kdone, n // 4 - 3)
                    ins = nc.tensor.transpose(ps[0:HD, n // 4, (n % 4) * P:(n % 4) * P + NCS], ko[:, n, :],
                                              c("ident")[0:NCS, 0:NCS])
                    if n % 4 == 3:
                        ins.then_inc(kturn, 1)

            @block.scalar
            def _(act):
                def gelu(b):
                    act.wait_ge(hid, b + 1)
                    if b >= 1:
                        act.wait_ge(outp, b)
                    for cc in range(2):
                        nc.scalar.activation(h[:, cc, :, :].rearrange("p g n -> p (g n)"), ps[:, 4 + cc, 0:NW],
                                             ACT.Gelu_apprx_tanh, bias=bias[:, cc:cc + 1]).then_inc(activated, 1)

                for b in range(B):
                    for k in range(0, NF, 2):
                        keep(act, b * NF + k)
                    if b >= 1:
                        gelu(b - 1)
                gelu(B - 1)

            @block.gpsimd
            def _(pool):
                for b in range(B):
                    if b >= 2:
                        pool.wait_ge(turned, NF * (b - 1))
                    load_pages(pool, I["cache_kv_cmp"], X[:, b % 2, :], pt, b, 1, in_xp[b % 2])
                pool.wait_ge(kmean, 1)
                nc.gpsimd.tensor_tensor(kss[:, :], kss[:, :], c("mhalf")[0:NCS, :].to_broadcast([NCS, B * G]),
                                        ALU.pow).then_inc(kroot, 1)

            @block.vector
            def _(dve):
                def out(b):
                    dve.wait_ge(outp, b + 1)
                    o4 = ps[0:NCS, 6 + b % 2, 0:4 * HD].rearrange("p (c g d) -> p c g d", c=2, g=2)
                    nc.vector.tensor_copy(vc[:, b, :, :], o4[:, 1])
                    nc.vector.tensor_copy(ko[:, 2 * b:2 * b + 2, :], o4[:, 0]).then_inc(okept, 1)

                for b in range(B):
                    for k in range(1, NF, 2):
                        keep(dve, b * NF + k)
                    if b >= 2:
                        out(b - 2)
                out(B - 2)
                out(B - 1)
                dve.wait_ge(okept, B)
                dve.wait_ge(hid, B)
                chain.link(dve, nc.vector.tensor_tensor(sq, ko[:, :, :], ko[:, :, :], ALU.mult))
                chain.link(dve, nc.vector.tensor_reduce(kss[:, :], sq, AX.X, ALU.add))
                nc.vector.tensor_scalar(kss[:, :], kss[:, :], 1.0 / HD, EPS, ALU.mult, ALU.add).then_inc(kmean, 1)
                dve.wait_ge(kroot, 1)
                chain.link(dve, nc.vector.tensor_tensor(ko[:, :, :], ko[:, :, :], bc(kss[:, :], 2, HD), ALU.mult))
                nc.vector.tensor_tensor(ko[:, :, :], ko[:, :, :], bc(gc[0:NCS, :], 1, B * G), ALU.mult).then_inc(knorm, 1)
                for f in range(4):
                    dve.wait_ge(kturn, f + 1)
                    nc.vector.tensor_copy(kcT[:, 4 * f:4 * f + 4, :],
                                          ps[0:HD, f, :].rearrange("p (n q) -> p n q", n=4)[:, :, 0:NCS]
                                          ).then_inc(kdone, 1)


def stage_s_select(M, A):
    nc, ps, c = (M[k] for k in ("nc", "ps", "c"))
    kcT, vc, qcS, gT, oacc, selneg = (A[k] for k in ("kcT", "vc", "qcS", "gT", "oacc", "selneg"))
    NB, R = PAST // 64 + 1, B * H
    with Stage(nc, "ss") as st:
        sT = st.sb("sT", [NCS, R])
        p_ = st.sb("p", [R, NCS])
        mx = st.sb("mx", [R, 1])
        sm = st.sb("sm", [R, 1])
        pT = st.sb("pT", [NCS, R])
        pg = st.sb("pg", [NCS, B * G])
        imp = st.sb("imp", [B * G, NB])
        cmpv = st.sb("cmpv", [B * G, NB, NB])
        eqv = st.sb("eqv", [B * G, NB, NB])
        tri = st.sb("tri", [B * G, NB, NB])
        cnt = st.sb("cnt", [B * G, NB])
        sem = st.sem
        scored, skept, sturned, maxed, exped, normed, pturned, pkept, attended, summed, ranked, spread, tri_ok = (
            sem(n) for n in ("scored", "skept", "sturned", "maxed", "exped", "normed", "pturned", "pkept",
                             "attended", "summed", "ranked", "spread", "tri_ok"))
        vrows = sem("vrows")
        chain = Chain(sem("step"))
        with st.block() as block:
            @block.sync
            def _(sp):
                kv = M["kvS"].rearrange("b (r c d) -> b r c d", c=2, d=HD)
                for b in range(B):
                    q = 32 * (b // 2)
                    sp.dma_start(A["vrow"][q:q + 1, b % 2, :, :], kv[b:b + 1, :, 1, :]).then_inc(vrows, 16)
                sp.wait_ge(vrows, 16 * B)

            @block.gpsimd
            def _(pool):
                nc.gpsimd.memset(tri[:, :, :], 1.0).then_inc(tri_ok, 1)
                pool.wait_ge(tri_ok, 1)
                nc.gpsimd.affine_select(out=tri[:, :, :], in_=tri[:, :, :], compare_op=ALU.is_ge, fill=0.0,
                                        base=-1, pattern=[[1, NB], [-1, NB]], channel_multiplier=0).then_inc(tri_ok, 1)

            @block.tensor
            def _(pe):
                for b in range(B):
                    for g in range(G):
                        lo = b * H + g * HPG
                        ins = nc.tensor.matmul(ps[0:NCS, 0, lo:lo + HPG], kcT[:, 2 * b + g, :],
                                               qcS[:, b, g * HPG:(g + 1) * HPG], start=True, stop=True)
                ins.then_inc(scored, 1)
                pe.wait_ge(skept, 1)
                nc.tensor.transpose(ps[0:R, 1, 0:NCS], sT[:, :], c("ident")[0:NCS, 0:NCS]).then_inc(sturned, 1)
                pe.wait_ge(normed, 1)
                nc.tensor.transpose(ps[0:NCS, 2, 0:R], p_[:, :], c("ident")[0:R, 0:R]).then_inc(pturned, 1)
                pe.wait_ge(pkept, 1)
                for b in range(B):
                    ins = nc.tensor.matmul(ps[0:H, 4 + b // 4, (b % 4) * P:(b % 4 + 1) * P], pT[:, b * H:(b + 1) * H],
                                           vc[:, b, :, :].rearrange("p g d -> p (g d)"), start=True, stop=True)
                ins.then_inc(attended, 1)
                pe.wait_ge(summed, 1)
                nc.tensor.matmul(ps[0:B * G, 3, 0:NB], pg[:, :], c("overlap")[0:NCS, :],
                                 start=True, stop=True).then_inc(attended, 1)
                pe.wait_ge(ranked, 1)
                for b in range(B):
                    ins = nc.tensor.matmul(ps[0:H, 6, b * NB:(b + 1) * NB], c("expand")[0:B * G, b * H:(b + 1) * H],
                                           imp[:, :], start=True, stop=True)
                ins.then_inc(spread, 1)

            @block.scalar
            def _(act):
                act.wait_ge(maxed, 1)
                nc.scalar.activation(p_[:, :], ps[0:R, 1, 0:NCS], ACT.Exp, scale=HD ** -0.5, bias=mx[:, :],
                                     accum_out=sm[:, :]).then_inc(exped, 1)

            @block.vector
            def _(dve):
                dve.wait_ge(scored, 1)
                nc.vector.tensor_copy(sT[:, :], ps[0:NCS, 0, 0:R]).then_inc(skept, 1)
                dve.wait_ge(sturned, 1)
                chain.link(dve, nc.vector.tensor_reduce(mx[:, :], ps[0:R, 1, 0:NCS], AX.X, ALU.max))
                nc.vector.tensor_scalar(mx[:, :], mx[:, :], -(HD ** -0.5), None, ALU.mult).then_inc(maxed, 1)
                dve.wait_ge(exped, 1)
                chain.link(dve, nc.vector.reciprocal(sm[:, :], sm[:, :]))
                nc.vector.tensor_scalar(p_[:, :], p_[:, :], sm[:, :], None, ALU.mult).then_inc(normed, 1)
                dve.wait_ge(pturned, 1)
                nc.vector.tensor_copy(pT[:, :], ps[0:NCS, 2, 0:R]).then_inc(pkept, 1)
                nc.vector.tensor_reduce(pg[:, :], ps[0:NCS, 2, 0:R].rearrange("p (n j) -> p n j", j=HPG), AX.X,
                                        ALU.add).then_inc(summed, 1)
                dve.wait_ge(attended, 1)
                nc.vector.tensor_tensor(oacc[:, :, :],
                                        ps[0:H, 4:6, :].rearrange("p k (b d) -> p (k b) d", d=P),
                                        bc(gT[:, 0, :], 2, P), ALU.mult)
                dve.wait_ge(attended, 2)
                chain.link(dve, nc.vector.tensor_copy(imp[:, :], ps[0:B * G, 3, 0:NB]))
                chain.link(dve, nc.vector.memset(imp[:, 0:1], BIG))
                chain.link(dve, nc.vector.memset(imp[:, NB - 1:NB], BIG))
                si, sj = bc(imp[:, :], 1, NB), bc(imp[:, :], 2, NB)
                nc.vector.tensor_tensor(cmpv[:, :, :], si, sj, ALU.is_gt)
                chain.link(dve, nc.vector.tensor_tensor(eqv[:, :, :], si, sj, ALU.is_equal))
                dve.wait_ge(tri_ok, 2)
                chain.link(dve, nc.vector.tensor_tensor(eqv[:, :, :], eqv[:, :, :], tri[:, :, :], ALU.mult))
                chain.link(dve, nc.vector.tensor_tensor(eqv[:, :, :], eqv[:, :, :], cmpv[:, :, :], ALU.add))
                chain.link(dve, nc.vector.tensor_reduce(cnt[:, :], eqv[:, :, :], AX.X, ALU.add))
                nc.vector.tensor_scalar(imp[:, :], cnt[:, :], 15.5, -BIG, ALU.is_ge, ALU.mult).then_inc(ranked, 1)
                dve.wait_ge(spread, 1)
                chain.link(dve, nc.vector.tensor_copy(selneg[:, :, :],
                                                      ps[0:H, 6, 0:B * NB].rearrange("p (b n) -> p b n", b=B)))


def stage_s_attend(M, A):
    nc, I, ps, c, brT = (M[k] for k in ("nc", "I", "ps", "c", "brT"))
    flat = M["x2"][:, :, :].rearrange("p t d -> p (t d)")
    pt, qz, qmz, knT, gT, oacc, selneg, vrow = (
        A[k] for k in ("pt", "qz", "qmz", "knT", "gT", "oacc", "selneg", "vrow"))
    units = [(k, b) for b in range(B) for k in ("win", "mem", "slc")]
    NU = len(units)
    fills_of = {"win": 2, "mem": 2, "slc": 8}
    chunks_of = {"win": 1, "mem": 1, "slc": 4}
    fill0, chunk0 = [0], [0]
    for k, _ in units:
        fill0.append(fill0[-1] + fills_of[k])
        chunk0.append(chunk0[-1] + chunks_of[k])
    LEN = PAST + 8
    with Stage(nc, "sa") as st:
        pages = st.sb("pages", [P, 2, NPG * 256])
        rows = [st.sb("rows", [P, 2, 2048])[:, :, :], flat[:, 4096:8192].rearrange("p (k n) -> p k n", k=2)]
        kTb = [flat[:, q * 2048:(q + 1) * 2048] for q in range(2)]
        s_ = st.sb("s", [H, 2, LEN])
        pT = st.sb("pT", [P, 2, (NPG + 1) * H])
        mx = st.sb("mx", [H, 4])
        sm = st.sb("sm", [H, 4])
        om = flat[0:XH, 8192:9216].rearrange("p (b d) -> p b d", d=XD)
        own = st.sb("own", [XH, XH, XD])
        snew = st.sb("snew", [H, 2, B])
        sem = st.sem
        in_s = [sem(f"in_s{q}") for q in range(2)]
        in_p = [sem(f"in_p{q}") for q in range(2)]
        in_win, in_mem = ([sem(f"in_{n}{q}") for q in range(2)] for n in ("win", "mem"))
        (turned, kept_a, kept_v, scored, skept, maxed, exped, pturned, pkept, attended, used, first, newk,
         oturned) = (
            sem(n) for n in ("turned", "kept_a", "kept_v", "scored", "skept", "maxed", "exped", "pturned", "pkept",
                             "attended", "used", "first", "newk", "oturned"))
        chain = Chain(sem("step"))

        def rows_of(u):
            k, b = units[u]
            return pages[:, b % 2, :] if k == "slc" else rows[b % 2][:, ("win", "mem").index(k), :]

        def wait_rows(pe, u):
            k, b = units[u]
            if k == "slc":
                pe.wait_ge(in_s[b % 2], 8 * NPG * (b // 2 + 1))
                pe.wait_ge(in_p[b % 2], 8 * NPG * (b // 2 + 1))
            else:
                pe.wait_ge((in_win if k == "win" else in_mem)[b % 2], 16 * (b // 2 + 1))

        bank = lambda f: ps[:, (0, 1, 2, 7)[f % 4], :]

        def heads(k):
            return XH if k == "mem" else H

        def length(k):
            return {"win": WIN + 1, "mem": XT, "slc": PAST + 1}[k]

        def keep(eng, f):
            u = max(n for n in range(NU) if fill0[n] <= f)
            k, b = units[u]
            j = f - fill0[u]
            eng.wait_ge(turned, f + 1)
            if u >= 2:
                eng.wait_ge(scored, chunk0[u - 1])
            if k == "mem":
                parts = [(kTb[u % 2][:, j * 512:(j + 1) * 512], bank(f))]
            else:
                parts = [(kTb[u % 2][g * HD:(g + 1) * HD, j * 256:(j + 1) * 256],
                          bank(f)[0:HD, g * 256:(g + 1) * 256]) for g in range(G)]
            for dst, src in parts:
                if f % 2 == 0:
                    ins = nc.scalar.activation(dst, src, ACT.Copy)
                else:
                    ins = nc.vector.tensor_copy(dst, src)
            ins.then_inc(kept_a if f % 2 == 0 else kept_v, 1)

        def wait_fills(eng, n):
            if (n + 1) // 2:
                eng.wait_ge(kept_a, (n + 1) // 2)
            if n // 2:
                eng.wait_ge(kept_v, n // 2)

        with st.block() as block:
            @block.sync
            def _(sp):
                for b in range(B):
                    if b >= 2:
                        sp.wait_ge(attended, 3 * (b - 2) + 1)
                    sp.dma_start(rows[b % 2][:, 0, 0:4 * 256].rearrange("p (t n) -> p t n", t=4),
                                 I["cache_kv_win"][b].rearrange("(t p) g c d -> p t (g c d)", p=P)
                                 ).then_inc(in_win[b % 2], 16)
                    if b >= 2:
                        sp.wait_ge(attended, 3 * (b - 2) + 2)
                    sp.dma_start(rows[b % 2][:, 1, :].rearrange("p (t n) -> p t n", t=2),
                                 I["cache_kv_mem"][b].rearrange("(t p) h c d -> p t (h c d)", p=P)
                                 ).then_inc(in_mem[b % 2], 16)
                    if b >= 2:
                        sp.wait_ge(attended, 3 * (b - 2) + 3)
                    load_pages(sp, I["cache_kv_slc"], pages[:, b % 2, :], pt, b, 0, in_s[b % 2])

            @block.gpsimd
            def _(pool):
                for b in range(B):
                    if b >= 2:
                        pool.wait_ge(attended, 3 * (b - 2) + 3)
                    load_pages(pool, I["cache_kv_slc"], pages[:, b % 2, :], pt, b, 1, in_p[b % 2])

            @block.tensor
            def _(pe):
                def turn(u):
                    k, b = units[u]
                    wait_rows(pe, u)
                    kv = rows_of(u)
                    for j in range(fills_of[k]):
                        f = fill0[u] + j
                        if f == 3:
                            pe.wait_ge(newk, 1)
                        if f >= 4:
                            wait_fills(pe, f - 3)
                        for a in range(4):
                            if k == "mem":
                                src, m = kv[:, j * 1024 + a * 256:j * 1024 + a * 256 + XD], P
                            else:
                                o = (2 * j + a % 2) * 256 + (a // 2) * 128
                                src, m = kv[:, o:o + HD], HD
                            ins = nc.tensor.transpose(bank(f)[0:m, a * P:(a + 1) * P], src, c("ident"))
                        ins.then_inc(turned, 1)

                def scores(u):
                    k, b = units[u]
                    wait_fills(pe, fill0[u + 1])
                    for j in range(chunks_of[k]):
                        n = chunk0[u] + j
                        if n >= 2:
                            pe.wait_ge(skept, n - 1)
                        out = ps[0:heads(k), 3 + n % 2, :]
                        if k == "mem":
                            kt = kTb[u % 2][:, 0:1024].rearrange("p (t h q) -> p t h q", t=2, h=XH)
                            for h in range(XH):
                                ins = nc.tensor.matmul(out[:, 0:XT], qmz[:, b, h, :], kt[:, :, h, :],
                                                       start=(h == 0), stop=(h == XH - 1))
                        else:
                            ins = nc.tensor.matmul(out, qz[:, b, :], kTb[u % 2][:, j * 512:(j + 1) * 512],
                                                   start=True, stop=True)
                        ins.then_inc(scored, 1)

                def turn_p(u):
                    k, b = units[u]
                    nh = heads(k)
                    pe.wait_ge(exped, u + 1)
                    if u >= 1:
                        pe.wait_ge(pkept, u)
                    full = length(k) // P
                    for t in range(full):
                        ins = nc.tensor.transpose(ps[:, 5, t * nh:(t + 1) * nh], s_[0:nh, u % 2, t * P:(t + 1) * P],
                                                  c("ident")[0:nh, 0:nh])
                    if k != "mem":
                        ins = nc.tensor.transpose(ps[0:1, 5, full * nh:(full + 1) * nh],
                                                  s_[0:nh, u % 2, full * P:full * P + 1], c("ident")[0:nh, 0:nh])
                    ins.then_inc(pturned, 1)

                def attend(u):
                    k, b = units[u]
                    kv = rows_of(u)
                    nh, full = heads(k), length(k) // P
                    pe.wait_ge(pkept, u + 1)
                    if u >= 1:
                        pe.wait_ge(used, u)
                    for t in range(full):
                        w = pT[:, u % 2, t * nh:(t + 1) * nh]
                        if k == "mem":
                            rhs = kv[:, t * 1024:(t + 1) * 1024].rearrange("p (h c d) -> p h c d", c=2, d=XD)[:, :, 1, :]
                            out = ps[0:nh, 6, 0:512]
                        else:
                            rhs = kv[:, t * 256:(t + 1) * 256].rearrange("p (g c d) -> p g c d", c=2, d=HD)[:, :, 1, :]
                            out = ps[0:nh, 6, 0:P]
                        ins = nc.tensor.matmul(out, w, rhs, start=(t == 0), stop=(t == full - 1 and k == "mem"))
                    if k != "mem":
                        br, q = 0 if k == "slc" else 1, 32 * (b // 2)
                        ins = nc.tensor.matmul(out, pT[q:q + 1, u % 2, full * nh:(full + 1) * nh],
                                               vrow[q:q + 1, b % 2, 2 * br:2 * br + 2, :].rearrange("p g d -> p (g d)"),
                                               start=False, stop=True)
                    ins.then_inc(attended, 1)

                for br in range(2):
                    for b in range(B):
                        ins = nc.tensor.matmul(ps[0:H, 7, br * B + b:br * B + b + 1], qz[:, b, :],
                                               knT[:, br, b:b + 1], start=True, stop=True)
                ins.then_inc(first, 1)
                turn(0)
                for u in range(NU):
                    if u + 1 < NU:
                        turn(u + 1)
                    scores(u)
                    if u >= 1:
                        turn_p(u - 1)
                    if u >= 2:
                        attend(u - 2)
                turn_p(NU - 1)
                attend(NU - 2)
                attend(NU - 1)
                pe.wait_ge(used, NU)
                for b in range(B):
                    nc.tensor.transpose(ps[:, 0, b * H:(b + 1) * H], oacc[:, b, :], c("ident")[0:H, 0:H])
                    ins = nc.tensor.transpose(ps[:, 1, b * XH:(b + 1) * XH], om[:, b, :], c("ident")[0:XH, 0:XH])
                ins.then_inc(oturned, 1)

            @block.scalar
            def _(act):
                def softmax(u):
                    k, b = units[u]
                    nh, n = heads(k), length(k)
                    act.wait_ge(maxed, u + 1)
                    sc = XD ** -0.5 if k == "mem" else HD ** -0.5
                    if u >= 4:
                        act.wait_ge(used, u - 3)
                    nc.scalar.activation(s_[0:nh, u % 2, 0:n], s_[0:nh, u % 2, 0:n], ACT.Exp, scale=sc,
                                         bias=mx[0:nh, u % 4:u % 4 + 1],
                                         accum_out=sm[0:nh, u % 4:u % 4 + 1]).then_inc(exped, 1)

                def keep_p(u):
                    k, b = units[u]
                    nh, full = heads(k), length(k) // P
                    act.wait_ge(pturned, u + 1)
                    if u >= 2:
                        act.wait_ge(attended, u - 1)
                    if k == "mem":
                        nc.scalar.activation(pT[:, u % 2, 0:full * nh], ps[:, 5, 0:full * nh], ACT.Copy).then_inc(pkept, 1)
                    else:
                        nc.scalar.activation(pT[:, u % 2, 0:full * nh], ps[:, 5, 0:full * nh], ACT.Copy)
                        nc.scalar.activation(pT[32 * (b // 2):32 * (b // 2) + 1, u % 2, full * nh:(full + 1) * nh],
                                             ps[0:1, 5, full * nh:(full + 1) * nh], ACT.Copy).then_inc(pkept, 1)

                for f in range(fill0[1]):
                    if f % 2 == 0:
                        keep(act, f)
                for u in range(NU):
                    if u + 1 < NU:
                        for f in range(fill0[u + 1], fill0[u + 2]):
                            if f % 2 == 0:
                                keep(act, f)
                    softmax(u)
                    if u >= 1:
                        keep_p(u - 1)
                keep_p(NU - 1)

            @block.vector
            def _(dve):
                def gather(u):
                    k, b = units[u]
                    nh, n = heads(k), length(k)
                    if u >= 2:
                        dve.wait_ge(pturned, u - 1)
                    for j in range(chunks_of[k]):
                        cn = chunk0[u] + j
                        dve.wait_ge(scored, cn + 1)
                        src = ps[0:nh, 3 + cn % 2, :]
                        if k == "mem":
                            ins = nc.vector.tensor_copy(s_[0:nh, u % 2, 0:XT], src[:, 0:XT])
                        elif k == "win":
                            ins = nc.vector.tensor_copy(s_[:, u % 2, 0:WIN], src)
                        else:
                            ins = nc.vector.tensor_tensor(
                                s_[:, u % 2, j * 512:(j + 1) * 512].rearrange("p (n e) -> p n e", e=64),
                                src.rearrange("p (n e) -> p n e", e=64), bc(selneg[:, b, 8 * j:8 * j + 8], 2, 64),
                                ALU.add)
                        ins.then_inc(skept, 1)
                    if k != "mem":
                        br = 0 if k == "slc" else 1
                        chain.link(dve, nc.vector.tensor_copy(s_[:, u % 2, n - 1:n], snew[:, br, b:b + 1]))
                    dve.wait_ge(skept, chunk0[u + 1])
                    chain.link(dve, nc.vector.tensor_reduce(mx[0:nh, u % 4:u % 4 + 1], s_[0:nh, u % 2, 0:n], AX.X,
                                                            ALU.max))
                    sc = XD ** -0.5 if k == "mem" else HD ** -0.5
                    nc.vector.tensor_scalar(mx[0:nh, u % 4:u % 4 + 1], mx[0:nh, u % 4:u % 4 + 1], -sc, None,
                                            ALU.mult).then_inc(maxed, 1)

                def use(u):
                    k, b = units[u]
                    nh = heads(k)
                    f = sm[0:nh, u % 4:u % 4 + 1]
                    dve.wait_ge(exped, u + 1)
                    chain.link(dve, nc.vector.reciprocal(f, f))
                    if k != "mem":
                        br = 1 if k == "slc" else 2
                        chain.link(dve, nc.vector.tensor_tensor(f, f, gT[:, br, b:b + 1], ALU.mult))
                    dve.wait_ge(attended, u + 1)
                    if k == "mem":
                        chain.link(dve, nc.vector.scalar_tensor_tensor(
                            own[:, :, :], ps[0:nh, 6, :].rearrange("p (h d) -> p h d", h=XH), f,
                            bc(c("ident")[0:XH, 0:XH], 2, XD), ALU.mult, ALU.mult))
                        nc.vector.tensor_reduce(om[:, b, :], own[:, :, :].rearrange("p h d -> p d h"), AX.X,
                                                ALU.add).then_inc(used, 1)
                    else:
                        if u >= 1:
                            dve.wait_ge(used, u)
                        nc.vector.scalar_tensor_tensor(oacc[:, b, :], ps[0:nh, 6, 0:P], f, oacc[:, b, :],
                                                       ALU.mult, ALU.add).then_inc(used, 1)

                dve.wait_ge(first, 1)
                nc.vector.tensor_copy(snew[:, :, :].rearrange("p r b -> p (r b)"), ps[0:H, 7, 0:2 * B]).then_inc(newk, 1)
                dve.wait_ge(newk, 1)
                for f in range(fill0[1]):
                    if f % 2 == 1:
                        keep(dve, f)
                for u in range(NU):
                    if u + 1 < NU:
                        for f in range(fill0[u + 1], fill0[u + 2]):
                            if f % 2 == 1:
                                keep(dve, f)
                    gather(u)
                    if u >= 2:
                        use(u - 2)
                use(NU - 2)
                use(NU - 1)
                dve.wait_ge(oturned, 1)
                for h in range(H):
                    lo, g = (h % 2) * HD, h // HPG
                    src = ps[g * HD:(g + 1) * HD, 0, 0:B * H].rearrange("p (b h) -> p b h", h=H)[:, :, h]
                    nc.vector.tensor_copy(brT[lo:lo + HD, h // 2, S:T], src)
                chain.link(dve, nc.vector.tensor_copy(brT[:, 8:12, S:T],
                                                      ps[:, 1, 0:B * XH].rearrange("p (b h) -> p h b", h=XH)))


def stage_samples(M):
    nc = M["nc"]
    with Stage(nc, "s") as st:
        A = dict(
            pt=st.sb("pt", [1, B * NPG], I32), vrow=st.sb("vrow", [P, 2, 4, HD]),
            qcS=st.sb("qcS", [HD, B, H]), qz=st.sb("qz", [P, B, H]), knT=st.sb("knT", [P, 2, B]),
            qmz=st.sb("qmz", [P, B, XH, XH]), gT=st.sb("gT", [H, 3, B]), oacc=st.sb("oacc", [H, B, P]),
            selneg=st.sb("selneg", [H, B, PAST // 64 + 1]), bias=M["bias"])
        stage_s_prep(M, A)
        with Stage(nc, "s2") as s2:
            flat = M["x2"][:, :, :].rearrange("p t d -> p (t d)")
            A["kcT"] = flat[0:HD, 0:B * G * NCS].rearrange("p (n q) -> p n q", q=NCS)
            A["vc"] = s2.sb("vc", [NCS, B, G, HD])
            stage_s_compress(M, A)
            stage_s_select(M, A)
        stage_s_attend(M, A)


def stage_merge(M):
    nc, I, xnT, brT, ps, x2 = (M[k] for k in ("nc", "I", "xnT", "brT", "ps", "x2"))
    mixT = M["mixT"]
    wg = I["w_in"].rearrange("(k p) n -> p k n", p=P)
    wb = I["w_branch"].rearrange("n (k p) d -> p n k d", p=P)
    loads = [(n, j) for n in range(3) for j in range(KT)]
    steps = [(l, b) for l in range(len(loads)) for b in range(NB3)]
    with Stage(nc, "mg") as st:
        xnR, brR = M["xnR"], M["brR"]
        w, wl = st.pair("w", [P, 2, 12, P])
        wh = st.sb("wh", [P, 2, 12, P], FR)
        bh = st.sb("bh", [P, 4, T], FR)
        xh = M["x2R"][:, :, :].rearrange("p t d -> p (t d)")[:, 0:KT * T].rearrange("p (k t) -> p k t", k=KT)
        mflat = M["memT"][:, :, :].rearrange("p k t -> p (k t)")
        sg = mflat[:, 0:2 * BLK].rearrange("p (s n) -> p s n", s=2)
        tm = mflat[:, 2 * BLK:3 * BLK]
        sem = st.sem
        in_w = [sem(f"in_w{q}") for q in range(2)]
        projected, gated, merged, w_high, w_low, x_high, x_low, b_high, b_low = (
            sem(n) for n in ("projected", "gated", "merged", "w_high", "w_low", "x_high", "x_low", "b_high",
                             "b_low"))
        chain = Chain(sem("step"))
        tok = lambda b: slice(b * BLK, (b + 1) * BLK)
        with st.block() as block:
            @block.sync
            def _(sp):
                for l, (n, j) in enumerate(loads):
                    if l >= 2:
                        sp.wait_ge(projected, NB3 * (l - 1))
                    q, cols = l % 2, slice(j * P, (j + 1) * P)
                    sp.dma_start(w[:, q, 0:KT, :], wg[:, :, C_MG + n * D + j * P:C_MG + n * D + (j + 1) * P]
                                 ).then_inc(in_w[q], 16)
                    sp.dma_start(w[:, q, KT:12, :], wb[:, n, :, cols]).then_inc(in_w[q], 16)

            @block.tensor
            def _(pe):
                for s, (l, b) in enumerate(steps):
                    n, j = loads[l]
                    if b == 0:
                        pe.wait_ge(w_low, l + 1)
                    if l == 0:
                        pe.wait_ge(x_low, b + 1)
                    if s >= 4:
                        pe.wait_ge(merged, s - 3)
                    wk = lambda k: (wh[:, l % 2, k, :], wl[:, l % 2, k, :])
                    products(nc, ps[:, s % 4, 0:BLK],
                             [(wk(k), (xh[:, k, tok(b)], xnR[:, k, tok(b)])) for k in range(KT)])
                    if j == 0:
                        pe.wait_ge(b_low, NB3 * n + b + 1)
                    products(nc, ps[:, 4 + s % 4, 0:BLK],
                             [(wk(KT + k), (bh[:, k, tok(b)], brR[:, 4 * n + k, tok(b)])) for k in range(4)]
                             ).then_inc(projected, 1)

            @block.scalar
            def _(act):
                def split_w(l):
                    act.wait_ge(in_w[l % 2], 32 * (l // 2 + 1))
                    high(nc, wh[:, l % 2, :, :], w[:, l % 2, :, :]).then_inc(w_high, 1)

                def split_b(n, b):
                    high(nc, bh[:, :, tok(b)], brT[:, 4 * n:4 * n + 4, tok(b)]).then_inc(b_high, 1)

                for b in range(NB3):
                    high(nc, xh[:, :, tok(b)], xnT[:, :, tok(b)]).then_inc(x_high, 1)
                    if b == 0:
                        split_w(0)
                    split_b(0, b)
                for s, (l, b) in enumerate(steps):
                    n, j = loads[l]
                    act.wait_ge(projected, s + 1)
                    if s >= 2:
                        act.wait_ge(merged, s - 1)
                    nc.scalar.activation(sg[:, s % 2, :], ps[:, s % 4, 0:BLK], ACT.Sigmoid).then_inc(gated, 1)
                    if b == 0 and l + 1 < len(loads):
                        if l >= 1:
                            act.wait_ge(projected, NB3 * l)
                        split_w(l + 1)
                    if j == KT - 1 and n < 2:
                        split_b(n + 1, b)

            @block.vector
            def _(dve):
                def split_w(l):
                    dve.wait_ge(w_high, l + 1)
                    low(nc, wl[:, l % 2, :, :], w[:, l % 2, :, :], wh[:, l % 2, :, :]).then_inc(w_low, 1)

                def split_b(n, b):
                    dve.wait_ge(b_high, NB3 * n + b + 1)
                    low(nc, brR[:, 4 * n:4 * n + 4, tok(b)], brT[:, 4 * n:4 * n + 4, tok(b)], bh[:, :, tok(b)]).then_inc(b_low, 1)

                for b in range(NB3):
                    dve.wait_ge(x_high, b + 1)
                    low(nc, xnR[:, :, tok(b)], xnT[:, :, tok(b)], xh[:, :, tok(b)]).then_inc(x_low, 1)
                    if b == 0:
                        split_w(0)
                    split_b(0, b)
                for s, (l, b) in enumerate(steps):
                    n, j = loads[l]
                    dve.wait_ge(gated, s + 1)
                    dst = mixT[:, j, tok(b)]
                    if n == 0:
                        nc.vector.tensor_tensor(dst, sg[:, s % 2, :], ps[:, 4 + s % 4, 0:BLK],
                                                ALU.mult).then_inc(merged, 1)
                    else:
                        dve.wait_ge(merged, s)
                        chain.link(dve, nc.vector.tensor_tensor(tm, sg[:, s % 2, :], ps[:, 4 + s % 4, 0:BLK],
                                                                ALU.mult))
                        nc.vector.tensor_tensor(dst, dst, tm, ALU.add).then_inc(merged, 1)
                    if b == 0 and l + 1 < len(loads):
                        split_w(l + 1)
                    if j == KT - 1 and n < 2:
                        split_b(n + 1, b)


def stage_out(M):
    nc, I, xnT, ps, x2, c = (M[k] for k in ("nc", "I", "xnT", "ps", "x2", "c"))
    mixT = M["mixT"]
    with Stage(nc, "out") as st:
        w, wl = st.pair("w", [P, 2, KT, 512])
        gain = st.sb("gain", [P, KT])
        ss = st.sb("ss", [P, TT])
        mixh, mixR = M["xnR"], M["mixR"]
        wh = M["brR"][:, 0:8, :].rearrange("p k t -> p (k t)")[:, 0:2 * KT * 512].rearrange(
            "p (q k n) -> p q k n", q=2, k=KT)
        xs = mixT[:, :, :].rearrange("p k t -> p (k t)")
        sem = st.sem
        in_w = [sem(f"in_w{q}") for q in range(4)]
        in_x, in_g, cleared, projected, added, squared, meaned, rooted, scaled, turned, stored = (
            sem(n) for n in ("in_x", "in_g", "cleared", "projected", "added", "squared", "meaned", "rooted", "scaled",
                             "turned", "stored"))
        m_high, m_low, w_high, w_low = (sem(n) for n in ("m_high", "m_low", "w_high", "w_low"))
        starts = (0, 1, 5)
        spans = (slice(0, P), slice(P, 5 * P), slice(5 * P, T))
        junk = st.sb("junk", [P, D])
        wv = I["w_out"].rearrange("(k p) n -> p k n", p=P)
        with st.block() as block:
            @block.sync
            def _(sp):
                for q in range(2):
                    for k in (0, 4):
                        sp.dma_start(w[:, q, k:k + 4, :], wv[:, k:k + 4, q * 512:(q + 1) * 512]
                                     ).then_inc(in_w[2 * q + k // 4], 16)
                sp.dma_start(x2[:, 0:QT, :], I["x_prompt"].rearrange("o (t p) d -> p (o t) d", p=P)
                             ).then_inc(in_x, 16)
                sp.dma_start(x2[0:B, QT, :], I["x_sample"].rearrange("b o d -> (b o) d")).then_inc(in_x, 16)
                sp.dma_start(gain[:, :], I["norm_ffn"].rearrange("(k p) -> p k", p=P),
                             allow_slow_non_contiguous=True).then_inc(in_g, 16)

            @block.gpsimd
            def _(pool):
                pool.wait_ge(meaned, 1)
                nc.gpsimd.tensor_tensor(ss[:, :], ss[:, :], c("mhalf").to_broadcast([P, TT]),
                                        ALU.pow).then_inc(rooted, 1)

            @block.tensor
            def _(pe):
                n = 0
                for q in range(2):
                    pe.wait_ge(w_low, 2 * q + 1)
                    for t in range(TT):
                        m = B if t == QT else P
                        if n >= 4:
                            pe.wait_ge(added, n - 3)
                        if q == 0 and t in starts:
                            pe.wait_ge(m_low, starts.index(t) + 1)
                        rows = slice(t * P, t * P + m)
                        terms = [((mixh[:, k, rows], mixR[:, k, rows]), (wh[:, q, k, :], wl[:, q, k, :]))
                                 for k in range(KT)]
                        products(nc, ps[0:m, n % 4, :], terms[:4], last=False)
                        if t == 0:
                            pe.wait_ge(w_low, 2 * q + 2)
                        products(nc, ps[0:m, n % 4, :], terms[4:], first=False).then_inc(projected, 1)
                        n += 1
                n = 0
                for t in range(TT):
                    m = B if t == QT else P
                    pe.wait_ge(scaled, t + 1)
                    for kk in range(2):
                        if n >= 4:
                            pe.wait_ge(stored, n - 3)
                        for a in range(4):
                            k = 4 * kk + a
                            ins = nc.tensor.transpose(ps[:, 4 + n % 4, a * P:a * P + m],
                                                      xs[0:m, (t % 4) * D + k * P:(t % 4) * D + (k + 1) * P],
                                                      c("ident")[0:m, 0:m])
                        ins.then_inc(turned, 1)
                        n += 1

            @block.scalar
            def _(act):
                def split_w(i):
                    act.wait_ge(in_w[i], 16)
                    q, ks = i // 2, slice(i % 2 * 4, i % 2 * 4 + 4)
                    high(nc, wh[:, q, ks, :], w[:, q, ks, :]).then_inc(w_high, 1)

                high(nc, mixh[:, :, spans[0]], mixT[:, :, spans[0]]).then_inc(m_high, 1)
                split_w(0)
                split_w(1)
                for tok in spans[1:]:
                    high(nc, mixh[:, :, tok], mixT[:, :, tok]).then_inc(m_high, 1)
                split_w(2)
                split_w(3)
                for t in range(TT):
                    m = B if t == QT else P
                    act.wait_ge(added, TT + t + 1)
                    if t:
                        act.wait_ge(squared, t)
                    nc.scalar.activation(junk[0:m, :], x2[0:m, t, :], ACT.Square,
                                         accum_out=ss[0:m, t:t + 1]).then_inc(squared, 1)

            def store(dve, n):
                t, kk = n // 2, n % 2
                m = B if t == QT else P
                dve.wait_ge(turned, n + 1)
                src = ps[:, 4 + n % 4, :].rearrange("p (a q) -> p a q", a=4)[:, :, 0:m]
                nc.vector.tensor_tensor(xnT[:, 4 * kk:4 * kk + 4, t * P:t * P + m], src,
                                        bc(gain[:, 4 * kk:4 * kk + 4], 2, m), ALU.mult).then_inc(stored, 1)

            @block.vector
            def _(dve):
                nc.vector.memset(ss[:, :], 1.0).then_inc(cleared, 1)

                def split_w(i):
                    dve.wait_ge(w_high, i + 1)
                    q, ks = i // 2, slice(i % 2 * 4, i % 2 * 4 + 4)
                    low(nc, wl[:, q, ks, :], w[:, q, ks, :], wh[:, q, ks, :]).then_inc(w_low, 1)

                for i, tok in enumerate(spans):
                    dve.wait_ge(m_high, i + 1)
                    low(nc, mixR[:, :, tok], mixT[:, :, tok], mixh[:, :, tok]).then_inc(m_low, 1)
                    if i == 0:
                        split_w(0)
                        split_w(1)
                dve.wait_ge(in_x, 32)
                n = 0
                for q in range(2):
                    for t in range(TT):
                        m = B if t == QT else P
                        dve.wait_ge(projected, n + 1)
                        dst = x2[0:m, t, q * 512:(q + 1) * 512]
                        nc.vector.tensor_tensor(dst, dst, ps[0:m, n % 4, :], ALU.add).then_inc(added, 1)
                        n += 1
                        if n in (3, 5):
                            split_w(2 + n // 5)
                dve.wait_ge(squared, TT)
                nc.vector.tensor_scalar(ss[:, :], ss[:, :], 1.0 / D, EPS, ALU.mult, ALU.add).then_inc(meaned, 1)
                dve.wait_ge(rooted, 1)
                dve.wait_ge(in_g, 16)
                for t in range(TT):
                    m = B if t == QT else P
                    if t >= 4:
                        dve.wait_ge(turned, 2 * (t - 3))
                    nc.vector.tensor_scalar(xs[0:m, (t % 4) * D:(t % 4 + 1) * D], x2[0:m, t, :], ss[0:m, t:t + 1],
                                            None, ALU.mult).then_inc(scaled, 1)
                    for n in range(2 * t - 2, 2 * t) if t else ():
                        store(dve, n)
                for n in range(2 * TT - 2, 2 * TT):
                    store(dve, n)


def stage_ffn(M):
    nc, I, O, xnT, brT, ps, x2 = (M[k] for k in ("nc", "I", "O", "xnT", "brT", "ps", "x2"))
    wiv = I["w_ffn_in"].rearrange("(k p) (s n) -> p k s n", p=P, s=2)
    wov = I["w_ffn_out"].rearrange("(j p) n -> p j n", p=P)
    NG, NT = FJ // 2, 2 * TT
    with Stage(nc, "ff") as st:
        xnR, brR = M["xnR"], M["brR"]
        xh = brR[:, 0:KT, :]
        more, moreR = st.pair("h", [P, 4, T])
        h = lambda g: (brT[:, 8:10, :], more[:, 0:2, :])[g % 2]
        hl = lambda g: (brR[:, 8:10, :], moreR[:, 0:2, :])[g % 2]
        hh = lambda g: (brR[:, 10:12, :], moreR[:, 2:4, :])[g % 2]
        wi, wil = st.pair("wi", [P, 2, KT, 2, P])
        wih = st.sb("wih", [P, 2, KT, 2, P], FR)
        wo, wol = st.pair("wo", [P, 2, 2, D])
        woh0 = st.sb("woh", [P, 2, D], FR)
        woh = lambda g: woh0[:, :, :] if g % 2 else M["memR"][:, :, :].rearrange("p k t -> p (k t)").rearrange(
            "p (j n) -> p j n", j=2)
        sa = st.sb("sa", [P, 2, BLK])
        sem = st.sem
        in_wi = [sem(f"in_wi{q}") for q in range(2)]
        in_wo = [sem(f"in_wo{q}") for q in range(2)]
        (x_high, x_low, wi_high, wi_low, wo_high, wo_low, projected, silued, multiplied, h_high, h_low, out_done,
         added, out) = (
            sem(n) for n in ("x_high", "x_low", "wi_high", "wi_low", "wo_high", "wo_low", "projected", "silued",
                             "multiplied", "h_high", "h_low", "out_done", "added", "out"))
        tok = lambda b: slice(b * BLK, (b + 1) * BLK)
        with st.block() as block:
            @block.sync
            def _(sp):
                for j in range(FJ):
                    if j >= 2:
                        sp.wait_ge(projected, NB3 * (j - 1))
                    for s in range(2):
                        sp.dma_start(wi[:, j % 2, :, s, :], wiv[:, :, s, j * P:(j + 1) * P]).then_inc(in_wi[j % 2], 16)
                    if j % 2:
                        g = j // 2
                        if g >= 2:
                            sp.wait_ge(out_done, NT * (g - 1))
                        sp.dma_start(wo[:, g % 2, :, :], wov[:, 2 * g:2 * g + 2, :]).then_inc(in_wo[g % 2], 16)
                for n in range(NT):
                    q, t = n // TT, n % TT
                    sp.wait_ge(added, NT * (NG - 1) + n + 1)
                    cols = slice(q * 512, (q + 1) * 512)
                    if t < QT:
                        sp.dma_start(O["y_prompt"][0, t * P:(t + 1) * P, cols], x2[:, t, cols]).then_inc(out, 16)
                    else:
                        sp.dma_start(O["y_sample"][:, 0, cols], x2[0:B, t, cols]).then_inc(out, 16)
                sp.wait_ge(out, 16 * NT)

            @block.tensor
            def _(pe):
                def hidden(g):
                    for j in (2 * g, 2 * g + 1):
                        pe.wait_ge(wi_low, j + 1)
                        for b in range(NB3):
                            s = NB3 * j + b
                            if j == 0:
                                pe.wait_ge(x_low, b + 1)
                            if s >= 2:
                                pe.wait_ge(multiplied, s - 1)
                            for half in range(2):
                                ins = products(nc, ps[:, 2 * half + s % 2, 0:BLK],
                                               [((wih[:, j % 2, k, half, :], wil[:, j % 2, k, half, :]),
                                                 (xh[:, k, tok(b)], xnR[:, k, tok(b)])) for k in range(KT)])
                            ins.then_inc(projected, 1)

                def project(g):
                    pe.wait_ge(h_low, 2 * NB3 * (g + 1))
                    pe.wait_ge(wo_low, g + 1)
                    for n in range(NT):
                        q, t = n // TT, n % TT
                        m = B if t == QT else P
                        i = NT * g + n
                        if i >= 4:
                            pe.wait_ge(added, i - 3)
                        rows, cols = slice(t * P, t * P + m), slice(q * 512, (q + 1) * 512)
                        products(nc, ps[0:m, 4 + i % 4, :],
                                 [((hh(g)[:, k, rows], hl(g)[:, k, rows]),
                                   (woh(g)[:, k, cols], wol[:, g % 2, k, cols])) for k in range(2)]
                                 ).then_inc(out_done, 1)

                hidden(0)
                for g in range(NG):
                    if g + 1 < NG:
                        hidden(g + 1)
                    project(g)

            @block.scalar
            def _(act):
                def split_wi(j):
                    if j >= 2:
                        act.wait_ge(projected, NB3 * (j - 1))
                    act.wait_ge(in_wi[j % 2], 32 * (j // 2 + 1))
                    high(nc, wih[:, j % 2, :, :, :], wi[:, j % 2, :, :, :]).then_inc(wi_high, 1)

                for b in range(NB3):
                    high(nc, xh[:, :, tok(b)], xnT[:, :, tok(b)]).then_inc(x_high, 1)
                    if b == 0:
                        split_wi(0)
                for j in range(FJ):
                    g = j // 2
                    for b in range(NB3):
                        s = NB3 * j + b
                        act.wait_ge(projected, s + 1)
                        if s >= 2:
                            act.wait_ge(multiplied, s - 1)
                        nc.scalar.activation(sa[:, s % 2, :], ps[:, s % 2, 0:BLK], ACT.Silu).then_inc(silued, 1)
                        if b == 0 and j + 1 < FJ:
                            split_wi(j + 1)
                        if b == 1 and j % 2:
                            if g >= 2:
                                act.wait_ge(out_done, NT * (g - 1))
                            act.wait_ge(in_wo[g % 2], 16 * (g // 2 + 1))
                            high(nc, woh(g), wo[:, g % 2, :, :]).then_inc(wo_high, 1)
                        act.wait_ge(multiplied, s + 1)
                        if g >= 2:
                            act.wait_ge(out_done, NT * (g - 1))
                        high(nc, hh(g)[:, j % 2, tok(b)], h(g)[:, j % 2, tok(b)]).then_inc(h_high, 1)

            @block.vector
            def _(dve):
                def split_wi(j):
                    dve.wait_ge(wi_high, j + 1)
                    low(nc, wil[:, j % 2, :, :, :], wi[:, j % 2, :, :, :], wih[:, j % 2, :, :, :]).then_inc(wi_low, 1)

                def add(g):
                    for n in range(NT):
                        q, t = n // TT, n % TT
                        m = B if t == QT else P
                        i = NT * g + n
                        dve.wait_ge(out_done, i + 1)
                        if i >= NT:
                            dve.wait_ge(added, i - NT + 1)
                        dst = x2[0:m, t, q * 512:(q + 1) * 512]
                        nc.vector.tensor_tensor(dst, dst, ps[0:m, 4 + i % 4, :], ALU.add).then_inc(added, 1)

                for b in range(NB3):
                    dve.wait_ge(x_high, b + 1)
                    low(nc, xnR[:, :, tok(b)], xnT[:, :, tok(b)], xh[:, :, tok(b)]).then_inc(x_low, 1)
                    if b == 0:
                        split_wi(0)
                for j in range(FJ):
                    g = j // 2
                    for b in range(NB3):
                        s = NB3 * j + b
                        dve.wait_ge(silued, s + 1)
                        if g >= 2:
                            dve.wait_ge(out_done, NT * (g - 1))
                        hid = h(g)[:, j % 2, tok(b)]
                        nc.vector.tensor_tensor(hid, sa[:, s % 2, :], ps[:, 2 + s % 2, 0:BLK],
                                                ALU.mult).then_inc(multiplied, 1)
                        if b == 0 and j + 1 < FJ:
                            split_wi(j + 1)
                        if b == 1 and j % 2:
                            dve.wait_ge(wo_high, g + 1)
                            low(nc, wol[:, g % 2, :, :], wo[:, g % 2, :, :], woh(g)).then_inc(wo_low, 1)
                        dve.wait_ge(h_high, s + 1)
                        low(nc, hl(g)[:, j % 2, tok(b)], hid, hh(g)[:, j % 2, tok(b)]).then_inc(h_low, 1)
                    if j % 2 and g >= 1:
                        add(g - 1)
                add(NG - 1)


def stage_tail(M):
    nc = M["nc"]
    with Stage(nc, "t1") as st:
        M["mixT"], M["mixR"] = st.pair("mixT", [P, KT, T])
        stage_merge(M)
        stage_out(M)
    stage_ffn(M)


STAGES = [stage_ml_proj, stage_mlstm, stage_attention, stage_samples, stage_tail]
RENEW_BEFORE = [stage_attention, stage_samples, stage_tail]

IN_SHAPES = None
OUT_SHAPES = [
    ("y_prompt", (1, S, D)), ("y_sample", (B, 1, D)),
    ("kv_cmp_prompt", (1, S, G, 2, HD)), ("kv_cmp_sample", (B, 1, G, 2, HD)),
    ("kv_slc_prompt", (1, S, G, 2, HD)), ("kv_slc_sample", (B, 1, G, 2, HD)),
    ("win_prompt", (1, WIN, G, 2, HD)), ("win_sample", (B, WIN, G, 2, HD)),
    ("kv_mem_prompt", (1, XT, XH, 2, XD)),
    ("C_prompt", (1, MH, MD, MD)), ("C_sample", (B, MH, MD, MD)),
    ("n_prompt", (1, MH, MD)), ("n_sample", (B, MH, MD)),
    ("m_prompt", (1, MH)), ("m_sample", (B, MH)),
    ("conv_prompt", (1, 3, MH * MD)), ("conv_sample", (B, 3, MH * MD)),
]


def kernel(**inputs):
    import concourse.bacc as bacc
    from concourse.bass_utils import run_bass_kernel_spmd

    nc = bacc.Bacc("TRN2", target_bir_lowering=False, num_devices=1)
    arrays, I, O = {}, {}, {}
    inputs = dict(inputs)
    inputs["const"] = CONST
    for name, a in inputs.items():
        a = np.ascontiguousarray(a)
        arrays[f"in_{name}"] = a
        I[name] = nc.dram_tensor(f"in_{name}", a.shape, mybir.dt.from_np(a.dtype), kind="ExternalInput").ap()
    for name, shape in OUT_SHAPES:
        O[name] = nc.dram_tensor(f"out_{name}", shape, F32, kind="ExternalOutput").ap()
    build(nc, I, O)
    r = run_bass_kernel_spmd(nc, [arrays], core_ids=[0])
    return tuple(r.results[0][f"out_{name}"] for name, _ in OUT_SHAPES)
```
